# Optimizing a Trainium2 kernel written in Bass

```python
import jax, jax.numpy as jnp
from jax import lax
import numpy as np

D_MODEL = 1024
BATCH = 1
SEQ = 256
DEPTH = 2

D_INNER = 2 * D_MODEL
D_MLSTM = D_INNER // 2
D_RET = D_INNER - D_MLSTM
N_HEADS_MLSTM = 4
N_HEADS_RET = 4
HD_M = D_MLSTM // N_HEADS_MLSTM
HD_R = D_RET // N_HEADS_RET
CONV_K = 4
CHUNK = 64
EPS = 1e-6
ROPE_BASE = 10000.0
D_IN_PROJ = 5 * D_MLSTM + 2 * N_HEADS_MLSTM + 4 * D_RET


def rmsnorm(x, g):
    xf = x.astype(jnp.float32)
    y = xf * lax.rsqrt(jnp.mean(xf * xf, axis=-1, keepdims=True) + EPS)
    return (y * g.astype(jnp.float32)).astype(x.dtype)

def head_layernorm(h, g, n_heads):
    B, S, W = h.shape
    hf = h.astype(jnp.float32).reshape(B, S, n_heads, W // n_heads)
    mu = jnp.mean(hf, axis=-1, keepdims=True)
    var = jnp.mean(jnp.square(hf - mu), axis=-1, keepdims=True)
    y = ((hf - mu) * lax.rsqrt(var + EPS)).reshape(B, S, W)
    return (y * g.astype(jnp.float32)).astype(h.dtype)

def causal_dwconv(x, w, b):
    S = x.shape[1]
    xp = jnp.pad(x, ((0, 0), (CONV_K - 1, 0), (0, 0)))
    y = xp[:, 0:S] * w[0]
    for t in range(1, CONV_K):
        y = y + xp[:, t:t + S] * w[t]
    return y + b

def split_cols(p):
    sizes = [D_MLSTM] * 5 + [N_HEADS_MLSTM] * 2 + [D_RET] * 4
    idx = np.cumsum(sizes)[:-1].tolist()
    return jnp.split(p, idx, axis=-1)

def to_chunks(t):
    B, S, H, d = t.shape
    return t.reshape(B, S // CHUNK, CHUNK, H, d).transpose(1, 0, 3, 2, 4)

def from_chunks(t):
    NC, B, H, L, d = t.shape
    return t.transpose(1, 0, 3, 2, 4).reshape(B, NC * L, H * d)

def gate_chunks(t):
    B, S, H = t.shape
    return t.reshape(B, S // CHUNK, CHUNK, H).transpose(1, 0, 3, 2)

def rotary(t, positions):
    d = t.shape[-1]
    inv_freq = 1.0 / (ROPE_BASE ** jnp.linspace(0.0, 1.0, d // 2, dtype=jnp.float32))
    ang = positions.astype(jnp.float32)[..., None] * inv_freq
    cos = jnp.cos(ang)[:, :, None, :].astype(t.dtype)
    sin = jnp.sin(ang)[:, :, None, :].astype(t.dtype)
    t1, t2 = jnp.split(t, 2, axis=-1)
    return jnp.concatenate([t1 * cos - t2 * sin, t2 * cos + t1 * sin], axis=-1)

def mlstm_chunkwise(q, k, v, i_pre, f_pre):
    B, S, H, d = q.shape
    k = k * (d ** -0.5)
    li = gate_chunks(i_pre.astype(jnp.float32))
    lf = gate_chunks(jax.nn.log_sigmoid(f_pre.astype(jnp.float32)))
    causal = jnp.tril(jnp.ones((CHUNK, CHUNK), dtype=bool))

    def step(carry, inp):
        C, n, m = carry
        qj, kj, vj, lij, lfj = inp
        b = jnp.cumsum(lfj, axis=-1)
        a = b + m[..., None]
        g = b[..., :, None] - b[..., None, :] + lij[..., None, :]
        g = jnp.where(causal, g, -jnp.inf)
        m_row = jnp.maximum(a, jnp.max(g, axis=-1))
        w_intra = jnp.exp(g - m_row[..., None])
        w_inter = jnp.exp(a - m_row)
        s = jnp.einsum('bhld,bhsd->bhls', qj, kj) * w_intra
        num = (jnp.einsum('bhls,bhsv->bhlv', s, vj)
               + w_inter[..., None] * jnp.einsum('bhvk,bhlk->bhlv', C, qj))
        den = jnp.sum(s, axis=-1) + w_inter * jnp.einsum('bhk,bhlk->bhl', n, qj)
        h = num / jnp.maximum(jnp.abs(den), jnp.exp(-m_row))[..., None]
        bL = b[..., -1]
        g_end = bL[..., None] - b + lij
        m_new = jnp.maximum(bL + m, jnp.max(g_end, axis=-1))
        w_end = jnp.exp(g_end - m_new[..., None])
        decay = jnp.exp(bL + m - m_new)
        C_new = decay[..., None, None] * C + jnp.einsum('bhs,bhsv,bhsk->bhvk', w_end, vj, kj)
        n_new = decay[..., None] * n + jnp.einsum('bhs,bhsk->bhk', w_end, kj)
        return (C_new, n_new, m_new), h.astype(q.dtype)

    init = (jnp.zeros((B, H, d, d), jnp.float32),
            jnp.zeros((B, H, d), jnp.float32),
            jnp.zeros((B, H), jnp.float32))
    _, hs = lax.scan(step, init, (to_chunks(q), to_chunks(k), to_chunks(v), li, lf))
    return from_chunks(hs)

def retention_chunkwise(q, k, v):
    B, S, H, d = q.shape
    k = k * (d ** -0.5)
    log_gamma = jnp.log(1.0 - 2.0 ** (-5.0 - jnp.arange(H, dtype=jnp.float32)))
    pos = jnp.arange(CHUNK, dtype=jnp.float32)
    diff = pos[:, None] - pos[None, :]
    Dmat = jnp.where(diff >= 0, jnp.exp(log_gamma[:, None, None] * jnp.maximum(diff, 0.0)), 0.0)
    xi = jnp.exp(log_gamma[:, None] * (pos + 1.0))
    zeta = jnp.exp(log_gamma[:, None] * (CHUNK - 1.0 - pos))
    g_chunk = jnp.exp(log_gamma * CHUNK)

    def step(R, inp):
        qj, kj, vj = inp
        s = jnp.einsum('bhld,bhsd->bhls', qj, kj) * Dmat
        o = (jnp.einsum('bhls,bhsv->bhlv', s, vj)
             + xi[..., None] * jnp.einsum('bhlk,bhkv->bhlv', qj, R))
        R_new = g_chunk[:, None, None] * R + jnp.einsum('bhsk,bhsv->bhkv', kj * zeta[..., None], vj)
        return R_new, o.astype(q.dtype)

    init = jnp.zeros((B, H, d, d), jnp.float32)
    _, os_ = lax.scan(step, init, (to_chunks(q), to_chunks(k), to_chunks(v)))
    return from_chunks(os_)

def first_inputs(seed: int = 0) -> dict:
    key = jax.random.key(seed)
    ks = jax.random.split(key, 16)
    f32 = jnp.float32
    x = jax.random.normal(ks[0], (BATCH, SEQ, D_MODEL), f32)
    c = jax.random.normal(ks[1], (BATCH, D_MODEL), f32)
    offset = jax.random.randint(ks[2], (BATCH, 1), 0, 4096, dtype=jnp.int32)
    positions = offset + jnp.arange(SEQ, dtype=jnp.int32)[None, :]
    w_ada = jax.random.normal(ks[3], (DEPTH, D_MODEL, 3 * D_MODEL), f32) * (0.5 * D_MODEL ** -0.5)
    b_ada = jax.random.normal(ks[4], (DEPTH, 3 * D_MODEL), f32) * 0.02
    norm_g = 1.0 + 0.02 * jax.random.normal(ks[5], (DEPTH, D_MODEL), f32)
    w_in = jax.random.normal(ks[6], (DEPTH, D_MODEL, D_IN_PROJ), f32) * (D_MODEL ** -0.5)
    conv_w = jax.random.normal(ks[7], (DEPTH, CONV_K, 2 * D_MLSTM), f32) * (CONV_K ** -0.5)
    conv_b = jax.random.normal(ks[8], (DEPTH, 2 * D_MLSTM), f32) * 0.02
    b_igate = jax.random.normal(ks[9], (DEPTH, N_HEADS_MLSTM), f32) * 0.1
    b_fgate = (jnp.linspace(3.0, 6.0, N_HEADS_MLSTM, dtype=f32)[None, :]
               + 0.1 * jax.random.normal(ks[10], (DEPTH, N_HEADS_MLSTM), f32))
    gn_m = 1.0 + 0.02 * jax.random.normal(ks[11], (DEPTH, D_MLSTM), f32)
    gn_r = 1.0 + 0.02 * jax.random.normal(ks[12], (DEPTH, D_RET), f32)
    w_out = jax.random.normal(ks[13], (DEPTH, D_INNER, D_MODEL), f32) * (D_INNER ** -0.5)
    final_g = 1.0 + 0.02 * jax.random.normal(ks[14], (D_MODEL,), f32)
    return {'x': x, 'c': c, 'positions': positions, 'w_ada': w_ada, 'b_ada': b_ada,
            'norm_g': norm_g, 'w_in': w_in, 'conv_w': conv_w, 'conv_b': conv_b,
            'b_igate': b_igate, 'b_fgate': b_fgate, 'gn_m': gn_m, 'gn_r': gn_r,
            'w_out': w_out, 'final_g': final_g}

def first_block(x, c, positions, w_ada, b_ada, norm_g, w_in, conv_w, conv_b,
              b_igate, b_fgate, gn_m, gn_r, w_out, final_g):
    B, S, _ = x.shape
    c_act = jax.nn.silu(c)
    for l in range(DEPTH):
        ada = c_act @ w_ada[l] + b_ada[l]
        shift, scale, gate = jnp.split(ada, 3, axis=-1)
        h = rmsnorm(x, norm_g[l]) * (1.0 + scale[:, None, :]) + shift[:, None, :]
        p = h @ w_in[l]
        mq, mk, mv, mo, mz, mi, mf, rq, rk, rv, rz = split_cols(p)

        qk = jax.nn.silu(causal_dwconv(jnp.concatenate([mq, mk], axis=-1), conv_w[l], conv_b[l]))
        mq_c, mk_c = jnp.split(qk, 2, axis=-1)
        cell = mlstm_chunkwise(mq_c.reshape(B, S, N_HEADS_MLSTM, HD_M),
                               mk_c.reshape(B, S, N_HEADS_MLSTM, HD_M),
                               mv.reshape(B, S, N_HEADS_MLSTM, HD_M),
                               mi + b_igate[l], mf + b_fgate[l])
        y_m = jax.nn.sigmoid(mo) * head_layernorm(cell, gn_m[l], N_HEADS_MLSTM) * jax.nn.silu(mz)

        rq_h = rotary(rq.reshape(B, S, N_HEADS_RET, HD_R), positions)
        rk_h = rotary(rk.reshape(B, S, N_HEADS_RET, HD_R), positions)
        ret = retention_chunkwise(rq_h, rk_h, rv.reshape(B, S, N_HEADS_RET, HD_R))
        y_r = head_layernorm(ret, gn_r[l], N_HEADS_RET) * jax.nn.silu(rz)

        y = jnp.concatenate([y_m, y_r], axis=-1) @ w_out[l]
        x = x + gate[:, None, :] * y
    return rmsnorm(x, final_g)


N_PREV_CHUNKS = 8
BAND = (N_PREV_CHUNKS + 1) * CHUNK
BAND_PAD = N_PREV_CHUNKS * CHUNK
D_CONV = D_MODEL // 2
D_ATT = D_MODEL - D_CONV
D_MIX = D_CONV + D_ATT
HEAD_DIM = 64
N_HEADS = D_ATT // HEAD_DIM
CONV_WIDTH = 31
MAX_REL = 128
N_REL = 2 * MAX_REL + 1
D_IN_COLS = 2 * D_CONV + 3 * D_ATT
D_FF_DENSE = 2816
N_EXPERTS = 8
TOP_K = 2
D_FF_EXPERT = 3584
N_DENSE = (DEPTH + 1) // 2
N_MOE = DEPTH // 2
NEG_INF = -1e30


def rmsnorm_2(x, g):
    xf = x.astype(jnp.float32)
    y = xf * lax.rsqrt(jnp.mean(xf * xf, axis=-1, keepdims=True) + EPS)
    return (y * g.astype(jnp.float32)).astype(x.dtype)

def layernorm(x, g, b):
    xf = x.astype(jnp.float32)
    mu = jnp.mean(xf, axis=-1, keepdims=True)
    xc = xf - mu
    var = jnp.mean(xc * xc, axis=-1, keepdims=True)
    y = xc * lax.rsqrt(var + EPS) * g.astype(jnp.float32) + b.astype(jnp.float32)
    return y.astype(x.dtype)

def modulate(h, shift, scale):
    return h * (1 + scale[:, None, :]) + shift[:, None, :]

def conformer_conv(u, conv_w, conv_b, ln_g, ln_b):
    a, g = jnp.split(u, 2, axis=-1)
    z = a * jax.nn.sigmoid(g)
    z = lax.conv_general_dilated(
        z, conv_w, window_strides=(1,), padding=[(CONV_WIDTH - 1, 0)],
        dimension_numbers=("NWC", "WIO", "NWC"),
        feature_group_count=D_CONV) + conv_b
    z = layernorm(z, ln_g, ln_b)
    return jax.nn.silu(z)

def chunk_band_attention(q, k, v, q_norm_g, k_norm_g, rel_bias):
    B, S = q.shape[0], q.shape[1]
    nc = S // CHUNK
    q = rmsnorm_2(q.reshape(B, S, N_HEADS, HEAD_DIM), q_norm_g)
    k = rmsnorm_2(k.reshape(B, S, N_HEADS, HEAD_DIM), k_norm_g)
    v = v.reshape(B, S, N_HEADS, HEAD_DIM)
    pad = ((0, 0), (BAND_PAD, 0), (0, 0), (0, 0))
    kp = jnp.pad(k, pad)
    vp = jnp.pad(v, pad)
    idx = jnp.arange(nc)[:, None] * CHUNK + jnp.arange(BAND)[None, :]
    kb = kp[:, idx]
    vb = vp[:, idx]
    qc = q.reshape(B, nc, CHUNK, N_HEADS, HEAD_DIM)
    s = jnp.einsum("bnqhd,bnkhd->bnhqk", qc, kb).astype(jnp.float32) * (HEAD_DIM ** -0.5)
    rel = jnp.arange(BAND)[None, :] - BAND_PAD - jnp.arange(CHUNK)[:, None]
    rel_idx = jnp.clip(rel, -MAX_REL, MAX_REL) + MAX_REL
    bias = rel_bias.astype(jnp.float32)[:, rel_idx]
    valid = idx >= BAND_PAD
    s = jnp.where(valid[None, :, None, None, :], s + bias[None, None], NEG_INF)
    p = jax.nn.softmax(s, axis=-1).astype(v.dtype)
    o = jnp.einsum("bnhqk,bnkhd->bnqhd", p, vb)
    return o.reshape(B, S, D_ATT)

def swiglu(h, w_gate, w_up, w_down):
    return (jax.nn.silu(h @ w_gate) * (h @ w_up)) @ w_down

def moe_swiglu(h, w_router, b_router, w_gate, w_up, w_down):
    B, S, D = h.shape
    t = h.reshape(B * S, D)
    logits = (t @ w_router).astype(jnp.float32) + b_router.astype(jnp.float32)
    top_val, top_idx = lax.top_k(logits, TOP_K)
    top_w = jax.nn.softmax(top_val, axis=-1)
    combine = jnp.sum(jax.nn.one_hot(top_idx, N_EXPERTS, dtype=jnp.float32)
                      * top_w[..., None], axis=1).astype(t.dtype)
    out = jnp.zeros_like(t)
    for e in range(N_EXPERTS):
        out = out + combine[:, e:e + 1] * swiglu(t, w_gate[e], w_up[e], w_down[e])
    return out.reshape(B, S, D)

def second_inputs(seed: int = 0) -> dict:
    key = jax.random.key(seed)
    ks = jax.random.split(key, 24)
    f32 = jnp.float32

    def nrm(k, shape, scale):
        return jax.random.normal(k, shape, f32) * scale

    return {
        "x": nrm(ks[0], (BATCH, SEQ, D_MODEL), 1.0),
        "c": nrm(ks[1], (BATCH, D_MODEL), 1.0),
        "w_ada": nrm(ks[2], (DEPTH, D_MODEL, 6 * D_MODEL), 0.5 * D_MODEL ** -0.5),
        "b_ada": nrm(ks[3], (DEPTH, 6 * D_MODEL), 0.02),
        "norm_mix_g": 1.0 + nrm(ks[4], (DEPTH, D_MODEL), 0.02),
        "norm_ffn_g": 1.0 + nrm(ks[5], (DEPTH, D_MODEL), 0.02),
        "w_in": nrm(ks[6], (DEPTH, D_MODEL, D_IN_COLS), D_MODEL ** -0.5),
        "w_out": nrm(ks[7], (DEPTH, D_MIX, D_MODEL), D_MIX ** -0.5),
        "conv_w": nrm(ks[8], (DEPTH, CONV_WIDTH, 1, D_CONV), CONV_WIDTH ** -0.5),
        "conv_b": nrm(ks[9], (DEPTH, D_CONV), 0.02),
        "conv_ln_g": 1.0 + nrm(ks[10], (DEPTH, D_CONV), 0.02),
        "conv_ln_b": nrm(ks[11], (DEPTH, D_CONV), 0.02),
        "q_norm_g": 1.0 + nrm(ks[12], (DEPTH, HEAD_DIM), 0.02),
        "k_norm_g": 1.0 + nrm(ks[13], (DEPTH, HEAD_DIM), 0.02),
        "rel_bias": nrm(ks[14], (DEPTH, N_HEADS, N_REL), 0.5),
        "ffn_w_gate": nrm(ks[15], (N_DENSE, D_MODEL, D_FF_DENSE), D_MODEL ** -0.5),
        "ffn_w_up": nrm(ks[16], (N_DENSE, D_MODEL, D_FF_DENSE), D_MODEL ** -0.5),
        "ffn_w_down": nrm(ks[17], (N_DENSE, D_FF_DENSE, D_MODEL), D_FF_DENSE ** -0.5),
        "moe_w_router": nrm(ks[18], (N_MOE, D_MODEL, N_EXPERTS), D_MODEL ** -0.5),
        "moe_b_router": nrm(ks[19], (N_MOE, N_EXPERTS), 0.01),
        "moe_w_gate": nrm(ks[20], (N_MOE, N_EXPERTS, D_MODEL, D_FF_EXPERT), D_MODEL ** -0.5),
        "moe_w_up": nrm(ks[21], (N_MOE, N_EXPERTS, D_MODEL, D_FF_EXPERT), D_MODEL ** -0.5),
        "moe_w_down": nrm(ks[22], (N_MOE, N_EXPERTS, D_FF_EXPERT, D_MODEL), D_FF_EXPERT ** -0.5),
    }

def second_block(x, c, w_ada, b_ada, norm_mix_g, norm_ffn_g, w_in, w_out,
              conv_w, conv_b, conv_ln_g, conv_ln_b, q_norm_g, k_norm_g, rel_bias,
              ffn_w_gate, ffn_w_up, ffn_w_down,
              moe_w_router, moe_b_router, moe_w_gate, moe_w_up, moe_w_down):
    c_act = jax.nn.silu(c)
    for l in range(DEPTH):
        mod = c_act @ w_ada[l] + b_ada[l]
        sh1, sc1, g1, sh2, sc2, g2 = jnp.split(mod, 6, axis=-1)

        h = modulate(rmsnorm_2(x, norm_mix_g[l]), sh1, sc1)
        proj = h @ w_in[l]
        u_conv = proj[..., :2 * D_CONV]
        q = proj[..., 2 * D_CONV:2 * D_CONV + D_ATT]
        k = proj[..., 2 * D_CONV + D_ATT:2 * D_CONV + 2 * D_ATT]
        v = proj[..., 2 * D_CONV + 2 * D_ATT:]
        y_conv = conformer_conv(u_conv, conv_w[l], conv_b[l], conv_ln_g[l], conv_ln_b[l])
        y_att = chunk_band_attention(q, k, v, q_norm_g[l], k_norm_g[l], rel_bias[l])
        y = jnp.concatenate([y_conv, y_att], axis=-1) @ w_out[l]
        x = x + g1[:, None, :] * y

        h = modulate(rmsnorm_2(x, norm_ffn_g[l]), sh2, sc2)
        if l % 2 == 0:
            i = l // 2
            f = swiglu(h, ffn_w_gate[i], ffn_w_up[i], ffn_w_down[i])
        else:
            i = l // 2
            f = moe_swiglu(h, moe_w_router[i], moe_b_router[i],
                           moe_w_gate[i], moe_w_up[i], moe_w_down[i])
        x = x + g2[:, None, :] * f
    return x


def setup_inputs(seed=0):
    out = dict(first_inputs(seed))
    for name, value in second_inputs(seed + 1).items():
        if name != "x":
            out[name + "_2"] = value
    return out


def reference(
    x, c, positions, w_ada, b_ada, norm_g, w_in, conv_w, conv_b, b_igate, b_fgate, gn_m, gn_r,
    w_out, final_g, c_2, w_ada_2, b_ada_2, norm_mix_g_2, norm_ffn_g_2, w_in_2, w_out_2,
    conv_w_2, conv_b_2, conv_ln_g_2, conv_ln_b_2, q_norm_g_2, k_norm_g_2, rel_bias_2,
    ffn_w_gate_2, ffn_w_up_2, ffn_w_down_2, moe_w_router_2, moe_b_router_2, moe_w_gate_2,
    moe_w_up_2, moe_w_down_2,
):
    x = first_block(
        x, c, positions, w_ada, b_ada, norm_g, w_in, conv_w, conv_b, b_igate, b_fgate, gn_m,
        gn_r, w_out, final_g,
    )
    return second_block(
        x, c_2, w_ada_2, b_ada_2, norm_mix_g_2, norm_ffn_g_2, w_in_2, w_out_2, conv_w_2,
        conv_b_2, conv_ln_g_2, conv_ln_b_2, q_norm_g_2, k_norm_g_2, rel_bias_2, ffn_w_gate_2,
        ffn_w_up_2, ffn_w_down_2, moe_w_router_2, moe_b_router_2, moe_w_gate_2, moe_w_up_2,
        moe_w_down_2,
    )


_drawn_inputs = setup_inputs


def setup_inputs(seed=0):
    import zlib

    import numpy as np

    out = dict(_drawn_inputs(seed))
    spreads = {}
    factors = {'norm_g': 3.784,
     'conv_b': 8.0,
     'b_igate': 64.0,
     'gn_m': 8.0,
     'gn_r': 5.732,
     'norm_mix_g_2': 5.961,
     'norm_ffn_g_2': 3.507,
     'conv_b_2': 6.891,
     'conv_ln_g_2': 5.942,
     'conv_ln_b_2': 6.975,
     'q_norm_g_2': 8.0,
     'k_norm_g_2': 6.651,
     'moe_b_router_2': 26.604}
    for name, (base, spread) in spreads.items():
        noise = np.random.default_rng([zlib.crc32(name.encode()), seed]).standard_normal(out[name].shape)
        drawn = base * np.exp(spread * noise) if base else spread * noise
        out[name] = __import__('jax').numpy.asarray(drawn.astype(out[name].dtype))
    for name, factor in factors.items():
        out[name] = (out[name] * factor).astype(out[name].dtype)
    return out
```

```python
import concourse.bass as bass
from concourse import mybir
from contextlib import ExitStack
import numpy as np

F32 = mybir.dt.float32
F32R = mybir.dt.float32r
I32 = mybir.dt.int32
ACT = mybir.ActivationFunctionType
ALU = mybir.AluOpType
AX = mybir.AxisListType

P = 128
S = 256
D = 1024
KD = D // P
L = 2
H = 4
HD = 256
D_INNER = 2048
D_MLSTM = 1024
D_RET = 1024
CONV_K = 4
EPS = 1e-6
GATE_COL = 5 * D_MLSTM
RET_COL = GATE_COL + 2 * H
D_CONV = 512
D_ATT = 512
CW = 31
NH2 = 8
HD2 = 64
NREL = 257
EXT = 127 + NREL
CHUNK = 64
FF = 2816
NE = 8
FE = 3584
CT = D_CONV // P
NEG = -1e30

C_ID = 0
C_CAUSAL = C_ID + P
C_DECAY = C_CAUSAL + S
C_BEFORE = C_DECAY + H * S
C_IOTA = C_BEFORE + P
C_FREQ = C_IOTA + P
C_HSUM = C_FREQ + 1
C_HBC = C_HSUM + CT * NH2
C_ALL = C_HBC + CT * P

P1_BADA, P1_NORM, P1_CW, P1_CB, P1_GNM, P1_GNR = 0, 24, 32, 96, 112, 120
P2_BADA, P2_MIX, P2_FFN, P2_CB, P2_LG, P2_LB, P2_QN, P2_KN, P2_C, P2_C2, P2_FIN = 0, 48, 56, 64, 68, 72, 76, 77, 78, 86, 94
P2_ROWS = (102, 78)

UW = 2048
RAW = 6
HL = 3
LOOK = 2
ADA1, ADA2 = 3 * D // 256, 6 * D // 256
ADA_UNITS = L * (ADA1 + ADA2)
HEAD_UNITS = 9
OUT1_UNITS = D_INNER * D // (P * UW)
MIX_UNITS = (2 * D_CONV + 3 * D_ATT) // 256
OUT2_UNITS = D * D // (P * UW)
FF_UNITS = 2 * FF // 256
DOWN_UNITS = FF // 256
JOB_UP = 4 * FE // 512
JOB_DOWN = FE // 256
JOB_UNITS = JOB_UP + JOB_DOWN
UNIT_L1 = H * HEAD_UNITS + OUT1_UNITS
UNIT_L2 = MIX_UNITS + OUT2_UNITS
S_B1 = 0
S_B2 = L * UNIT_L1
S_FF = S_B2 + UNIT_L2
S_B3 = S_FF + FF_UNITS + DOWN_UNITS
S_MOE = S_B3 + UNIT_L2
assert (2 * HEAD_UNITS) % RAW == 0 and JOB_UNITS % RAW == 0 and (2 * HEAD_UNITS) % HL == 0 and JOB_UNITS % HL == 0

N_FINAL, N_MIX, N_FFN = 2, (3, 5), (4, 6)
SHIFT = {0: 0, 1: 72, 3: 24, 4: 48, 5: 96, 6: 120}
ROWS_LOADED = 592
STEPS_PAIR = 58
BEFORE_QACC = 2 * D_INNER // P * S + 2 * S + 4 * (CONV_K - 1 + S)
TWO_PI_2 = round((2 * np.pi - 6.28125) * 2 ** 21) / 2 ** 21
TWO_PI = (6.28125, TWO_PI_2, float(np.float32(2 * np.pi - 6.28125 - TWO_PI_2)))
ROUND = 12582912.0
PI_BELOW = 3.1415925
NPAIR = H // 2


class Unit:

    def __init__(self, n, turn=0, per=0):
        self.n, self.turn, self.per = n, turn, per

    def count(self, k=1):
        return self.turn * self.per + (self.n + k) if self.per else self.n + k

    def ring(self, k=1):
        return self.turn * self.per + (ADA_UNITS + self.n + k) if self.per else ADA_UNITS + self.n + k

    @property
    def raw(self):
        return (ADA_UNITS + self.n) % RAW

    @property
    def loads(self):
        first = 16 * ((ADA_UNITS + self.n) // RAW + 1)
        return self.turn * (16 * self.per // RAW) + first if self.per else first

    @property
    def hl(self):
        return self.n % HL

    @property
    def bank(self):
        return self.n % 2

    def plus(self, k):
        return Unit(self.n + k, self.turn, self.per)


class Chain:

    def __init__(self, eng, sem):
        self.eng, self.sem, self.n, self.turn, self.per = eng, sem, 0, 0, 0

    def __call__(self, ins):
        self.mark(ins)
        self.wait()

    def mark(self, ins):
        ins.then_inc(self.sem, 1)
        self.n += 1

    def wait(self, back=0):
        v = self.n - back
        self.eng.wait_ge(self.sem, self.turn * self.per + v if self.per else v)

    def enter(self, turn, per):
        self.n0, self.turn, self.per = self.n, turn, per

    def leave(self, turns):
        got = self.n - self.n0
        assert got == self.per, f"steps in one turn: {got}, not {self.per}"
        self.n, self.turn, self.per = self.n0 + turns * got, 0, 0


def two_block_model(nc, x, positions, consts, c, w_ada, b_ada, norm_g, w_in, conv_w, conv_b, b_igate, b_fgate,
                    gn_m, gn_r, w_out, final_g, c_2, w_ada_2, b_ada_2, norm_mix_g, norm_ffn_g, w_in_2, w_out_2,
                    conv_w_2, conv_b_2, conv_ln_g, conv_ln_b, q_norm_g, k_norm_g, rel_bias, ffn_w_gate, ffn_w_up,
                    ffn_w_down, w_router, b_router, moe_w_gate, moe_w_up, moe_w_down, out):
    ctx = ExitStack()
    with ctx:
        def sb(name, shape, dt=F32, stack=ctx):
            return stack.enter_context(nc.sbuf_tensor(name, shape, dt))

        def sem(name):
            return ctx.enter_context(nc.semaphore(name))

        raw = sb("raw", [P, RAW, UW])
        whi = sb("whi", [P, HL, UW], F32R)
        wlo = sb("wlo", [P, HL, UW], F32R)
        xT = sb("xT", [P, KD, S])
        h = sb("h", [P, KD, S])
        hhi = sb("hhi", [P, KD, S], F32R)
        hlo = sb("hlo", [P, KD, S], F32R)
        cst = sb("cst", [P, C_ALL])
        ones = sb("ones", [P, S])
        mean256 = sb("mean256", [P, P])
        mean512 = sb("mean512", [P, P])
        eps = sb("eps", [P, 1])
        par1 = sb("par1", [P, L, P])
        par2 = sb("par2", [P, L, P])
        taps2 = sb("taps2", [P, L, P])
        cact = sb("cact", [P, 2, KD])
        mod = sb("mod", [P, ADA_UNITS * 2])
        amul = sb("amul", [P, 7, KD])
        wgate = sb("wgate", [P, L, KD, 2 * H])
        gbias = sb("gbias", [H, L, 2])
        rstd = sb("rstd", [P, S])

        b1 = ExitStack()
        yhi = sb("yhi", [P, D_INNER // P, S], F32R, b1)
        ylo = sb("ylo", [P, D_INNER // P, S], F32R, b1)
        cosT = sb("cosT", [P, S], F32, b1)
        sinT = sb("sinT", [P, S], F32, b1)
        qpad = sb("qpad", [P, 2, 2, CONV_K - 1 + S], F32, b1)
        qacc = sb("qacc", [P, 2, 2, S], F32, b1)
        rot = sb("rot", [P, 2, 2, S], F32, b1)
        qk = sb("qk", [P, 2, 2, S], F32, b1)
        vtok = sb("vtok", [P, 2, HD], F32, b1)
        osig = sb("osig", [P, 2, S], F32, b1)
        zsil = sb("zsil", [P, 2, S], F32, b1)
        bcs = sb("bcs", [P, 2, S], F32, b1)
        arg = sb("arg", [P, S + P], F32, b1)
        sT = sb("sT", [P, S + P], F32, b1)
        den = rstd
        hn = sb("hn", [P, 2, S], F32, b1)
        sq, yf = (qpad[:, i, :, CONV_K - 1:] for i in range(2))
        gdiag = h[0:H].rearrange("q (h a) s -> q h a s", h=H)
        acol = sb("acol", [P, 2, H], F32, b1)
        b1.close()
        bg = ExitStack()
        sb("before_qacc", [P, BEFORE_QACC], F32, bg)
        gt = sb("gt", [H, 8, S], F32, bg)
        bg.close()
        b0 = ExitStack()
        xtok = sb("xtok", [P, 2, D], F32, b0)
        prow = sb("prow", [P, 6, P], F32, b0)
        acc = sb("acc", [P, 2, S], F32, b0)
        b0.close()
        bt = ExitStack()
        sb("behind_y", [P, 2 * D_INNER // P * S], F32, bt)
        sb("behind_cos", [P, 2 * S], F32, bt)
        posi = sb("posi", [P, S], I32, bt)
        posf = sb("posf", [P, S], F32, bt)
        turns = sb("turns", [P, 2, S], F32, bt)
        ang = sb("ang", [P, S], F32, bt)
        bt.close()

        b2 = ExitStack()
        y2hi = sb("y2hi", [P, KD, S], F32R, b2)
        y2lo = sb("y2lo", [P, KD, S], F32R, b2)
        zpad = sb("zpad", [P, CT, CW - 1 + S], F32, b2)
        zacc = sb("zacc", [P, CT, S], F32, b2)
        sig = sb("sig", [P, 2, S], F32, b2)
        q2 = sb("q2", [P, 2, CT, S], F32, b2)
        sq2 = h[:, :, :].rearrange("p (a j) s -> p a j s", a=2)
        rs2 = sb("rs2", [NH2, 2, S], F32, b2)
        v2 = sb("v2", [P, 2, D_ATT], F32, b2)
        bias2 = sb("bias2", [P, NH2, S], F32, b2)
        s2 = sb("s2", [P, 2, S + P], F32, b2)
        p2 = sb("p2", [P, 2, S + P], F32, b2)
        pT = sb("pT", [P, 2, S + P], F32, b2)
        st2 = sb("st2", [P, 2, 8], F32, b2)
        b2.close()

        bf = ExitStack()
        fhi = sb("fhi", [P, FF // P, S], F32R, bf)
        flo = sb("flo", [P, FF // P, S], F32R, bf)
        fg = sb("fg", [P, 2, 2, S], F32, bf)
        fa = sb("fa", [P, 2, 2, S], F32, bf)
        bf.close()

        bm = ExitStack()
        thi = sb("thi", [P, FE // P, P], F32R, bm)
        tlo = sb("tlo", [P, FE // P, P], F32R, bm)
        htok = sb("htok", [P, 2, D], F32, bm)
        xghi = sb("xghi", [P, KD, P], F32R, bm)
        xglo = sb("xglo", [P, KD, P], F32R, bm)
        mg = sb("mg", [P, 2, 512], F32, bm)
        ma = sb("ma", [P, 2, 512], F32, bm)
        pick = sb("pick", [P, 2, P], F32, bm)
        pickw = sb("pickw", [P, 2, P], F32, bm)
        pickT = sb("pickT", [P, S], F32, bm)
        yexp = sb("yexp", [P, D], F32, bm)
        moe = h
        wr = sb("wr", [P, KD, NE], F32, bm)
        rb = sb("rb", [P, NE], F32, bm)
        lg = sb("lg", [P, 12, 2, NE], F32, bm)
        comb = sb("comb", [P, 2, NE + 1], F32, bm)
        posm = sb("posm", [P, 2, NE + 1], F32, bm)
        r1 = sb("r1", [1, 10, NE], F32, bm)
        jobs = sb("jobs", [1, NE], I32, bm)
        otok = h[:, :, :].rearrange("p (t k) s -> p t (k s)", t=2)
        bm.close()

        ps = [ctx.enter_context(nc.psum_tensor(f"ps{i}", [P, 512], F32)) for i in range(8)]
        ps2 = [b[:, :].rearrange("p (a s) -> p a s", a=2) for b in ps]
        ps4 = [b[:, :].rearrange("p (a s) -> p a s", a=4) for b in ps]
        ext = nc.dram_tensor("extended_bias", [L, NH2, EXT], F32, kind="Internal").ap()
        rep = nc.dram_tensor("repeated_bias", [L, NH2, P, EXT], F32, kind="Internal").ap()

        ident = cst[:, C_ID:C_ID + P]
        causal = cst[:, C_CAUSAL:C_CAUSAL + S]
        before = cst[:, C_BEFORE:C_BEFORE + P]
        iota = cst[:, C_IOTA:C_IOTA + P]
        hsum = cst[:, C_HSUM:C_HSUM + CT * NH2].rearrange("p (j h) -> p j h", j=CT)
        hbc = cst[0:NH2, C_HBC:C_HBC + CT * P].rearrange("p (j m) -> p j m", j=CT)

        raw_in = [sem(f"raw_in{i}") for i in range(RAW)]
        x_in, const_in, rows_in, gate_in, pos_in = sem("x_in"), sem("const_in"), sem("rows_in"), sem("gate_in"), sem("pos_in")
        ext_out, bias_in, router_in, stored = sem("ext_out"), sem("bias_in"), sem("router_in"), sem("stored")
        raw_free = sem("raw_free")
        hi_ready = sem("hi_ready")
        unit_done = sem("unit_done")
        memset_done, x_turned, x_ready = sem("memset_done"), sem("x_turned"), sem("x_ready")
        rows_turned, cols_ready, cact_ready = sem("rows_turned"), sem("cols_ready"), sem("cact_ready")
        ada_done = sem("ada_done")
        angle_ready, sin_ready = sem("angle_ready"), sem("sin_ready")
        squares, sum_ready, std_ready, h_ready, hhi_ready, hlo_ready = (
            sem("squares"), sem("sum_ready"), sem("std_ready"), sem("h_ready"), sem("hhi_ready"), sem("hlo_ready"))
        gates_done, gate_f, gate_ln, gate_em, gate_m, a_ready, a_turned, acol_ready = (
            sem("gates_done"), sem("gate_f"), sem("gate_ln"), sem("gate_em"), sem("gate_m"), sem("a_ready"),
            sem("a_turned"), sem("acol_ready"))
        taken_v, taken_s = sem("taken_v"), sem("taken_s")
        conv_done, act_done, rot_done = sem("conv_done"), sem("act_done"), sem("rot_done")
        bc_done, bc_copied, arg_ready, exp_ready = sem("bc_done"), sem("bc_copied"), sem("arg_ready"), sem("exp_ready")
        scores_done, sT_ready, pv_done = sem("scores_done"), sem("sT_ready"), sem("pv_done")
        hn_ready, mean_done, hc_ready, sq_ready, var_done, sd_ready = (
            sem("hn_ready"), sem("mean_done"), sem("hc_ready"), sem("sq_ready"), sem("var_done"), sem("sd_ready"))
        y_ready, yhi_ready, ylo_ready = sem("y_ready"), sem("yhi_ready"), sem("ylo_ready")
        gemm_taken, sig_ready, sq2_ready, hss_done, hstd_ready, hr_ready, hbc_done, qn_ready = (
            sem("gemm_taken"), sem("sig_ready"), sem("sq2_ready"), sem("hss_done"), sem("hstd_ready"), sem("hr_ready"),
            sem("hbc_done"), sem("qn_ready"))
        v2_ready, sc2_done, s2_ready, p2_sum, p2_ready, pT_done, pT_ready, o2_done, o2_ready = (
            sem("v2_ready"), sem("sc2_done"), sem("s2_ready"), sem("p2_sum"), sem("p2_ready"), sem("pT_done"),
            sem("pT_ready"), sem("o2_done"), sem("o2_ready"))
        conv_step, zc_ready, zmean_done, zsq_ready, zvar_done, zstd_ready, zn_ready, zact_ready = (
            sem("conv_step"), sem("zc_ready"), sem("zmean_done"), sem("zsq_ready"), sem("zvar_done"),
            sem("zstd_ready"), sem("zn_ready"), sem("zact_ready"))
        y2hi_ready, y2lo_ready = sem("y2hi_ready"), sem("y2lo_ready")
        fg_ready, fa_ready, fhi_ready, flo_ready = sem("fg_ready"), sem("fa_ready"), sem("fhi_ready"), sem("flo_ready")
        logits_done, e_ready, route_ready, rank_done, jobs_ready, htok_done, htok_ready = (
            sem("logits_done"), sem("e_ready"), sem("route_ready"), sem("rank_done"), sem("jobs_ready"),
            sem("htok_done"), sem("htok_ready"))
        route_exp, pick_ready, xg_done, xghi_ready, xglo_ready = (
            sem("route_exp"), sem("pick_ready"), sem("xg_done"), sem("xghi_ready"), sem("xglo_ready"))
        mg_ready, ma_ready, turned, thi_ready, tlo_ready = (
            sem("mg_ready"), sem("ma_ready"), sem("turned"), sem("thi_ready"), sem("tlo_ready"))
        pickT_done, pickT_ready, yexp_ready, spread_done, spread_taken = (
            sem("pickT_done"), sem("pickT_ready"), sem("yexp_ready"), sem("spread_done"), sem("spread_taken"))
        out_turned, out_ready = sem("out_turned"), sem("out_ready")
        vector_step, scalar_step = sem("vector_step"), sem("scalar_step")
        block = ctx.enter_context(nc.Block())

        @block.sync
        def _(sp):
            sp.dma_start(cst[:], consts).then_inc(const_in, 16)
            sp.dma_start(xtok[:], x[0].rearrange("(t p) d -> p t d", p=P)).then_inc(x_in, 16)

            r = 0
            for l in range(L):
                for w, cols in ((w_ada, 3 * D), (w_ada_2, 6 * D)):
                    for n in range(cols // 256):
                        if r >= RAW:
                            sp.wait_ge(raw_free, r - RAW + 1)
                        sp.dma_start(raw[:, r % RAW, :].rearrange("p (k n) -> p k n", k=KD),
                                     w[l].rearrange("(k p) n -> p k n", p=P)[:, :, 256 * n:256 * n + 256])\
                            .then_inc(raw_in[r % RAW], 16)
                        r += 1
            assert r == ADA_UNITS

            def load(u, src, k):
                sp.wait_ge(raw_free, u.ring(1 - RAW))
                sp.dma_start(raw[:, u.raw, :].rearrange("p (k n) -> p k n", k=k), src).then_inc(raw_in[u.raw], 16)

            for l in range(L):
                wl = w_in[l].rearrange("(k p) n -> p k n", p=P)
                u0 = Unit(S_B1 + l * UNIT_L1)
                with sp.Fori(0, NPAIR) as pair:
                    for j in range(2 * HEAD_UNITS):
                        part, hh = j % HEAD_UNITS, j // HEAD_UNITS
                        col = part * D_MLSTM if part < 5 else RET_COL + (part - 5) * D_RET
                        load(Unit(u0.n + j, pair, 2 * HEAD_UNITS), wl[:, :, bass.ds(pair * (2 * HD) + (col + hh * HD), HD)], KD)
                for j in range(OUT1_UNITS):
                    load(Unit(u0.n + H * HEAD_UNITS + j),
                         w_out[l].rearrange("(k p) n -> p k n", p=P)[:, 2 * j:2 * j + 2, :], 2)

            def mixer_loads(l, first):
                wl = w_in_2[l].rearrange("(k p) n -> p k n", p=P)
                for j, col in enumerate((0, 2, 1, 3, 4, 5, 6, 7, 8, 9)):
                    load(Unit(first + j), wl[:, :, 256 * col:256 * col + 256], KD)
                for j, d in enumerate((2, 3, 0, 1)):
                    load(Unit(first + MIX_UNITS + j),
                         w_out_2[l].rearrange("(k p) n -> p k n", p=P)[:, 2 * d:2 * d + 2, :], 2)

            mixer_loads(0, S_B2)
            for j in range(FF_UNITS):
                w = (ffn_w_gate, ffn_w_up)[j % 2][0]
                load(Unit(S_FF + j), w.rearrange("(k p) n -> p k n", p=P)[:, :, 128 * (j - j % 2):128 * (j - j % 2) + 256], KD)
            for j in range(DOWN_UNITS):
                load(Unit(S_FF + FF_UNITS + j), ffn_w_down[0].rearrange("(k p) n -> p k n", p=P)[:, 2 * j:2 * j + 2, :], 2)
            mixer_loads(1, S_B3)

            def job_loads(e, turn, first, units):
                wg, wu = (w[0, bass.ds(e, 1)].rearrange("e (k p) n -> p (e k) n", p=P) for w in (moe_w_gate, moe_w_up))
                wd = moe_w_down[0, bass.ds(e, 1)].rearrange("e (k p) n -> p (e k) n", p=P)
                for j in units:
                    u = Unit(first + j, turn, JOB_UNITS)
                    if j < JOB_UP:
                        w, c, half = (wg, wu)[j % 4 // 2], j // 4, j % 2
                        load(u, w[:, 4 * half:4 * half + 4, 512 * c:512 * c + 512], 4)
                    else:
                        f = 2 * (j - JOB_UP)
                        load(u, wd[:, f:f + 2, :], 2)

            with sp.Fori(0, NE) as e:
                job_loads(e, e, S_MOE, range(JOB_UNITS))
            sp.wait_ge(jobs_ready, 1)
            nx = sp.value_load(jobs[0:1, 0:1], min_val=0, max_val=3)
            e = sp.value_load(jobs[0:1, 1:2], min_val=0, max_val=NE - 1)
            job_loads(e, NE, S_MOE, range(LOOK))
            with sp.If(nx > 0):
                with sp.Fori(0, nx) as j:
                    e = sp.value_load(jobs[0:1, bass.ds(j + 1, 1)], min_val=0, max_val=NE - 1)
                    job_loads(e, j, S_MOE + NE * JOB_UNITS, range(LOOK, JOB_UNITS))
                    e2 = sp.value_load(jobs[0:1, bass.ds(j + 2, 1)], min_val=0, max_val=NE - 1)
                    job_loads(e2, j, S_MOE + (NE + 1) * JOB_UNITS, range(LOOK))
            for t in range(2):
                sp.wait_ge(out_ready, t + 1)
                sp.dma_start(out[0, t * P:(t + 1) * P, :], otok[:, t]).then_inc(stored, 16)
            sp.wait_ge(stored, 32)

        @block.gpsimd
        def _(pool):
            pool.dma_start(posi[:], positions[0:1, :].broadcast_to([P, S])).then_inc(pos_in, 16)
            n = 0

            def row(dst, src):
                nonlocal n
                pool.dma_start(dst, src).then_inc(rows_in, 16)
                n += 1

            for l in range(L):
                for at, v in ((P1_BADA, b_ada[l]), (P1_NORM, norm_g[l]), (P1_CB, conv_b[l]), (P1_GNM, gn_m[l]), (P1_GNR, gn_r[l])):
                    k = v.shape[0] // P
                    row(prow[at:at + k, l, :], v.rearrange("(k p) -> k p", p=P))
                row(prow[P1_CW:P1_CW + 64, l, :], conv_w[l].rearrange("t (k p) -> (t k) p", p=P))
                for at, v in ((P2_BADA, b_ada_2[l]), (P2_MIX, norm_mix_g[l]), (P2_FFN, norm_ffn_g[l]), (P2_CB, conv_b_2[l]),
                              (P2_LG, conv_ln_g[l]), (P2_LB, conv_ln_b[l])):
                    k = v.shape[0] // P
                    row(prow[at:at + k, 2 + l, :], v.rearrange("(k p) -> k p", p=P))
                for at, v in ((P2_QN, q_norm_g[l:l + 1, :]), (P2_KN, k_norm_g[l:l + 1, :])):
                    for half in range(2):
                        row(prow[at:at + 1, 2 + l, half * HD2:(half + 1) * HD2], v)
                row(prow[0:CW * CT, 4 + l, :], conv_w_2[l, :, 0, :].rearrange("t (k p) -> (t k) p", p=P))
            row(prow[P2_C:P2_C + KD, 2, :], c[0].rearrange("(k p) -> k p", p=P))
            row(prow[P2_C2:P2_C2 + KD, 2, :], c_2[0].rearrange("(k p) -> k p", p=P))
            row(prow[P2_FIN:P2_FIN + KD, 2, :], final_g.rearrange("(k p) -> k p", p=P))
            assert 16 * n == ROWS_LOADED, n
            for l in range(L):
                pool.dma_start(wgate[:, l], w_in[l].rearrange("(k p) n -> p k n", p=P)[:, :, GATE_COL:RET_COL]).then_inc(gate_in, 16)
                pool.dma_start(gbias[:, l, 0:1], b_igate[l].rearrange("(h o) -> h o", o=1)).then_inc(gate_in, 16)
                pool.dma_start(gbias[:, l, 1:2], b_fgate[l].rearrange("(h o) -> h o", o=1)).then_inc(gate_in, 16)
            for l in range(L):
                pool.dma_start(ext[l, :, 0:127].unsqueeze(2), rel_bias[l, :, 0:1].unsqueeze(1).broadcast_to([NH2, 127, 1])).then_inc(ext_out, 16)
                pool.dma_start(ext[l, :, 127:EXT], rel_bias[l]).then_inc(ext_out, 16)
            pool.wait_ge(ext_out, 16 * 2 * L)
            for l in range(L):
                pool.dma_start(rep[l], ext[l].unsqueeze(1).broadcast_to([NH2, P, EXT])).then_inc(ext_out, 16)
            pool.wait_ge(ext_out, 16 * 3 * L)
            for l in range(L):
                pool.wait_ge(x_ready, N_FINAL + 1 if l == 0 else N_MIX[1] + 1)
                src = bass.AP(tensor=rep.tensor, offset=l * NH2 * P * EXT + 127, ap=[[EXT - 1, P], [P * EXT, NH2], [1, S]])
                pool.dma_start(bias2[:], src).then_inc(bias_in, 16)
            pool.wait_ge(x_ready, N_FFN[1] + 1)
            pool.dma_start(wr[:], w_router[0].rearrange("(k p) n -> p k n", p=P)).then_inc(router_in, 16)
            pool.dma_start(rb[:], b_router[0:1, :].broadcast_to([P, NE])).then_inc(router_in, 16)

        class Head:

            def __init__(self, layer, hh, pair):
                self.n, self.pair, self.h = H * layer + hh, pair, pair * 2 + hh

            def count(self, per, k):
                return self.pair * (2 * per) + (self.n * per + k)

        class Job:

            def __init__(self, n, turn):
                self.n, self.turn = n, turn

            def count(self, per, k):
                return self.turn * per + (self.n * per + k)

            def unit(self, i):
                return Unit(S_MOE + self.n * JOB_UNITS + i, self.turn, JOB_UNITS)

        def split_no(n):
            return n if n < N_FINAL else n - 1

        @block.scalar
        def _(act):
            step = Chain(act, scalar_step)

            def high(u):
                act.wait_ge(raw_in[u.raw], u.loads)
                if u.n >= HL or u.per:
                    act.wait_ge(unit_done, u.count(1 - HL))
                nc.scalar.copy(whi[:, u.hl, :], raw[:, u.raw, :]).then_inc(hi_ready, 1)

            def norm(n):
                act.wait_ge(x_ready, n + 1)
                nc.scalar.activation(h[:], xT[:], ACT.Square).then_inc(squares, 1)
                act.wait_ge(sum_ready, n + 1)
                nc.scalar.activation(rstd[:], ps2[7][:, 0], ACT.Sqrt, bias=eps[:], scale=1.0 / D).then_inc(std_ready, 1)
                if n != N_FINAL:
                    for half in range(2):
                        act.wait_ge(h_ready, 2 * split_no(n) + half + 1)
                        nc.scalar.copy(hhi[:, 4 * half:4 * half + 4], h[:, 4 * half:4 * half + 4]).then_inc(hhi_ready, 1)

            act.wait_ge(cols_ready, 1)
            nc.scalar.activation(cact[:], par2[:, 0, P2_C:P2_C + 2 * KD].rearrange("p (a k) -> p a k", a=2), ACT.Silu)\
                .then_inc(cact_ready, 1)
            act.wait_ge(angle_ready, 1)
            nc.scalar.activation(sinT[:], ang[:], ACT.Sin).then_inc(sin_ready, 1)
            step(nc.scalar.activation(turns[:, 0], ang[:], ACT.Abs))
            step(nc.scalar.activation(turns[:, 1], turns[:, 0], ACT.Copy, bias=float(np.pi / 2), scale=-1.0))
            nc.scalar.activation(cosT[:], turns[:, 1], ACT.Sin).then_inc(sin_ready, 1)

            for i in range(LOOK):
                high(Unit(S_B1 + i))
            for l in range(L):
                norm(l)
                act.wait_ge(gate_f, l + 1)
                step(nc.scalar.activation(gt[:, 2], gt[:, 1], ACT.Abs))
                step(nc.scalar.activation(gt[:, 2], gt[:, 2], ACT.Exp, scale=-1.0))
                nc.scalar.activation(gt[:, 2], gt[:, 2], ACT.Ln, bias=ones[0:H, 0:1]).then_inc(gate_ln, 1)
                act.wait_ge(gate_m, l + 1)
                nc.scalar.activation(gt[:, 7], gt[:, 7], ACT.Exp, scale=-1.0).then_inc(gate_em, 1)
                with act.Fori(0, NPAIR) as pair:
                    for hh in range(2):
                        hd = Head(l, hh, pair)
                        u0 = Unit(S_B1 + l * UNIT_L1 + hh * HEAD_UNITS, pair, 2 * HEAD_UNITS)
                        q, k, v, o, z, rq, rk, rv, rz = (u0.plus(i) for i in range(HEAD_UNITS))
                        high(q.plus(LOOK))
                        high(k.plus(LOOK))
                        high(v.plus(LOOK))
                        act.wait_ge(unit_done, v.count())
                        nc.scalar.copy(vtok[:], ps2[v.bank]).then_inc(taken_s, 1)
                        act.wait_ge(conv_done, hd.count(1, 1))
                        nc.scalar.activation(qk[:], qacc[:], ACT.Silu).then_inc(act_done, 1)
                        high(o.plus(LOOK))
                        act.wait_ge(bc_done, hd.count(1, 1))
                        nc.scalar.copy(bcs[:], ps2[3]).then_inc(bc_copied, 1)
                        act.wait_ge(unit_done, o.count())
                        nc.scalar.activation(osig[:], ps2[o.bank], ACT.Tanh, scale=0.5).then_inc(taken_s, 1)
                        high(z.plus(LOOK))
                        act.wait_ge(arg_ready, hd.count(1, 1))
                        nc.scalar.activation(arg[:], arg[:], ACT.Exp).then_inc(exp_ready, 1)
                        act.wait_ge(unit_done, z.count())
                        nc.scalar.activation(zsil[:], ps2[z.bank], ACT.Silu).then_inc(taken_s, 1)
                        high(rq.plus(LOOK))
                        high(rk.plus(LOOK))
                        act.wait_ge(hc_ready, hd.count(2, 1))
                        nc.scalar.activation(sq, hn[:], ACT.Square).then_inc(sq_ready, 1)
                        high(rv.plus(LOOK))
                        act.wait_ge(var_done, hd.count(2, 1))
                        nc.scalar.activation(sq[:, 0], ps2[6][:, 1], ACT.Sqrt, bias=eps[:]).then_inc(sd_ready, 1)
                        act.wait_ge(unit_done, rv.count())
                        nc.scalar.copy(vtok[:], ps2[rv.bank]).then_inc(taken_s, 1)
                        high(rz.plus(LOOK))
                        act.wait_ge(y_ready, hd.count(2, 1))
                        nc.scalar.copy(yhi[:, bass.ds(hd.h * 2, 2), :], yf).then_inc(yhi_ready, 1)
                        act.wait_ge(unit_done, rz.count())
                        nc.scalar.activation(zsil[:], ps2[rz.bank], ACT.Silu).then_inc(taken_s, 1)
                        act.wait_ge(hc_ready, hd.count(2, 2))
                        nc.scalar.activation(sq, hn[:], ACT.Square).then_inc(sq_ready, 1)
                        act.wait_ge(var_done, hd.count(2, 2))
                        nc.scalar.activation(sq[:, 0], ps2[6][:, 1], ACT.Sqrt, bias=eps[:]).then_inc(sd_ready, 1)
                        act.wait_ge(y_ready, hd.count(2, 2))
                        nc.scalar.copy(yhi[:, bass.ds(hd.h * 2 + KD, 2), :], yf).then_inc(yhi_ready, 1)
                for j in range(OUT1_UNITS):
                    high(Unit(S_B1 + l * UNIT_L1 + H * HEAD_UNITS + j + LOOK))
            norm(N_FINAL)

            def mixer(l, first):
                norm(N_MIX[l])
                for j in range(MIX_UNITS):
                    u = Unit(first + j)
                    high(u.plus(LOOK))
                    if j in (1, 3):
                        act.wait_ge(unit_done, u.count())
                        if j == 3:
                            act.wait_ge(gemm_taken, 6 * l + 1)
                        nc.scalar.activation(sig[:], ps2[u.bank], ACT.Tanh, scale=0.5).then_inc(sig_ready, 1)
                    if j in (5, 7):
                        i = j // 2 - 2
                        act.wait_ge(gemm_taken, 6 * l + 4 + 2 * i)
                        nc.scalar.activation(sq2[:, i], q2[:, i], ACT.Square).then_inc(sq2_ready, 1)
                    if j >= 8:
                        act.wait_ge(unit_done, u.count())
                        nc.scalar.copy(v2[:, :, 256 * (j - 8):256 * (j - 7)], ps2[u.bank]).then_inc(v2_ready, 1)
                act.wait_ge(hss_done, l + 1)
                nc.scalar.activation(rs2[:], ps2[2][0:NH2], ACT.Sqrt, bias=eps[0:NH2]).then_inc(hstd_ready, 1)
                for n in range(NH2):
                    b, at = n % 2, NH2 * l + n
                    act.wait_ge(s2_ready, at + 1)
                    step.mark(nc.scalar.activation(p2[:, b, 0:P], s2[:, b, 0:P], ACT.Exp, bias=st2[:, b, 2:3],
                                                   accum_out=st2[:, b, 4:5]))
                    nc.scalar.activation(p2[:, b, P:P + S], s2[:, b, P:P + S], ACT.Exp, bias=st2[:, b, 3:4],
                                         accum_out=st2[:, b, 5:6]).then_inc(p2_sum, 1)
                    if n % 2 == 0 and n:
                        act.wait_ge(o2_done, at)
                        nc.scalar.copy(y2hi[:, CT + n // 2 - 1], ps2[6 + (n // 2 - 1) % 2][:, 0]).then_inc(y2hi_ready, 1)
                act.wait_ge(o2_done, NH2 * (l + 1))
                nc.scalar.copy(y2hi[:, KD - 1], ps2[7][:, 0]).then_inc(y2hi_ready, 1)
                for j in range(2):
                    high(Unit(first + MIX_UNITS + LOOK + j))
                act.wait_ge(zc_ready, l + 1)
                nc.scalar.activation(sq2[:, 0], zacc[:], ACT.Square).then_inc(zsq_ready, 1)
                act.wait_ge(zvar_done, l + 1)
                nc.scalar.activation(sig[:, 0], ps2[1][:, 0], ACT.Sqrt, bias=eps[:]).then_inc(zstd_ready, 1)
                act.wait_ge(zn_ready, l + 1)
                for t in range(CT):
                    step(nc.scalar.activation(q2[:, 0, t], zacc[:, t], ACT.Silu, bias=par2[:, l, P2_LB + t:P2_LB + t + 1],
                                              scale=par2[:, l, P2_LG + t:P2_LG + t + 1]))
                nc.scalar.copy(y2hi[:, 0:CT], q2[:, 0]).then_inc(y2hi_ready, 1)
                for j in range(2, OUT2_UNITS):
                    high(Unit(first + MIX_UNITS + LOOK + j))

            mixer(0, S_B2)
            norm(N_FFN[0])
            for j in range(FF_UNITS):
                u, i = Unit(S_FF + j), j // 2
                high(u.plus(LOOK))
                if j % 2 == 0:
                    act.wait_ge(unit_done, u.count())
                    nc.scalar.activation(fg[:, i % 2], ps2[u.bank], ACT.Silu).then_inc(fg_ready, 1)
                else:
                    act.wait_ge(fa_ready, i + 1)
                    nc.scalar.copy(fhi[:, 2 * i:2 * i + 2], fa[:, i % 2]).then_inc(fhi_ready, 1)
            for j in range(DOWN_UNITS):
                high(Unit(S_FF + FF_UNITS + j + LOOK))
            mixer(1, S_B3)
            norm(N_FFN[1])
            act.wait_ge(htok_done, 1)
            step.mark(nc.scalar.copy(htok[:, 0, 0:512], ps[0][:, :]))
            nc.scalar.copy(htok[:, 0, 512:D], ps[1][:, :]).then_inc(htok_ready, 1)
            act.wait_ge(e_ready, 1)
            nc.scalar.activation(lg[:, 11, 0, 0:2], lg[:, 10, 1, 0:2], ACT.Exp).then_inc(route_exp, 1)

            def take_tokens(gather, half):
                act.wait_ge(xg_done, gather.count(2, half + 1))
                nc.scalar.copy(xghi[:, 4 * half:4 * half + 4], ps4[7]).then_inc(xghi_ready, 1)

            def expert(job, following):
                for i in range(JOB_UNITS):
                    high(job.unit(i + LOOK))
                    c = i // 4
                    if i < JOB_UP and i % 4 == 1:
                        act.wait_ge(unit_done, job.unit(i).count())
                        nc.scalar.activation(mg[:, c % 2], ps[c % 2][:, :], ACT.Silu).then_inc(mg_ready, 1)
                    if i % 4 == 2 and 1 <= c <= JOB_UP // 4:
                        act.wait_ge(turned, job.count(JOB_UP // 4, c))
                        nc.scalar.copy(thi[:, 4 * c - 4:4 * c], ps4[4]).then_inc(thi_ready, 1)
                    if following is not None and i in (JOB_UP + 2, JOB_UP + 6):
                        take_tokens(following, (i - JOB_UP) // 4)
                act.wait_ge(unit_done, job.unit(JOB_UNITS - 1).count())
                step.mark(nc.scalar.copy(yexp[:, 0:512], ps[5][:, :]))
                nc.scalar.copy(yexp[:, 512:D], ps[6][:, :]).then_inc(yexp_ready, 1)

            for half in range(2):
                take_tokens(Job(0, 0), half)
            with act.Fori(0, NE) as e:
                step.enter(e, 1)
                expert(Job(0, e), Job(1, e))
            step.leave(NE)
            act.wait_ge(jobs_ready, 1)
            nx = act.value_load(jobs[0:1, 0:1], min_val=0, max_val=3)
            with act.If(nx > 0):
                with act.Fori(0, nx) as j:
                    step.enter(j, 1)
                    for half in range(2):
                        take_tokens(Job(NE + 1, j), half)
                    expert(Job(NE, j), None)
            for t in range(2):
                act.wait_ge(out_turned, 2 * t + 1)
                nc.scalar.copy(otok[:, t, 0:512], ps[2 * t][:, :]).then_inc(scalar_step, 1)
                act.wait_ge(out_turned, 2 * t + 2)
                nc.scalar.copy(otok[:, t, 512:D], ps[2 * t + 1][:, :]).then_inc(out_ready, 1)

        @block.tensor
        def _(pe):
            mm = nc.tensor.matmul

            def products(u):
                pe.wait_ge(raw_free, u.ring())
                for j in range(2):
                    for k in range(KD):
                        w = slice(256 * k + P * j, 256 * k + P * j + P)
                        mm(ps2[u.bank][:, j], whi[:, u.hl, w], hhi[:, k], start=k == 0, stop=False)
                        mm(ps2[u.bank][:, j], whi[:, u.hl, w], hlo[:, k], start=False, stop=False)
                        last = mm(ps2[u.bank][:, j], wlo[:, u.hl, w], hhi[:, k], start=False, stop=k == KD - 1)
                last.then_inc(unit_done, 1)

            def token_products(u):
                pe.wait_ge(raw_free, u.ring())
                for t in range(2):
                    for k in range(KD):
                        w, s = slice(256 * k, 256 * k + 256), slice(P * t, P * t + P)
                        mm(ps2[u.bank][:, t], hhi[:, k, s], whi[:, u.hl, w], start=k == 0, stop=False)
                        mm(ps2[u.bank][:, t], hlo[:, k, s], whi[:, u.hl, w], start=False, stop=False)
                        last = mm(ps2[u.bank][:, t], hhi[:, k, s], wlo[:, u.hl, w], start=False, stop=k == KD - 1)
                last.then_inc(unit_done, 1)

            def rows_product(u, hi, lo, tile, first, final):
                pe.wait_ge(raw_free, u.ring())
                for i in range(2):
                    for d in range(KD):
                        w = slice(D * i + P * d, D * i + P * d + P)
                        o = ps2[2 + d // 2][:, d % 2]
                        start, stop = first and i == 0 and d % 2 == 0, final and i == 1
                        mm(o, whi[:, u.hl, w], hi[:, tile + i], start=start, stop=False, skip_group_check=True)
                        mm(o, whi[:, u.hl, w], lo[:, tile + i], start=False, stop=False, skip_group_check=True)
                        last = mm(o, wlo[:, u.hl, w], hi[:, tile + i], start=False, stop=stop, skip_group_check=True)
                last.then_inc(unit_done, 1)

            def norm(n):
                pe.wait_ge(squares, n + 1)
                for k in range(KD):
                    last = mm(ps2[7][:, 0], ones[:, 0:P], h[:, k], start=k == 0, stop=k == KD - 1)
                last.then_inc(sum_ready, 1)

            pe.wait_ge(const_in, 16)
            pe.wait_ge(x_in, 16)
            for k in range(KD):
                for t in range(2):
                    last = nc.tensor.transpose(ps2[k // 2][:, k % 2, t * P:(t + 1) * P], xtok[:, t, k * P:(k + 1) * P], ident)
            last.then_inc(x_turned, 1)
            pe.wait_ge(rows_in, ROWS_LOADED)
            for i, rows in enumerate((P, P) + P2_ROWS + (CW * CT, CW * CT)):
                last = nc.tensor.transpose(ps4[4 + i // 4][:, i % 4, 0:rows], prow[0:rows, i, :], ident[0:rows, 0:rows])
            last.then_inc(rows_turned, 1)
            pe.wait_ge(memset_done, 1)
            for r in range(ADA_UNITS):
                pe.wait_ge(raw_free, r + 1)
                for j in range(2):
                    last = mm(ps[6][:, 2 * r + j:2 * r + j + 1], acc[:, r % 2, j * P:(j + 1) * P], ones[:, 0:1],
                              start=True, stop=True)
                last.then_inc(ada_done, 1)

            for l in range(L):
                norm(l)
                pe.wait_ge(gate_in, 16 * 3 * L)
                pe.wait_ge(h_ready, 2 * l + 2)
                for g in range(2):
                    for k in range(KD):
                        last = mm(ps2[7][0:H, g], wgate[:, l, k, g * H:(g + 1) * H], h[:, k], start=k == 0, stop=k == KD - 1)
                last.then_inc(gates_done, 1)
                pe.wait_ge(a_ready, l + 1)
                for t in range(2):
                    last = mm(ps[7][:, t * H:(t + 1) * H], gt[:, 5, t * P:(t + 1) * P], ident[0:H, 0:H], start=True, stop=True)
                last.then_inc(a_turned, 1)
                pe.wait_ge(hlo_ready, 2 * l + 2)
                if l == 0:
                    pe.wait_ge(sin_ready, 2)

                def scores(x):
                    for s, (o, t) in enumerate(((ps[2][:, 0:S], slice(0, S)), (ps[2][:, S:S + P], slice(P, S)))):
                        for d in range(2):
                            last = mm(o, x[:, 1, d, s * P:(s + 1) * P], x[:, 0, d, t], start=d == 0, stop=d == 1)
                    last.then_inc(scores_done, 1)

                def values(normaliser):
                    for o, w in [(ps2[4][:, v], lambda s, v=v: vtok[:, s, v * P:(v + 1) * P]) for v in range(2)] + \
                            ([(ps2[5][:, 0], lambda s: ones[:, 0:P])] if normaliser else []):
                        mm(o, w(0), sT[:, 0:S], start=True, stop=False)
                        last = mm(o[:, P:S], w(1), sT[:, S:S + P], start=False, stop=True)
                    last.then_inc(pv_done, 1)

                def head_mean(x, half, done):
                    for v in range(2):
                        last = mm(ps2[6][:, half], mean256[:], x[:, v], start=v == 0, stop=v == 1)
                    last.then_inc(done, 1)

                with pe.Fori(0, NPAIR) as pair:
                    for hh in range(2):
                        hd = Head(l, hh, pair)
                        u0 = Unit(S_B1 + l * UNIT_L1 + hh * HEAD_UNITS, pair, 2 * HEAD_UNITS)
                        q, k, v, o, z, rq, rk, rv, rz = (u0.plus(i) for i in range(HEAD_UNITS))
                        products(q)
                        products(k)
                        pe.wait_ge(taken_v, hd.count(4, 1))
                        token_products(v)
                        mm(ps[3][:, :], ones[0:H, 0:P], gdiag[:, bass.ds(hd.h, 1)].rearrange("p a b s -> p (a b s)"),
                           start=True, stop=True).then_inc(bc_done, 1)
                        pe.wait_ge(taken_v, hd.count(4, 2))
                        products(o)
                        pe.wait_ge(act_done, hd.count(1, 1))
                        scores(qk)
                        pe.wait_ge(taken_s, hd.count(5, 1))
                        products(z)
                        pe.wait_ge(sT_ready, hd.count(2, 1))
                        values(True)
                        pe.wait_ge(taken_s, hd.count(5, 2))
                        products(rq)
                        pe.wait_ge(hn_ready, hd.count(2, 1))
                        head_mean(hn, 0, mean_done)
                        pe.wait_ge(taken_s, hd.count(5, 3))
                        products(rk)
                        pe.wait_ge(sq_ready, hd.count(2, 1))
                        head_mean(sq, 1, var_done)
                        pe.wait_ge(taken_v, hd.count(4, 3))
                        token_products(rv)
                        pe.wait_ge(rot_done, hd.count(1, 1))
                        scores(rot)
                        pe.wait_ge(taken_v, hd.count(4, 4))
                        products(rz)
                        pe.wait_ge(sT_ready, hd.count(2, 2))
                        pe.wait_ge(taken_s, hd.count(5, 4))
                        values(False)
                        pe.wait_ge(taken_s, hd.count(5, 5))
                        pe.wait_ge(hn_ready, hd.count(2, 2))
                        head_mean(hn, 0, mean_done)
                        pe.wait_ge(sq_ready, hd.count(2, 2))
                        head_mean(sq, 1, var_done)
                pe.wait_ge(ylo_ready, 2 * H * (l + 1))
                for j in range(OUT1_UNITS):
                    rows_product(Unit(S_B1 + l * UNIT_L1 + H * HEAD_UNITS + j), yhi, ylo, 2 * j, j == 0, j == OUT1_UNITS - 1)
            norm(N_FINAL)

            def mixer(l, first):
                n0 = NH2 * l
                norm(N_MIX[l])
                pe.wait_ge(hlo_ready, 2 * split_no(N_MIX[l]) + 2)
                free = {2: (gemm_taken, 6 * l + 1), 3: (sig_ready, 2 * l + 1), 4: (gemm_taken, 6 * l + 2),
                        5: (sig_ready, 2 * l + 2), 6: (gemm_taken, 6 * l + 3), 7: (gemm_taken, 6 * l + 4),
                        8: (gemm_taken, 6 * l + 5), 9: (gemm_taken, 6 * l + 6)}
                for j in range(MIX_UNITS):
                    u = Unit(first + j)
                    if j in free:
                        pe.wait_ge(*free[j])
                    (token_products if j >= 8 else products)(u)
                    if j == 8:
                        for i in range(2):
                            pe.wait_ge(sq2_ready, 2 * l + i + 1)
                            for t in range(CT):
                                last = mm(ps2[2][0:NH2, i], hsum[:, t, :], sq2[:, i, t], start=t == 0, stop=t == CT - 1)
                        last.then_inc(hss_done, 1)
                pe.wait_ge(hr_ready, l + 1)
                for i in range(2):
                    for t in range(CT):
                        last = mm(ps2[3 + 2 * i + t // 2][:, t % 2], hbc[:, t, :], rs2[:, i], start=True, stop=True)
                last.then_inc(hbc_done, 1)

                def scores(n):
                    o, part = ps[2 + n % 2], slice(HD2 * (n % 2), HD2 * (n % 2) + HD2)
                    if n >= 2:
                        pe.wait_ge(s2_ready, n0 + n - 1)
                    mm(o[:, 0:P], q2[part, 0, n // 2, 0:P], q2[part, 1, n // 2, 0:P], start=True, stop=True)
                    mm(o[:, P:P + S], q2[part, 0, n // 2, P:S], q2[part, 1, n // 2, 0:S], start=True, stop=True)\
                        .then_inc(sc2_done, 1)

                pe.wait_ge(qn_ready, l + 1)
                pe.wait_ge(v2_ready, 2 * l + 2)
                scores(0)
                for n in range(NH2):
                    if n + 1 < NH2:
                        scores(n + 1)
                    pe.wait_ge(p2_ready, n0 + n + 1)
                    if n >= 2:
                        pe.wait_ge(pT_ready, n0 + n - 1)
                    for i in range(3):
                        last = nc.tensor.transpose(ps[4 + n % 2][:, i * P:(i + 1) * P], p2[:, n % 2, i * P:(i + 1) * P], ident)
                    last.then_inc(pT_done, 1)
                    pe.wait_ge(pT_ready, n0 + n + 1)
                    if n % 2 == 0 and n >= 4:
                        pe.wait_ge(y2lo_ready, (CT + 1) * l + n // 2 - 1)
                    o = ps[6 + n // 2 % 2][HD2 * (n % 2):HD2 * (n % 2) + HD2, 0:S]
                    mm(o, v2[:, 0, HD2 * n:HD2 * n + HD2], pT[:, n % 2, 0:S], start=True, stop=False)
                    mm(o[:, P:S], v2[:, 1, HD2 * n:HD2 * n + HD2], pT[:, n % 2, S:S + P], start=False, stop=True)\
                        .then_inc(o2_done, 1)
                for j in range(OUT2_UNITS):
                    u = Unit(first + MIX_UNITS + j)
                    if j == 0:
                        pe.wait_ge(y2lo_ready, (CT + 1) * l + CT)
                    if j == 2:
                        pe.wait_ge(y2lo_ready, (CT + 1) * (l + 1))
                    rows_product(u, y2hi, y2lo, (4, 6, 0, 2)[j], j == 0, j == OUT2_UNITS - 1)
                    if j == 1:
                        pe.wait_ge(conv_step, CW * CT * (l + 1))
                        for t in range(CT):
                            last = mm(ps2[0][:, 0], mean512[:], zacc[:, t], start=t == 0, stop=t == CT - 1)
                        last.then_inc(zmean_done, 1)
                        pe.wait_ge(zsq_ready, l + 1)
                        for t in range(CT):
                            last = mm(ps2[1][:, 0], mean512[:], sq2[:, 0, t], start=t == 0, stop=t == CT - 1)
                        last.then_inc(zvar_done, 1)

            mixer(0, S_B2)
            norm(N_FFN[0])
            pe.wait_ge(hlo_ready, 2 * split_no(N_FFN[0]) + 2)
            for j in range(FF_UNITS):
                if j >= 2:
                    pe.wait_ge((fg_ready, fa_ready)[j % 2], j // 2)
                products(Unit(S_FF + j))
            for j in range(DOWN_UNITS):
                pe.wait_ge(flo_ready, j + 1)
                rows_product(Unit(S_FF + FF_UNITS + j), fhi, flo, 2 * j, j == 0, j == DOWN_UNITS - 1)
            mixer(1, S_B3)
            norm(N_FFN[1])

            pe.wait_ge(router_in, 32)
            pe.wait_ge(h_ready, 2 * split_no(N_FFN[1]) + 2)
            for t in range(2):
                for k in range(KD):
                    last = mm(ps[7][:, t * NE:(t + 1) * NE], h[:, k, t * P:(t + 1) * P], wr[:, k], start=k == 0, stop=k == KD - 1)
            last.then_inc(logits_done, 1)
            for t in range(2):
                for k in range(KD):
                    last = nc.tensor.transpose(ps[2 * t + k // 4][:, P * (k % 4):P * (k % 4) + P], h[:, k, t * P:(t + 1) * P], ident)
            last.then_inc(htok_done, 1)
            pe.wait_ge(route_ready, 1)
            chosen = [lg[:, 9, t] for t in range(2)]
            mm(ps[6][:, 0:NE], before, chosen[0], start=True, stop=True)
            mm(ps[6][:, NE:2 * NE], ones[:, 0:P], chosen[0], start=True, stop=False)
            mm(ps[6][:, NE:2 * NE], before, chosen[1], start=False, stop=True)
            mm(ps[6][:, 2 * NE:3 * NE], ones[:, 0:P], chosen[0], start=True, stop=False)
            mm(ps[6][:, 2 * NE:3 * NE], ones[:, 0:P], chosen[1], start=False, stop=True).then_inc(rank_done, 1)

            def gather(g, half):
                for kk in range(4):
                    for t in range(2):
                        k = 4 * half + kk
                        last = mm(ps4[7][:, kk], htok[:, t, k * P:(k + 1) * P], pick[:, t], start=t == 0, stop=t == 1)
                last.then_inc(xg_done, 1)

            def spread(job, rnd):
                for i in range(2):
                    d = 2 * rnd + i
                    last = mm(ps2[7][:, i], yexp[:, d * P:(d + 1) * P], pickT[:], start=True, stop=True)
                last.then_inc(spread_done, 1)

            def expert(job, mine, following):
                chunks = JOB_UP // 4
                pe.wait_ge(xglo_ready, mine.count(2, 2))

                def turn(c):
                    pe.wait_ge(ma_ready, job.count(chunks, c + 1))
                    if c:
                        pe.wait_ge(tlo_ready, job.count(chunks, c))
                    for i in range(4):
                        last = nc.tensor.transpose(ps4[4][:, i], ma[:, c % 2, i * P:(i + 1) * P], ident)
                    last.then_inc(turned, 1)

                for i in range(JOB_UP):
                    u, c, kind, half = job.unit(i), i // 4, i % 4 // 2, i % 2
                    if c >= 2 and half == 0:
                        pe.wait_ge((mg_ready, ma_ready)[kind], job.count(chunks, c - 1))
                    pe.wait_ge(raw_free, u.ring())
                    o = ps[2 * kind + c % 2][:, :]
                    for kk in range(4):
                        k, w = 4 * half + kk, slice(512 * kk, 512 * kk + 512)
                        mm(o, xghi[:, k], whi[:, u.hl, w], start=k == 0, stop=False)
                        mm(o, xglo[:, k], whi[:, u.hl, w], start=False, stop=False)
                        last = mm(o, xghi[:, k], wlo[:, u.hl, w], start=False, stop=k == KD - 1)
                    last.then_inc(unit_done, 1)
                    if c and i % 4 == 1:
                        turn(c - 1)
                    if i % 4 == 3 and 1 <= c <= 4:
                        if c == 1:
                            pe.wait_ge(yexp_ready, job.count(1, 1))
                            pe.wait_ge(pickT_ready, job.count(1, 1))
                        else:
                            pe.wait_ge(spread_taken, job.count(4, c - 1))
                        spread(job, c - 1)
                    if i == 4 * 5 + 3:
                        pe.wait_ge(spread_taken, job.count(4, 4))
                        for t in range(2):
                            last = nc.tensor.transpose(ps[7][:, t * P:(t + 1) * P], pickw[:, t], ident)
                        last.then_inc(pickT_done, 1)
                for d in range(JOB_DOWN):
                    u = job.unit(JOB_UP + d)
                    pe.wait_ge(tlo_ready, job.count(chunks, d // 2 + 1))
                    pe.wait_ge(raw_free, u.ring())
                    for i in range(2):
                        f = 2 * d + i
                        for n in range(2):
                            o, w = ps[5 + n][:, :], slice(D * i + 512 * n, D * i + 512 * n + 512)
                            mm(o, thi[:, f], whi[:, u.hl, w], start=f == 0, stop=False)
                            mm(o, tlo[:, f], whi[:, u.hl, w], start=False, stop=False)
                            last = mm(o, thi[:, f], wlo[:, u.hl, w], start=False, stop=f == FE // P - 1)
                    last.then_inc(unit_done, 1)
                    if d == 0:
                        turn(chunks - 1)
                    if following is not None and d in (1, 5):
                        if d == 1:
                            pe.wait_ge(pick_ready, following.count(1, 1))
                            pe.wait_ge(pickT_ready, job.count(1, 2))
                        else:
                            pe.wait_ge(xglo_ready, following.count(2, 1))
                        gather(following, d // 4)

            pe.wait_ge(htok_ready, 2)
            pe.wait_ge(pick_ready, 1)
            for half in range(2):
                if half:
                    pe.wait_ge(xglo_ready, 1)
                gather(Job(0, 0), half)
            with pe.Fori(0, NE) as e:
                expert(Job(0, e), Job(0, e), Job(1, e))
            pe.wait_ge(jobs_ready, 1)
            nx = pe.value_load(jobs[0:1, 0:1], min_val=0, max_val=3)
            with pe.If(nx > 0):
                with pe.Fori(0, nx) as j:
                    mine = Job(NE + 1, j)
                    pe.wait_ge(pick_ready, mine.count(1, 1))
                    for half in range(2):
                        pe.wait_ge(xglo_ready, mine.count(2, half))
                        gather(mine, half)
                    expert(Job(NE, j), mine, None)
            end = Job(NE, nx)
            pe.wait_ge(yexp_ready, end.count(1, 1))
            pe.wait_ge(pickT_ready, end.count(1, 1))
            for rnd in range(4):
                if rnd:
                    pe.wait_ge(spread_taken, end.count(4, rnd))
                spread(end, rnd)
            pe.wait_ge(x_ready, 8)
            for t in range(2):
                for k in range(KD):
                    last = nc.tensor.transpose(ps[2 * t + k // 4][:, P * (k % 4):P * (k % 4) + P], xT[:, k, t * P:(t + 1) * P], ident)
                    if k % 4 == 3:
                        last.then_inc(out_turned, 1)

        @block.vector
        def _(dve):
            step = Chain(dve, vector_step)
            V = nc.vector

            def bc(ap, n):
                return ap.unsqueeze(1).broadcast_to([ap.shape[0], n, ap.shape[1]])

            def low(u):
                dve.wait_ge(hi_ready, u.count())
                if u.n >= HL or u.per:
                    dve.wait_ge(unit_done, u.count(1 - HL))
                V.tensor_tensor(wlo[:, u.hl, :], raw[:, u.raw, :], whi[:, u.hl, :].bitcast(F32), ALU.subtract).then_inc(raw_free, 1)

            def norm(n):
                dve.wait_ge(std_ready, n + 1)
                step(V.reciprocal(rstd[:], rstd[:]))
                to = xT if n == N_FINAL else h
                step(V.tensor_tensor(to[:], xT[:], bc(rstd[:], KD), ALU.mult))
                for k in range(KD):
                    if n == N_FINAL:
                        last = V.tensor_scalar(xT[:, k], xT[:, k], par2[:, 0, P2_FIN + k:P2_FIN + k + 1], None, ALU.mult)
                    else:
                        shift = SHIFT[n] + k
                        last = V.tensor_scalar(h[:, k], h[:, k], amul[:, n, k:k + 1], mod[:, shift:shift + 1], ALU.mult, ALU.add)
                        if k % 4 == 3:
                            last.then_inc(h_ready, 1)
                if n == N_FINAL:
                    last.then_inc(x_ready, 1)
                    return
                for half in range(2):
                    at = slice(4 * half, 4 * half + 4)
                    dve.wait_ge(hhi_ready, 2 * split_no(n) + half + 1)
                    V.tensor_tensor(hlo[:, at], h[:, at], hhi[:, at].bitcast(F32), ALU.subtract).then_inc(hlo_ready, 1)

            def residual(last_unit, gate):
                dve.wait_ge(unit_done, Unit(last_unit).count())
                for d in range(KD):
                    last = V.scalar_tensor_tensor(xT[:, d], ps2[2 + d // 2][:, d % 2], mod[:, gate + d:gate + d + 1], xT[:, d],
                                                  ALU.mult, ALU.add)
                last.then_inc(x_ready, 1)

            V.memset(ones[:], 1.0)
            V.memset(mean256[:], 1.0 / HD)
            V.memset(mean512[:], 1.0 / D_CONV)
            V.memset(eps[:], EPS).then_inc(memset_done, 1)
            dve.wait_ge(x_turned, 1)
            for b in range(4):
                last = V.tensor_copy(xT[:, 2 * b:2 * b + 2], ps2[b])
            last.then_inc(x_ready, 1)
            dve.wait_ge(rows_turned, 1)
            V.tensor_copy(par1[:], ps4[4][:, 0:2])
            for l in range(L):
                V.tensor_copy(par2[:, l, 0:P2_ROWS[l]], ps4[4][:, 2 + l, 0:P2_ROWS[l]])
                last = V.tensor_copy(taps2[:, l, 0:CW * CT], ps4[5][:, l, 0:CW * CT])
            last.then_inc(cols_ready, 1)
            dve.wait_ge(pos_in, 16)
            dve.wait_ge(const_in, 16)
            step(V.tensor_copy(posf[:], posi[:]))
            step(V.tensor_scalar(ang[:], posf[:], cst[:, C_FREQ:C_FREQ + 1], None, ALU.mult))
            step(V.tensor_scalar(turns[:, 0], ang[:], float(np.float32(1 / (2 * np.pi))), ROUND, ALU.mult, ALU.add))
            step(V.tensor_scalar(turns[:, 0], turns[:, 0], -ROUND, None, ALU.add))
            for part in TWO_PI:
                step(V.scalar_tensor_tensor(ang[:], turns[:, 0], -part, ang[:], ALU.mult, ALU.add))
            V.tensor_scalar(ang[:], ang[:], -PI_BELOW, PI_BELOW, ALU.max, ALU.min).then_inc(angle_ready, 1)
            dve.wait_ge(cact_ready, 1)
            r = 0
            for l in range(L):
                for b, units in enumerate((ADA1, ADA2)):
                    for n in range(units):
                        dve.wait_ge(raw_in[r % RAW], 16 * (r // RAW + 1))
                        if r >= 2:
                            dve.wait_ge(ada_done, r - 1)
                        w = raw[:, r % RAW, :].rearrange("p (k n) -> p k n", k=KD)
                        a = acc[:, r % 2]
                        step(V.tensor_scalar(a, w[:, 0], cact[:, b, 0:1], None, ALU.mult))
                        for k in range(1, KD):
                            last = V.scalar_tensor_tensor(a, w[:, k], cact[:, b, k:k + 1], a, ALU.mult, ALU.add)
                            step(last) if k < KD - 1 else last.then_inc(raw_free, 1)
                        r += 1
            dve.wait_ge(ada_done, ADA_UNITS)
            for l in range(L):
                m0 = 72 * l
                V.tensor_tensor(mod[:, m0:m0 + 24], ps[6][:, m0:m0 + 24], par1[:, l, P1_BADA:P1_BADA + 24], ALU.add)
                step(V.tensor_tensor(mod[:, m0 + 24:m0 + 72], ps[6][:, m0 + 24:m0 + 72], par2[:, l, P2_BADA:P2_BADA + 48], ALU.add))
            for n in SHIFT:
                l = (0, 1, None, 0, 0, 1, 1)[n]
                g = par1[:, l, P1_NORM:P1_NORM + KD] if n < 2 else \
                    par2[:, l, P2_MIX:P2_MIX + KD] if n in N_MIX else par2[:, l, P2_FFN:P2_FFN + KD]
                last = V.scalar_tensor_tensor(amul[:, n], mod[:, SHIFT[n] + KD:SHIFT[n] + 2 * KD], 1.0, g, ALU.add, ALU.mult)
            step(last)

            for i in range(LOOK):
                low(Unit(S_B1 + i))
            V.memset(qpad[:, :, :, 0:CONV_K - 1], 0.0)
            for l in range(L):
                norm(l)
                dve.wait_ge(gates_done, l + 1)
                dve.wait_ge(gate_in, 16 * 3 * L)
                V.tensor_scalar(gt[:, 1], ps2[7][0:H, 1], gbias[:, l, 1:2], None, ALU.add).then_inc(gate_f, 1)
                V.tensor_scalar(gt[:, 0], ps2[7][0:H, 0], gbias[:, l, 0:1], None, ALU.add)
                dve.wait_ge(gate_f, l + 1)
                dve.wait_ge(gate_ln, l + 1)
                step(V.scalar_tensor_tensor(gt[:, 3], gt[:, 1], 0.0, gt[:, 2], ALU.min, ALU.subtract))
                step(V.tensor_tensor_scan(gt[:, 4], ones[0:H], gt[:, 3], 0.0, ALU.mult, ALU.add))
                V.tensor_tensor(gt[:, 5], gt[:, 0], gt[:, 4], ALU.subtract).then_inc(a_ready, 1)
                dve.wait_ge(a_ready, l + 1)
                step(V.tensor_tensor_scan(gt[:, 6], ones[0:H], gt[:, 5], 0.0, ALU.mult, ALU.max))
                V.tensor_tensor(gt[:, 7], gt[:, 4], gt[:, 6], ALU.add).then_inc(gate_m, 1)
                for i in range(H):
                    V.tensor_scalar(gdiag[:, i, 0], gt[:, 6], cst[0:H, C_ID + i:C_ID + i + 1], -1.0, ALU.mult, ALU.mult)
                dve.wait_ge(gate_em, l + 1)
                for i in range(H):
                    V.tensor_scalar(gdiag[:, i, 1], gt[:, 7], cst[0:H, C_ID + i:C_ID + i + 1], None, ALU.mult)
                dve.wait_ge(a_turned, l + 1)
                V.tensor_copy(acol[:], ps[7][:, 0:2 * H].rearrange("p (t h) -> p t h", t=2)).then_inc(acol_ready, 1)
                dve.wait_ge(acol_ready, l + 1)

                with dve.Fori(0, NPAIR) as pair:
                    step.enter(pair, STEPS_PAIR)
                    for hh in range(2):
                        hd = Head(l, hh, pair)
                        u0 = Unit(S_B1 + l * UNIT_L1 + hh * HEAD_UNITS, pair, 2 * HEAD_UNITS)
                        q, k, v, o, z, rq, rk, rv, rz = (u0.plus(i) for i in range(HEAD_UNITS))

                        def column(base, tile):
                            return par1[:, l, bass.ds(hd.h * 2 + (base + tile), 1)]

                        def take(u, x):
                            dve.wait_ge(unit_done, u.count())
                            V.tensor_copy(qpad[:, x, :, CONV_K - 1:], ps2[u.bank]).then_inc(taken_v, 1)

                        low(q.plus(LOOK))
                        dve.wait_ge(raw_free, q.plus(LOOK).ring())
                        take(q, 0)
                        low(k.plus(LOOK))
                        take(k, 1)
                        dve.wait_ge(taken_v, hd.count(4, 2))
                        for tap in range(CONV_K):
                            for x in range(2):
                                for t in range(2):
                                    w = column(P1_CW + tap * 2 * KD + x * KD, t)
                                    src = qpad[:, x, t, tap:tap + S]
                                    if tap == 0:
                                        last = V.tensor_scalar(qacc[:, x, t], src, w, column(P1_CB + x * KD, t), ALU.mult, ALU.add)
                                    else:
                                        step.wait(back=3)
                                        last = V.scalar_tensor_tensor(qacc[:, x, t], src, w, qacc[:, x, t], ALU.mult, ALU.add)
                                    if (tap, x, t) == (CONV_K - 1, 1, 1):
                                        last.then_inc(conv_done, 1)
                                    else:
                                        step.mark(last)
                        low(v.plus(LOOK))
                        low(o.plus(LOOK))
                        dve.wait_ge(bc_copied, hd.count(1, 1))
                        V.scalar_tensor_tensor(arg[:, 0:S], bcs[:, 0], acol[:, 0, bass.ds(hd.h, 1)], causal, ALU.add, ALU.add)
                        V.scalar_tensor_tensor(arg[:, S:S + P], bcs[:, 0, P:S], acol[:, 1, bass.ds(hd.h, 1)], causal[:, 0:P],
                                               ALU.add, ALU.add).then_inc(arg_ready, 1)
                        low(z.plus(LOOK))
                        dve.wait_ge(scores_done, hd.count(2, 1))
                        dve.wait_ge(exp_ready, hd.count(1, 1))
                        V.scalar_tensor_tensor(sT[:], ps[2][:, 0:S + P], HD ** -0.5, arg[:], ALU.mult, ALU.mult).then_inc(sT_ready, 1)
                        dve.wait_ge(taken_s, hd.count(5, 3))
                        step(V.tensor_scalar(osig[:], osig[:], 0.5, 0.5, ALU.mult, ALU.add))
                        step(V.tensor_tensor(osig[:], osig[:], zsil[:], ALU.mult))
                        low(rq.plus(LOOK))
                        dve.wait_ge(pv_done, hd.count(2, 1))
                        step(V.scalar_tensor_tensor(den[:], ps2[5][:, 0], -1.0, bcs[:, 1], ALU.mult, ALU.max))
                        step(V.tensor_tensor(den[:], ps2[5][:, 0], den[:], ALU.max))
                        step(V.reciprocal(den[:], den[:]))
                        V.tensor_tensor(hn[:], ps2[4], bc(den[:], 2), ALU.mult).then_inc(hn_ready, 1)

                        def rotate(u, x):
                            dve.wait_ge(unit_done, u.count())
                            if x:
                                step.wait()
                            step.mark(V.tensor_tensor(qacc[:, 0], ps2[u.bank], bc(cosT[:], 2), ALU.mult))
                            V.tensor_tensor(qacc[:, 1], ps2[u.bank], bc(sinT[:], 2), ALU.mult).then_inc(taken_v, 1)
                            dve.wait_ge(taken_v, hd.count(4, 3 + x))
                            step.mark(V.tensor_tensor(rot[:, x, 0], qacc[:, 0, 0], qacc[:, 1, 1], ALU.subtract))
                            last = V.tensor_tensor(rot[:, x, 1], qacc[:, 0, 1], qacc[:, 1, 0], ALU.add)
                            last.then_inc(rot_done, 1) if x else step.mark(last)

                        def centre(i):
                            dve.wait_ge(mean_done, hd.count(2, i))
                            V.tensor_tensor(hn[:], hn[:], bc(ps2[6][:, 0], 2), ALU.subtract).then_inc(hc_ready, 1)

                        def finish(i, base, gate):
                            dve.wait_ge(sd_ready, hd.count(2, i))
                            step(V.reciprocal(den[:], sq[:, 0]))
                            step(V.tensor_tensor(hn[:], hn[:], bc(den[:], 2), ALU.mult))
                            for t in range(2):
                                last = V.scalar_tensor_tensor(yf[:, t], hn[:, t], column(base, t), gate[:, t], ALU.mult, ALU.mult)
                            last.then_inc(y_ready, 1)

                        def y_low(i, tile):
                            dve.wait_ge(yhi_ready, hd.count(2, i))
                            at = bass.ds(hd.h * 2 + tile, 2)
                            V.tensor_tensor(ylo[:, at, :], yf, yhi[:, at, :].bitcast(F32), ALU.subtract).then_inc(ylo_ready, 1)

                        rotate(rq, 0)
                        low(rk.plus(LOOK))
                        centre(1)
                        rotate(rk, 1)
                        low(rv.plus(LOOK))
                        finish(1, P1_GNM, osig)
                        low(rz.plus(LOOK))
                        y_low(1, 0)
                        dve.wait_ge(scores_done, hd.count(2, 2))
                        for o, t in ((slice(0, S), S), (slice(S, S + P), P)):
                            last = V.scalar_tensor_tensor(sT[:, o], ps[2][:, o], HD ** -0.5,
                                                          cst[:, bass.ds(hd.h * S + C_DECAY, t)], ALU.mult, ALU.mult)
                        last.then_inc(sT_ready, 1)
                        dve.wait_ge(pv_done, hd.count(2, 2))
                        V.tensor_copy(hn[:], ps2[4]).then_inc(hn_ready, 1)
                        centre(2)
                        dve.wait_ge(taken_s, hd.count(5, 5))
                        finish(2, P1_GNR, zsil)
                        y_low(2, KD)
                step.leave(NPAIR)
                for j in range(OUT1_UNITS):
                    low(Unit(S_B1 + l * UNIT_L1 + H * HEAD_UNITS + j + LOOK))
                residual(S_B1 + (l + 1) * UNIT_L1 - 1, 72 * l + 16)
            norm(N_FINAL)

            def mixer(l, first):
                V.memset(zpad[:, :, 0:CW - 1], 0.0)
                norm(N_MIX[l])
                dve.wait_ge(bias_in, 16 * (l + 1))
                step(V.memset(bias2[0:CHUNK, :, S - CHUNK:S], NEG))
                taps = [(t, tap) for tap in range(CW) for t in range(CT)]
                done = CW * CT * l

                def conv(n):
                    for _ in range(min(n, len(taps))):
                        t, tap = taps.pop(0)
                        at = done + CW * CT - len(taps)
                        w, src = taps2[:, l, tap * CT + t:tap * CT + t + 1], zpad[:, t, tap:tap + S]
                        if tap == 0:
                            last = V.tensor_scalar(zacc[:, t], src, w, par2[:, l, P2_CB + t:P2_CB + t + 1], ALU.mult, ALU.add)
                        else:
                            dve.wait_ge(conv_step, at - CT)
                            last = V.scalar_tensor_tensor(zacc[:, t], src, w, zacc[:, t], ALU.mult, ALU.add)
                        last.then_inc(conv_step, 1)

                for j in range(MIX_UNITS):
                    u = Unit(first + j)
                    low(u.plus(LOOK))
                    if j in (1, 3):
                        dve.wait_ge(sig_ready, 2 * l + j // 2 + 1)
                        step(V.tensor_scalar(sig[:], sig[:], 0.5, 0.5, ALU.mult, ALU.add))
                        V.tensor_tensor(zpad[:, j - 1:j + 1, CW - 1:], ps2[1 - u.bank], sig[:], ALU.mult).then_inc(gemm_taken, 1)
                        dve.wait_ge(gemm_taken, 6 * l + j // 2 + 1)
                    if 4 <= j < 8:
                        i, half = (j - 4) // 2, j % 2
                        dve.wait_ge(unit_done, u.count())
                        V.tensor_copy(q2[:, i, 2 * half:2 * half + 2], ps2[u.bank]).then_inc(gemm_taken, 1)
                    if j >= 4:
                        conv(8)
                dve.wait_ge(hstd_ready, l + 1)
                V.reciprocal(rs2[:], rs2[:]).then_inc(hr_ready, 1)
                dve.wait_ge(hbc_done, l + 1)
                for i in range(2):
                    for t in range(CT):
                        last = V.scalar_tensor_tensor(q2[:, i, t], q2[:, i, t], par2[:, l, P2_QN + i:P2_QN + i + 1],
                                                      ps2[3 + 2 * i + t // 2][:, t % 2], ALU.mult, ALU.mult)
                last.then_inc(qn_ready, 1)

                def pair_low(i):
                    dve.wait_ge(y2hi_ready, (CT + 1) * l + i + 1)
                    V.tensor_tensor(y2lo[:, CT + i], ps2[6 + i % 2][:, 0], y2hi[:, CT + i].bitcast(F32), ALU.subtract)\
                        .then_inc(y2lo_ready, 1)

                for n in range(NH2 + 1):
                    b, at = n % 2, NH2 * l + n
                    if n < NH2:
                        dve.wait_ge(sc2_done, at + 1)
                        step.mark(V.scalar_tensor_tensor(s2[:, b, 0:P], ps[2 + b][:, 0:P], HD2 ** -0.5, bias2[:, n, P:S],
                                                         ALU.mult, ALU.add))
                        step(V.scalar_tensor_tensor(s2[:, b, P:P + S], ps[2 + b][:, P:P + S], HD2 ** -0.5, bias2[:, n, :],
                                                    ALU.mult, ALU.add))
                        step.mark(V.reduce_max(st2[:, b, 0:1], s2[:, b, 0:P], AX.X))
                        step(V.reduce_max(st2[:, b, 1:2], s2[:, b, P:P + S], AX.X))
                        V.tensor_scalar(st2[:, b, 2:4], st2[:, b, 0:2], -1.0, None, ALU.mult).then_inc(s2_ready, 1)
                        conv(5)
                    if n:
                        b = (n - 1) % 2
                        dve.wait_ge(p2_sum, at)
                        step(V.reciprocal(st2[:, b, 6:8], st2[:, b, 4:6]))
                        V.tensor_scalar(p2[:, b, 0:P], p2[:, b, 0:P], st2[:, b, 6:7], None, ALU.mult)
                        V.tensor_scalar(p2[:, b, P:P + S], p2[:, b, P:P + S], st2[:, b, 7:8], None, ALU.mult).then_inc(p2_ready, 1)
                        conv(5)
                        dve.wait_ge(pT_done, at)
                        V.tensor_copy(pT[:, b], ps[4 + b][:, 0:S + P]).then_inc(pT_ready, 1)
                    if n >= 3 and n % 2:
                        pair_low((n - 3) // 2)
                pair_low(CT - 1)
                for j in range(2):
                    low(Unit(first + MIX_UNITS + LOOK + j))
                conv(len(taps))
                dve.wait_ge(zmean_done, l + 1)
                V.tensor_tensor(zacc[:], zacc[:], bc(ps2[0][:, 0], CT), ALU.subtract).then_inc(zc_ready, 1)
                dve.wait_ge(zstd_ready, l + 1)
                step(V.reciprocal(sig[:, 1], sig[:, 0]))
                V.tensor_tensor(zacc[:], zacc[:], bc(sig[:, 1], CT), ALU.mult).then_inc(zn_ready, 1)
                dve.wait_ge(y2hi_ready, (CT + 1) * (l + 1))
                V.tensor_tensor(y2lo[:, 0:CT], q2[:, 0], y2hi[:, 0:CT].bitcast(F32), ALU.subtract).then_inc(y2lo_ready, 1)
                for j in range(2, OUT2_UNITS):
                    low(Unit(first + MIX_UNITS + LOOK + j))
                residual(first + UNIT_L2 - 1, 72 * l + 24 + 16)

            mixer(0, S_B2)
            norm(N_FFN[0])

            def ff_low(i):
                dve.wait_ge(fhi_ready, i + 1)
                V.tensor_tensor(flo[:, 2 * i:2 * i + 2], fa[:, i % 2], fhi[:, 2 * i:2 * i + 2].bitcast(F32), ALU.subtract)\
                    .then_inc(flo_ready, 1)

            for j in range(FF_UNITS):
                u, i = Unit(S_FF + j), j // 2
                low(u.plus(LOOK))
                if j % 2:
                    dve.wait_ge(fg_ready, i + 1)
                    dve.wait_ge(unit_done, u.count())
                    V.tensor_tensor(fa[:, i % 2], fg[:, i % 2], ps2[u.bank], ALU.mult).then_inc(fa_ready, 1)
                elif i:
                    ff_low(i - 1)
            for j in range(DOWN_UNITS):
                low(Unit(S_FF + FF_UNITS + j + LOOK))
                if j == 0:
                    ff_low(FF_UNITS // 2 - 1)
            residual(S_B3 - 1, 24 + 40)
            mixer(1, S_B3)
            norm(N_FFN[1])

            dve.wait_ge(router_in, 32)
            dve.wait_ge(logits_done, 1)
            step(V.tensor_tensor(lg[:, 0], ps[7][:, 0:2 * NE].rearrange("p (t e) -> p t e", t=2), bc(rb[:], 2), ALU.add))

            def largest(src, col, dst):
                step(V.tensor_reduce(lg[:, 10, col, 4:6], lg[:, src], axis=AX.X, op=ALU.max))
                for t in range(2):
                    last = V.tensor_scalar(lg[:, dst, t], lg[:, src, t], lg[:, 10, col, 4 + t:5 + t], None, ALU.is_equal)
                step(last)
                for t in range(2):
                    last = V.tensor_tensor_scan(lg[:, dst + 1, t], ones[:, 0:NE], lg[:, dst, t], 0.0, ALU.mult, ALU.add)
                step(last)
                step(V.scalar_tensor_tensor(lg[:, dst], lg[:, dst + 1], 1.0, lg[:, dst], ALU.is_equal, ALU.mult))

            largest(0, 0, 1)
            step(V.scalar_tensor_tensor(lg[:, 3], lg[:, 1], NEG, lg[:, 0], ALU.mult, ALU.add))
            largest(3, 1, 4)
            V.tensor_tensor(lg[:, 9], lg[:, 1], lg[:, 4], ALU.add).then_inc(route_ready, 1)
            V.tensor_tensor(lg[:, 10, 1, 0:2], lg[:, 10, 1, 4:6], lg[:, 10, 0, 4:6], ALU.subtract).then_inc(e_ready, 1)
            dve.wait_ge(route_ready, 1)
            dve.wait_ge(htok_done, 1)
            step.mark(V.tensor_copy(htok[:, 1, 0:512], ps[2][:, :]))
            V.tensor_copy(htok[:, 1, 512:D], ps[3][:, :]).then_inc(htok_ready, 1)
            V.memset(comb[:], 0.0)
            V.memset(r1[:], 0.0)
            dve.wait_ge(route_exp, 1)
            step(V.tensor_scalar(lg[:, 11, 0, 2:4], lg[:, 11, 0, 0:2], 1.0, None, ALU.add))
            step(V.reciprocal(lg[:, 11, 0, 4:6], lg[:, 11, 0, 2:4]))
            step(V.tensor_tensor(lg[:, 11, 0, 6:8], lg[:, 11, 0, 0:2], lg[:, 11, 0, 4:6], ALU.mult))
            for t in range(2):
                step(V.tensor_scalar(comb[:, t, 0:NE], lg[:, 1, t], lg[:, 11, 0, 4 + t:5 + t], None, ALU.mult))
                step(V.scalar_tensor_tensor(comb[:, t, 0:NE], lg[:, 4, t], lg[:, 11, 0, 6 + t:7 + t], comb[:, t, 0:NE],
                                            ALU.mult, ALU.add))
            step(V.memset(posm[:], -1e6))
            dve.wait_ge(rank_done, 1)
            step(V.scalar_tensor_tensor(posm[:, :, 0:NE], ps[6][:, 0:2 * NE].rearrange("p (t e) -> p t e", t=2), 1e6, lg[:, 9],
                                        ALU.add, ALU.mult))
            step(V.tensor_scalar(posm[:, :, 0:NE], posm[:, :, 0:NE], -1e6, None, ALU.add))
            step(V.tensor_scalar(r1[:, 0], ps[6][0:1, 2 * NE:3 * NE], P + 0.5, None, ALU.is_gt))
            step(V.tensor_tensor_scan(r1[:, 1], ones[0:1, 0:NE], r1[:, 0], 0.0, ALU.mult, ALU.add))
            step(V.tensor_tensor(r1[:, 2], r1[:, 1], r1[:, 0], ALU.subtract))
            step(V.tensor_copy(r1[:, 9, 0:1], r1[:, 1, NE - 1:NE]))
            for j in range(3):
                step(V.scalar_tensor_tensor(r1[:, 3], r1[:, 2], float(j), r1[:, 0], ALU.is_equal, ALU.mult))
                step(V.tensor_tensor(r1[:, 4], r1[:, 3], iota[0:1, 0:NE], ALU.mult))
                step(V.reduce_sum(r1[:, 9, j + 1:j + 2], r1[:, 4], AX.X))
            V.tensor_copy(jobs[:], r1[:, 9]).then_inc(jobs_ready, 1)

            def picks(e, first):
                for t in range(2):
                    step.mark(V.tensor_scalar(pick[:, t], iota, float(first), posm[:, t, bass.ds(e, 1)], ALU.add, ALU.is_equal))
                step.wait()
                for t in range(2):
                    last = V.tensor_scalar(pickw[:, t], pick[:, t], comb[:, t, bass.ds(e, 1)], None, ALU.mult)
                last.then_inc(pick_ready, 1)

            def take_tokens(gather, half):
                at = slice(4 * half, 4 * half + 4)
                dve.wait_ge(xghi_ready, gather.count(2, half + 1))
                V.tensor_tensor(xglo[:, at], ps4[7], xghi[:, at].bitcast(F32), ALU.subtract).then_inc(xglo_ready, 1)

            def expert(job, following):
                chunks = JOB_UP // 4
                for i in range(JOB_UNITS):
                    u, c = job.unit(i), i // 4
                    low(u.plus(LOOK))
                    if i < JOB_UP and i % 4 == 3:
                        dve.wait_ge(mg_ready, job.count(chunks, c + 1))
                        dve.wait_ge(unit_done, u.count())
                        V.tensor_tensor(ma[:, c % 2], mg[:, c % 2], ps[2 + c % 2][:, :], ALU.mult).then_inc(ma_ready, 1)
                    if i % 4 == 2 and 1 <= c <= chunks:
                        dve.wait_ge(thi_ready, job.count(chunks, c))
                        at = slice(4 * c - 4, 4 * c)
                        V.tensor_tensor(tlo[:, at], ps4[4], thi[:, at].bitcast(F32), ALU.subtract).then_inc(tlo_ready, 1)
                    if i % 4 == 0 and 2 <= c <= 5:
                        rnd = c - 2
                        dve.wait_ge(spread_done, job.count(4, rnd + 1))
                        V.tensor_tensor(moe[:, 2 * rnd:2 * rnd + 2], moe[:, 2 * rnd:2 * rnd + 2], ps2[7], ALU.add)\
                            .then_inc(spread_taken, 1)
                    if i == 25:
                        dve.wait_ge(pickT_done, job.count(1, 1))
                        V.tensor_copy(pickT[:], ps[7][:, 0:S]).then_inc(pickT_ready, 1)
                    if following is not None and i == 26:
                        picks(following.turn + following.n, 0)
                    if following is not None and i in (JOB_UP + 3, JOB_UP + 7):
                        take_tokens(following, (i - JOB_UP) // 4)

            V.memset(pickT[:], 0.0).then_inc(pickT_ready, 1)
            V.memset(moe[:], 0.0)
            step.mark(V.memset(yexp[:, 0:512], 0.0))
            V.memset(yexp[:, 512:D], 0.0).then_inc(yexp_ready, 1)
            dve.wait_ge(yexp_ready, 1)
            picks(0, 0)
            for half in range(2):
                take_tokens(Job(0, 0), half)
            with dve.Fori(0, NE) as e:
                step.enter(e, 2)
                expert(Job(0, e), Job(1, e))
            step.leave(NE)
            dve.wait_ge(jobs_ready, 1)
            nx = dve.value_load(jobs[0:1, 0:1], min_val=0, max_val=3)
            with dve.If(nx > 0):
                with dve.Fori(0, nx) as j:
                    step.enter(j, 2)
                    picks(dve.value_load(jobs[0:1, bass.ds(j + 1, 1)], min_val=0, max_val=NE - 1), P)
                    for half in range(2):
                        take_tokens(Job(NE + 1, j), half)
                    expert(Job(NE, j), None)
            end = Job(NE, nx)
            for rnd in range(4):
                dve.wait_ge(spread_done, end.count(4, rnd + 1))
                V.tensor_tensor(moe[:, 2 * rnd:2 * rnd + 2], moe[:, 2 * rnd:2 * rnd + 2], ps2[7], ALU.add).then_inc(spread_taken, 1)
            dve.wait_ge(spread_taken, end.count(4, 4))
            for d in range(KD):
                g = 72 + 24 + 40 + d
                last = V.scalar_tensor_tensor(xT[:, d], moe[:, d], mod[:, g:g + 1], xT[:, d], ALU.mult, ALU.add)
            last.then_inc(x_ready, 1)


def _shape_constants():
    c = np.zeros((P, C_ALL), np.float32)
    p, t = np.arange(P)[:, None], np.arange(S)[None, :]
    c[:, C_ID:C_ID + P] = np.eye(P)
    c[:, C_CAUSAL:C_CAUSAL + S] = np.where(p <= t, 0.0, NEG)
    for i in range(H):
        c[:, C_DECAY + S * i:C_DECAY + S * (i + 1)] = np.where(p <= t, (1.0 - 2.0 ** (-5.0 - i)) ** np.maximum(t - p, 0), 0.0)
    c[:, C_BEFORE:C_BEFORE + P] = p < np.arange(P)[None, :]
    c[:, C_IOTA:C_IOTA + P] = np.arange(P)[None, :]
    c[:, C_FREQ] = np.float32(1.0) / np.float32(10000.0) ** np.linspace(0.0, 1.0, P, dtype=np.float32)
    for j in range(CT):
        for half in range(2):
            c[HD2 * half:HD2 * half + HD2, C_HSUM + NH2 * j + 2 * j + half] = 1.0 / HD2
            at = C_HBC + P * j + HD2 * half
            c[2 * j + half, at:at + HD2] = 1.0
    return c


_INS = ['x', 'positions', 'consts', 'c', 'w_ada', 'b_ada', 'norm_g', 'w_in', 'conv_w', 'conv_b', 'b_igate', 'b_fgate',
        'gn_m', 'gn_r', 'w_out', 'final_g', 'c_2', 'w_ada_2', 'b_ada_2', 'norm_mix_g_2', 'norm_ffn_g_2', 'w_in_2',
        'w_out_2', 'conv_w_2', 'conv_b_2', 'conv_ln_g_2', 'conv_ln_b_2', 'q_norm_g_2', 'k_norm_g_2', 'rel_bias_2',
        'ffn_w_gate_2', 'ffn_w_up_2', 'ffn_w_down_2', 'moe_w_router_2', 'moe_b_router_2', 'moe_w_gate_2',
        'moe_w_up_2', 'moe_w_down_2']
_OUTS = [((1, S, D), 'float32')]


def kernel(**inputs):
    import numpy as _np
    import concourse.bacc as _bacc
    from concourse import mybir as _mybir
    from concourse.bass_utils import run_bass_kernel_spmd as _run

    nc = _bacc.Bacc("TRN2", target_bir_lowering=False, num_devices=1)
    arrays, args = {}, []
    for name in _INS:
        a = _shape_constants() if name == 'consts' else _np.ascontiguousarray(inputs[name])
        arrays[f"in_{name}_dram"] = a
        args.append(nc.dram_tensor(f"in_{name}_dram", a.shape, _mybir.dt.from_np(a.dtype), kind="ExternalInput").ap())
    for i, (shape, dtype) in enumerate(_OUTS):
        dt = _mybir.dt.from_np(_np.dtype(dtype))
        args.append(nc.dram_tensor(f"out_{i}_dram", shape, dt, kind="ExternalOutput").ap())
    two_block_model(nc, *args)
    r = _run(nc, [arrays], core_ids=[0])
    got = tuple(r.results[0][f"out_{i}_dram"] for i in range(len(_OUTS)))
    return got[0]
```

```python
import concourse.bass as bass
from concourse import mybir
from contextlib import ExitStack
import numpy as np

F32 = mybir.dt.float32
F32R = mybir.dt.float32r
I32 = mybir.dt.int32
ACT = mybir.ActivationFunctionType
ALU = mybir.AluOpType
AX = mybir.AxisListType

P = 128
S = 256
D = 1024
KD = D // P
L = 2
H = 4
HD = 256
D_INNER = 2048
D_MLSTM = 1024
D_RET = 1024
NPAIR = H // 2
CONV_K = 4
EPS = 1e-6
GATE_COL = 5 * D_MLSTM
RET_COL = GATE_COL + 2 * H
D_CONV = 512
D_ATT = 512
CW = 31
NH2 = 8
HD2 = 64
NREL = 257
EXT = 127 + NREL
CHUNK = 64
FF = 2816
NE = 8
FE = 3584
CT = D_CONV // P
NEG = -1e30

C_ID = 0
C_CAUSAL = C_ID + P
C_DECAY = C_CAUSAL + S
C_FREQ = C_DECAY + H * S
C_BEFORE = C_FREQ + 1
C_IOTA = C_BEFORE + P
C_HSUM = C_IOTA + P
C_HBC = C_HSUM + CT * NH2
C_ALL = C_HBC + CT * P

P1_BADA, P1_NORM, P1_CW, P1_CB, P1_GNM, P1_GNR = 0, 24, 32, 96, 112, 120
P2_BADA, P2_MIX, P2_FFN, P2_CB, P2_LG, P2_LB, P2_QN, P2_KN, P2_FIN = 0, 48, 56, 64, 68, 72, 76, 77, 78
P2_ROWS = (86, 78)

UW = 2048
RAW = 6
HALF = 3
MOE_SLOTS = (3, 4, 5, 2, 0, 1)
HL = 3
LOOK = 2
ADA1, ADA2 = 3 * D // 256, 6 * D // 256
ADA_UNITS = L * (ADA1 + ADA2)
ADA_START, ADA_TURN, ADA_MIX, ADA_FF = 8, (9, 6), (10, 8), 16
A_L0 = ADA_START
A_L1 = A_L0 + NPAIR * ADA_TURN[0]
A_MIX0 = A_L1 + NPAIR * ADA_TURN[1]
A_FF = A_MIX0 + ADA_MIX[0]
A_MIX1 = A_FF + ADA_FF
HEAD_UNITS = 9
OUT1_UNITS = D_INNER * D // (P * UW)
MIX_UNITS = (2 * D_CONV + 3 * D_ATT) // 256
OUT2_UNITS = D * D // (P * UW)
FF_UNITS = 2 * FF // 256
DOWN_UNITS = FF // 256
JOB_UP = 4 * FE // 512
JOB_DOWN = FE // 256
JOB_UNITS = JOB_UP + JOB_DOWN
UNIT_L1 = H * HEAD_UNITS + OUT1_UNITS
UNIT_L2 = MIX_UNITS + OUT2_UNITS
S_B1 = 0
S_B2 = L * UNIT_L1
S_FF = S_B2 + UNIT_L2
S_B3 = S_FF + FF_UNITS + DOWN_UNITS
S_MOE = S_B3 + UNIT_L2
assert S_MOE % HALF == 2 and A_MIX1 + ADA_MIX[1] == ADA_UNITS and (2 * HEAD_UNITS) % HALF == 0 and JOB_UNITS % RAW == 0 and JOB_UNITS % HL == 0 and ADA_TURN[0] % HALF == 0 and ADA_TURN[1] % HALF == 0
FREE0, DONE0 = HALF, 1

N_FINAL, N_MIX, N_FFN = 2, (3, 5), (4, 6)
SHIFT = {0: 0, 1: 72, 3: 24, 4: 48, 5: 96, 6: 120}
ROWS1_LOADED = 16 * 6 * L
ROWS_LOADED = 16 * (11 * L + 1)
STEPS_PAIR = (126, 102)
BEFORE_QACC = 2 * D_INNER // P * S + 2 * S + 4 * (CONV_K - 1 + S)
TWO_PI_2 = round((2 * np.pi - 6.28125) * 2 ** 21) / 2 ** 21
TWO_PI = (6.28125, TWO_PI_2, float(np.float32(2 * np.pi - 6.28125 - TWO_PI_2)))
ROUND = 12582912.0
PI_BELOW = 3.1415925


class Unit:

    def __init__(self, n, turn=0, per=0):
        self.n, self.turn, self.per = n, turn, per

    def count(self, k=1):
        return self.turn * self.per + (self.n + k) if self.per else self.n + k

    def free(self, k=1):
        return self.count(k + FREE0)

    def done(self, k=1):
        return self.count(k + DONE0)

    @property
    def raw(self):
        return self.n % HALF if self.n < S_MOE else MOE_SLOTS[(self.n - S_MOE) % RAW]

    @property
    def loads(self):
        slots = HALF if self.n < S_MOE else RAW
        if self.n < S_MOE:
            first = self.n // HALF
        else:
            first = (self.n - S_MOE) // RAW + ((S_MOE + HALF - 1 - self.raw) // HALF if self.raw < HALF else ADA_UNITS // HALF)
        return self.turn * (16 * self.per // slots) + (16 * first + 16) if self.per else 16 * first + 16

    @property
    def hl(self):
        return self.n % HL

    @property
    def bank(self):
        return self.n % 2

    def plus(self, k):
        return Unit(self.n + k, self.turn, self.per)


class Ada:

    def __init__(self, n, first, turn=0, per=0):
        self.n, self.turn, self.per, self.col = n, turn, per, 2 * (n - first)

    def count(self, k=1):
        return self.turn * self.per + (self.n + k) if self.per else self.n + k

    def sums(self, k=1):
        return self.count(k) if self.n < A_MIX0 else self.count(k - ADA_MIX[0])

    @property
    def raw(self):
        return HALF + self.n % HALF

    @property
    def loads(self):
        first = 16 * (self.n // HALF + 1)
        return self.turn * (16 * self.per // HALF) + first if self.per else first


def ada_l0(pair):
    at = [(0, 0, pair * 2 + (8 + i)) for i in range(2)] + [(0, 1, pair * 6 + i) for i in range(6)] + [(1, 0, pair)]
    return [(Ada(A_L0 + i, A_L0, pair, ADA_TURN[0]),) + a for i, a in enumerate(at)]


def ada_l1(pair):
    return [(Ada(A_L1 + i, A_L1, pair, ADA_TURN[1]), 1, 0, pair * 6 + (2 + i)) for i in range(ADA_TURN[1])]


def ada_beside(l, j):
    if l == 0:
        return j // 2 if j >= 0 and j % 2 == 0 else None
    return j // 3 if j >= 0 and j % 3 == 1 else None


ADA_AT_START = [(Ada(i, 0), 0, 0, i) for i in range(ADA_START)]
ADA_AT_FF = [(Ada(A_FF + i, A_FF), 1, 1, i) for i in range(ADA_FF)]
ADA_AT_MIX = [[(Ada(first + i, first), 1, l, ADA2 - ADA_MIX[l] + i) for i in range(ADA_MIX[l])] for l, first in enumerate((A_MIX0, A_MIX1))]


class Chain:

    def __init__(self, eng, sem):
        self.eng, self.sem, self.n, self.turn, self.per = eng, sem, 0, 0, 0

    def __call__(self, ins):
        self.mark(ins)
        self.wait()

    def mark(self, ins):
        ins.then_inc(self.sem, 1)
        self.n += 1

    def wait(self, back=0):
        v = self.n - back
        self.eng.wait_ge(self.sem, self.turn * self.per + v if self.per else v)

    def enter(self, turn, per):
        self.n0, self.turn, self.per = self.n, turn, per

    def leave(self, turns):
        got = self.n - self.n0
        assert got == self.per, f"steps in one turn: {got}, not {self.per}"
        self.n, self.turn, self.per = self.n0 + turns * got, 0, 0


def two_block_model(nc, x, positions, consts, c, w_ada, b_ada, norm_g, w_in, conv_w, conv_b, b_igate, b_fgate,
                    gn_m, gn_r, w_out, final_g, c_2, w_ada_2, b_ada_2, norm_mix_g, norm_ffn_g, w_in_2, w_out_2,
                    conv_w_2, conv_b_2, conv_ln_g, conv_ln_b, q_norm_g, k_norm_g, rel_bias, ffn_w_gate, ffn_w_up,
                    ffn_w_down, w_router, b_router, moe_w_gate, moe_w_up, moe_w_down, out):
    ctx = ExitStack()
    with ctx:
        def sb(name, shape, dt=F32, stack=ctx):
            return stack.enter_context(nc.sbuf_tensor(name, shape, dt))

        def sem(name):
            return ctx.enter_context(nc.semaphore(name))

        raw = sb("raw", [P, RAW, UW])
        whi = sb("whi", [P, HL, UW], F32R)
        wlo = sb("wlo", [P, HL, UW], F32R)
        xT = sb("xT", [P, KD, S])
        h = sb("h", [P, KD, S])
        hhi = sb("hhi", [P, KD, S], F32R)
        hlo = sb("hlo", [P, KD, S], F32R)
        cst = sb("cst", [P, C_BEFORE])
        ones = sb("ones", [P, S])
        mean256 = sb("mean256", [P, P])
        eps = sb("eps", [P, 1])
        ln_eps = sb("ln_eps", [P, 1])
        par1 = sb("par1", [P, L, P])
        par2 = sb("par2", [P, L, P])
        taps2 = sb("taps2", [P, L, P])
        cact = sb("cact", [P, 2, KD])
        mod = sb("mod", [P, ADA_UNITS * 2])
        amul = sb("amul", [P, 7, KD])
        wgate = sb("wgate", [P, L, KD, 2 * H])
        gbias = sb("gbias", [H, L, 2])
        rstd = sb("rstd", [P, S])
        acc = sb("acc", [P, HALF, S])
        acc2 = sb("acc2", [P, S])

        b1 = ExitStack()
        yhi = sb("yhi", [P, D_INNER // P, S], F32R, b1)
        ylo = sb("ylo", [P, D_INNER // P, S], F32R, b1)
        cosT = sb("cosT", [P, S], F32, b1)
        sinT = sb("sinT", [P, S], F32, b1)
        qpad = sb("qpad", [P, 2, 2, CONV_K - 1 + S], F32, b1)
        qacc = sb("qacc", [P, 2, 2, S], F32, b1)
        rot = sb("rot", [P, 2, 2, S], F32, b1)
        qk = sb("qk", [P, 2, 2, S], F32, b1)
        vtok = sb("vtok", [P, 2, HD], F32, b1)
        osig = sb("osig", [P, 2, S], F32, b1)
        zsil = sb("zsil", [P, 2, S], F32, b1)
        bcs = sb("bcs", [P, 2, S], F32, b1)
        arg = sb("arg", [P, S + P], F32, b1)
        sT = sb("sT", [P, S + P], F32, b1)
        den = rstd
        hn = sb("hn", [P, 2, S], F32, b1)
        sq, yf = (qpad[:, i, :, CONV_K - 1:] for i in range(2))
        gdiag = h[0:H].rearrange("q (h a) s -> q h a s", h=H)
        acol = sb("acol", [P, 2, H], F32, b1)
        b1.close()
        bg = ExitStack()
        sb("before_qacc", [P, BEFORE_QACC], F32, bg)
        gt = sb("gt", [H, 8, S], F32, bg)
        bg.close()
        b0 = ExitStack()
        xtok = sb("xtok", [P, 2, D], F32, b0)
        prow = sb("prow", [P, 6, P], F32, b0)
        crow = sb("crow", [2 * KD, P], F32, b0)
        b0.close()
        bt = ExitStack()
        sb("behind_y", [P, 2 * D_INNER // P * S], F32, bt)
        sb("behind_cos", [P, 2 * S], F32, bt)
        posi = sb("posi", [P, S], I32, bt)
        posf = sb("posf", [P, S], F32, bt)
        turns = sb("turns", [P, 2, S], F32, bt)
        ang = sb("ang", [P, S], F32, bt)
        bt.close()

        b2 = ExitStack()
        y2hi = sb("y2hi", [P, KD, S], F32R, b2)
        y2lo = sb("y2lo", [P, KD, S], F32R, b2)
        zpad = sb("zpad", [P, CT, CW - 1 + S], F32, b2)
        zacc = sb("zacc", [P, CT, S], F32, b2)
        sig = sb("sig", [P, 2, S], F32, b2)
        q2 = sb("q2", [P, 2, CT, S], F32, b2)
        sq2 = h[:, :, :].rearrange("p (a j) s -> p a j s", a=2)
        rs2 = sb("rs2", [NH2, 2, S], F32, b2)
        v2 = sb("v2", [P, 2, D_ATT], F32, b2)
        bias2 = sb("bias2", [P, NH2, S], F32, b2)
        s2 = sb("s2", [P, 2, S + P], F32, b2)
        p2 = sb("p2", [P, 2, S + P], F32, b2)
        pT = sb("pT", [P, 2, S + P], F32, b2)
        st2 = sb("st2", [P, 2, 8], F32, b2)
        mean512 = sb("mean512", [P, P], F32, b2)
        cpad = sb("cpad", [P, KD, 2 * max(ADA_MIX) - 1], F32, b2)
        arow = sb("arow", [max(ADA_MIX), S], F32, b2)
        hc = sb("hc", [P, C_ALL - C_HSUM], F32, b2)
        b2.close()

        bf = ExitStack()
        fhi = sb("fhi", [P, FF // P, S], F32R, bf)
        flo = sb("flo", [P, FF // P, S], F32R, bf)
        fg = sb("fg", [P, 2, 2, S], F32, bf)
        fa = sb("fa", [P, 2, 2, S], F32, bf)
        bf.close()

        bm = ExitStack()
        thi = sb("thi", [P, FE // P, P], F32R, bm)
        tlo = sb("tlo", [P, FE // P, P], F32R, bm)
        htok = sb("htok", [P, 2, D], F32, bm)
        xghi = sb("xghi", [P, KD, P], F32R, bm)
        xglo = sb("xglo", [P, KD, P], F32R, bm)
        mg = sb("mg", [P, 2, 512], F32, bm)
        ma = sb("ma", [P, 2, 512], F32, bm)
        pick = sb("pick", [P, 2, P], F32, bm)
        pickw = sb("pickw", [P, 2, P], F32, bm)
        pickT = sb("pickT", [P, S], F32, bm)
        yexp = sb("yexp", [P, D], F32, bm)
        moe = h
        wr = sb("wr", [P, KD, NE], F32, bm)
        rb = sb("rb", [P, NE], F32, bm)
        lg = sb("lg", [P, 12, 2, NE], F32, bm)
        comb = sb("comb", [P, 2, NE + 1], F32, bm)
        posm = sb("posm", [P, 2, NE + 1], F32, bm)
        r1 = sb("r1", [1, 10, NE], F32, bm)
        jobs = sb("jobs", [1, NE], I32, bm)
        bi = sb("bi", [P, C_HSUM - C_BEFORE], F32, bm)
        otok = h[:, :, :].rearrange("p (t k) s -> p t (k s)", t=2)
        bm.close()

        ps = [ctx.enter_context(nc.psum_tensor(f"ps{i}", [P, 512], F32)) for i in range(8)]
        ps2 = [b[:, :].rearrange("p (a s) -> p a s", a=2) for b in ps]
        ps4 = [b[:, :].rearrange("p (a s) -> p a s", a=4) for b in ps]
        ext = nc.dram_tensor("extended_bias", [L, NH2, EXT], F32, kind="Internal").ap()
        rep = nc.dram_tensor("repeated_bias", [L, NH2, P, EXT], F32, kind="Internal").ap()

        ident = cst[:, C_ID:C_ID + P]
        causal = cst[:, C_CAUSAL:C_CAUSAL + S]
        freq = cst[:, C_FREQ:C_FREQ + 1]
        before, iota = bi[:, 0:P], bi[:, P:2 * P]
        hsum = hc[:, 0:CT * NH2].rearrange("p (j h) -> p j h", j=CT)
        hbc = hc[0:NH2, CT * NH2:CT * NH2 + CT * P].rearrange("p (j m) -> p j m", j=CT)

        raw_in = [sem(f"raw_in{i}") for i in range(RAW)]
        c_in, rows1_in = sem("c_in"), sem("rows1_in")
        x_in, const_in, rows_in, gate_in, pos_in = sem("x_in"), sem("const_in"), sem("rows_in"), sem("gate_in"), sem("pos_in")
        ext_out, bias_in, router_in, stored = sem("ext_out"), sem("bias_in"), sem("router_in"), sem("stored")
        raw_free = sem("raw_free")
        hi_ready = sem("hi_ready")
        unit_done = sem("unit_done")
        memset_done, x_turned = sem("memset_done"), sem("x_turned")
        x_ready = sem("x_ready")
        rows_turned, c_turned, cact_ready = sem("rows_turned"), sem("c_turned"), sem("cact_ready")
        ada_free = sem("ada_free")
        ada_done = sem("ada_done")
        mod_taken = sem("mod_taken")
        cpad_ready, arow_ready, arow_turned = sem("cpad_ready"), sem("arow_ready"), sem("arow_turned")
        angle_ready, sin_ready = sem("angle_ready"), sem("sin_ready")
        squares, sum_ready, std_ready, h_ready, hhi_ready, hlo_ready = (
            sem("squares"), sem("sum_ready"), sem("std_ready"), sem("h_ready"), sem("hhi_ready"), sem("hlo_ready"))
        gates_done, gate_f, gate_ln, gate_em, gate_m, a_ready, a_turned, acol_ready = (
            sem("gates_done"), sem("gate_f"), sem("gate_ln"), sem("gate_em"), sem("gate_m"), sem("a_ready"),
            sem("a_turned"), sem("acol_ready"))
        taken_v, taken_s = sem("taken_v"), sem("taken_s")
        conv_done, act_done, rot_done = sem("conv_done"), sem("act_done"), sem("rot_done")
        bc_done, bc_copied, arg_ready, exp_ready = sem("bc_done"), sem("bc_copied"), sem("arg_ready"), sem("exp_ready")
        scores_done, sT_ready, pv_done = sem("scores_done"), sem("sT_ready"), sem("pv_done")
        hn_ready, mean_done, hc_ready, sq_ready, var_done, sd_ready = (
            sem("hn_ready"), sem("mean_done"), sem("hc_ready"), sem("sq_ready"), sem("var_done"), sem("sd_ready"))
        y_ready, yhi_ready, ylo_ready = sem("y_ready"), sem("yhi_ready"), sem("ylo_ready")
        gemm_taken, sig_ready, sq2_ready, hss_done, hr_ready, hbc_done, qn_ready = (
            sem("gemm_taken"), sem("sig_ready"), sem("sq2_ready"), sem("hss_done"), sem("hr_ready"),
            sem("hbc_done"), sem("qn_ready"))
        v2_ready, sc2_done, s2_ready, p2_sum, p2_ready, pT_done, pT_ready, o2_done, o2_ready = (
            sem("v2_ready"), sem("sc2_done"), sem("s2_ready"), sem("p2_sum"), sem("p2_ready"), sem("pT_done"),
            sem("pT_ready"), sem("o2_done"), sem("o2_ready"))
        conv_step, zc_ready, zmean_done, zsq_ready, zvar_done, zstd_ready, zn_ready, zact_ready = (
            sem("conv_step"), sem("zc_ready"), sem("zmean_done"), sem("zsq_ready"), sem("zvar_done"),
            sem("zstd_ready"), sem("zn_ready"), sem("zact_ready"))
        y2hi_ready, y2lo_ready = sem("y2hi_ready"), sem("y2lo_ready")
        fg_ready, fa_ready, fhi_ready, flo_ready = sem("fg_ready"), sem("fa_ready"), sem("fhi_ready"), sem("flo_ready")
        logits_done, e_ready, route_ready, rank_done, jobs_ready, htok_done, htok_ready = (
            sem("logits_done"), sem("e_ready"), sem("route_ready"), sem("rank_done"), sem("jobs_ready"),
            sem("htok_done"), sem("htok_ready"))
        route_exp, pick_ready, xg_done, xghi_ready, xglo_ready = (
            sem("route_exp"), sem("pick_ready"), sem("xg_done"), sem("xghi_ready"), sem("xglo_ready"))
        mg_ready, ma_ready, turned, thi_ready, tlo_ready = (
            sem("mg_ready"), sem("ma_ready"), sem("turned"), sem("thi_ready"), sem("tlo_ready"))
        pickT_done, pickT_ready, yexp_ready, spread_done, spread_taken = (
            sem("pickT_done"), sem("pickT_ready"), sem("yexp_ready"), sem("spread_done"), sem("spread_taken"))
        out_turned, out_ready = sem("out_turned"), sem("out_ready")
        vector_step, scalar_step = sem("vector_step"), sem("scalar_step")
        block = ctx.enter_context(nc.Block())

        @block.sync
        def _(sp):
            for i, v in enumerate((c, c_2)):
                sp.dma_start(crow[KD * i:KD * (i + 1), :], v[0].rearrange("(k p) -> k p", p=P)).then_inc(c_in, 16)
            sp.dma_start(cst[:], consts[:, 0:C_BEFORE]).then_inc(const_in, 16)
            sp.dma_start(xtok[:], x[0].rearrange("(t p) d -> p t d", p=P)).then_inc(x_in, 16)

            def load(u, src, k):
                sp.wait_ge(raw_free, u.free(1 - (HALF if u.n < S_MOE else RAW)))
                sp.dma_start(raw[:, u.raw, :].rearrange("p (k n) -> p k n", k=k), src).then_inc(raw_in[u.raw], 16)

            def ada_load(a, block, l, at):
                if a.n >= HALF:
                    sp.wait_ge(ada_done, a.count(1 - HALF))
                w = (w_ada, w_ada_2)[block][l].rearrange("(k p) n -> p k n", p=P)
                sp.dma_start(raw[:, a.raw, :].rearrange("p (k n) -> p k n", k=KD), w[:, :, bass.ds(at * 256, 256)])\
                    .then_inc(raw_in[a.raw], 16)

            for a in ADA_AT_START:
                ada_load(*a)
            for l in range(L):
                wl = w_in[l].rearrange("(k p) n -> p k n", p=P)
                u0 = Unit(S_B1 + l * UNIT_L1)
                with sp.Fori(0, NPAIR) as pair:
                    ada = (ada_l0, ada_l1)[l](pair)
                    for j in range(2 * HEAD_UNITS):
                        part, hh = j % HEAD_UNITS, j // HEAD_UNITS
                        col = part * D_MLSTM if part < 5 else RET_COL + (part - 5) * D_RET
                        load(Unit(u0.n + j, pair, 2 * HEAD_UNITS), wl[:, :, bass.ds(pair * (2 * HD) + (col + hh * HD), HD)], KD)
                        if j and ada_beside(l, j - 1) is not None:
                            ada_load(*ada[ada_beside(l, j - 1)])
                for j in range(OUT1_UNITS):
                    load(Unit(u0.n + H * HEAD_UNITS + j),
                         w_out[l].rearrange("(k p) n -> p k n", p=P)[:, 2 * j:2 * j + 2, :], 2)

            def mixer_loads(l, first):
                wl = w_in_2[l].rearrange("(k p) n -> p k n", p=P)
                for j, col in enumerate((0, 2, 1, 3, 4, 5, 6, 7, 8, 9)):
                    load(Unit(first + j), wl[:, :, 256 * col:256 * col + 256], KD)
                for a in ADA_AT_MIX[l][:HALF]:
                    ada_load(*a)
                for j, d in enumerate((2, 3, 0, 1)):
                    load(Unit(first + MIX_UNITS + j),
                         w_out_2[l].rearrange("(k p) n -> p k n", p=P)[:, 2 * d:2 * d + 2, :], 2)
                for a in ADA_AT_MIX[l][HALF:]:
                    ada_load(*a)

            mixer_loads(0, S_B2)
            for j in range(FF_UNITS):
                w = (ffn_w_gate, ffn_w_up)[j % 2][0]
                load(Unit(S_FF + j), w.rearrange("(k p) n -> p k n", p=P)[:, :, 128 * (j - j % 2):128 * (j - j % 2) + 256], KD)
                if j % 2 == 0 and j // 2 < ADA_FF:
                    ada_load(*ADA_AT_FF[j // 2])
            for j in range(DOWN_UNITS):
                load(Unit(S_FF + FF_UNITS + j), ffn_w_down[0].rearrange("(k p) n -> p k n", p=P)[:, 2 * j:2 * j + 2, :], 2)
                if j % 2 == 0 and (FF_UNITS + j) // 2 < ADA_FF:
                    ada_load(*ADA_AT_FF[(FF_UNITS + j) // 2])
            mixer_loads(1, S_B3)

            def job_loads(e, turn, first, units):
                wg, wu = (w[0, bass.ds(e, 1)].rearrange("e (k p) n -> p (e k) n", p=P) for w in (moe_w_gate, moe_w_up))
                wd = moe_w_down[0, bass.ds(e, 1)].rearrange("e (k p) n -> p (e k) n", p=P)
                for j in units:
                    u = Unit(first + j, turn, JOB_UNITS)
                    if j < JOB_UP:
                        w, c, half = (wg, wu)[j % 4 // 2], j // 4, j % 2
                        load(u, w[:, 4 * half:4 * half + 4, 512 * c:512 * c + 512], 4)
                    else:
                        f = 2 * (j - JOB_UP)
                        load(u, wd[:, f:f + 2, :], 2)

            sp.wait_ge(ada_done, ADA_UNITS)
            with sp.Fori(0, NE) as e:
                job_loads(e, e, S_MOE, range(JOB_UNITS))
            sp.wait_ge(jobs_ready, 1)
            nx = sp.value_load(jobs[0:1, 0:1], min_val=0, max_val=3)
            e = sp.value_load(jobs[0:1, 1:2], min_val=0, max_val=NE - 1)
            job_loads(e, NE, S_MOE, range(LOOK))
            with sp.If(nx > 0):
                with sp.Fori(0, nx) as j:
                    e = sp.value_load(jobs[0:1, bass.ds(j + 1, 1)], min_val=0, max_val=NE - 1)
                    job_loads(e, j, S_MOE + NE * JOB_UNITS, range(LOOK, JOB_UNITS))
                    e2 = sp.value_load(jobs[0:1, bass.ds(j + 2, 1)], min_val=0, max_val=NE - 1)
                    job_loads(e2, j, S_MOE + (NE + 1) * JOB_UNITS, range(LOOK))
            for t in range(2):
                sp.wait_ge(out_ready, t + 1)
                sp.dma_start(out[0, t * P:(t + 1) * P, :], otok[:, t]).then_inc(stored, 16)
            sp.wait_ge(stored, 32)

        @block.gpsimd
        def _(pool):
            pool.dma_start(posi[:], positions[0:1, :].broadcast_to([P, S])).then_inc(pos_in, 16)
            for l in range(L):
                pool.dma_start(wgate[:, l], w_in[l].rearrange("(k p) n -> p k n", p=P)[:, :, GATE_COL:RET_COL]).then_inc(gate_in, 16)
                pool.dma_start(gbias[:, l, 0:1], b_igate[l].rearrange("(h o) -> h o", o=1)).then_inc(gate_in, 16)
                pool.dma_start(gbias[:, l, 1:2], b_fgate[l].rearrange("(h o) -> h o", o=1)).then_inc(gate_in, 16)
            for l in range(L):
                for at, v in ((P2_BADA, b_ada_2[l]), (P2_MIX, norm_mix_g[l]), (P2_FFN, norm_ffn_g[l]), (P2_CB, conv_b_2[l]),
                              (P2_LG, conv_ln_g[l]), (P2_LB, conv_ln_b[l])):
                    k = v.shape[0] // P
                    pool.dma_start(prow[at:at + k, 2 + l, :], v.rearrange("(k p) -> k p", p=P)).then_inc(rows_in, 16)
                for at, v in ((P2_QN, q_norm_g[l:l + 1, :]), (P2_KN, k_norm_g[l:l + 1, :])):
                    for half in range(2):
                        pool.dma_start(prow[at:at + 1, 2 + l, half * HD2:(half + 1) * HD2], v).then_inc(rows_in, 16)
                pool.dma_start(prow[0:CW * CT, 4 + l, :], conv_w_2[l, :, 0, :].rearrange("t (k p) -> (t k) p", p=P)).then_inc(rows_in, 16)
            pool.dma_start(prow[P2_FIN:P2_FIN + KD, 2, :], final_g.rearrange("(k p) -> k p", p=P)).then_inc(rows_in, 16)
            for l in range(L):
                pool.dma_start(ext[l, :, 0:127].unsqueeze(2), rel_bias[l, :, 0:1].unsqueeze(1).broadcast_to([NH2, 127, 1])).then_inc(ext_out, 16)
                pool.dma_start(ext[l, :, 127:EXT], rel_bias[l]).then_inc(ext_out, 16)
            pool.wait_ge(ext_out, 16 * 2 * L)
            for l in range(L):
                pool.dma_start(rep[l], ext[l].unsqueeze(1).broadcast_to([NH2, P, EXT])).then_inc(ext_out, 16)
            pool.wait_ge(ext_out, 16 * 3 * L)
            for l in range(L):
                pool.wait_ge(x_ready, 4 * (N_FINAL + 1) if l == 0 else 4 * (N_MIX[1] + 1))
                src = bass.AP(tensor=rep.tensor, offset=l * NH2 * P * EXT + 127, ap=[[EXT - 1, P], [P * EXT, NH2], [1, S]])
                pool.dma_start(bias2[:], src).then_inc(bias_in, 16)
                pool.dma_start(hc[:], consts[:, C_HSUM:C_ALL]).then_inc(bias_in, 16)
            pool.wait_ge(x_ready, 4 * (N_FFN[1] + 1))
            pool.dma_start(wr[:], w_router[0].rearrange("(k p) n -> p k n", p=P)).then_inc(router_in, 16)
            pool.dma_start(bi[:], consts[:, C_BEFORE:C_HSUM]).then_inc(router_in, 16)
            pool.dma_start(rb[:], b_router[0:1, :].broadcast_to([P, NE])).then_inc(router_in, 16)

        class Head:

            def __init__(self, layer, hh, pair):
                self.n, self.pair, self.h = H * layer + hh, pair, pair * 2 + hh

            def count(self, per, k):
                return self.pair * (2 * per) + (self.n * per + k)

        class Job:

            def __init__(self, n, turn):
                self.n, self.turn = n, turn

            def count(self, per, k):
                return self.turn * per + (self.n * per + k)

            def unit(self, i):
                return Unit(S_MOE + self.n * JOB_UNITS + i, self.turn, JOB_UNITS)

        def split_no(n):
            return n if n < N_FINAL else n - 1

        @block.scalar
        def _(act):
            step = Chain(act, scalar_step)

            def high(u):
                act.wait_ge(raw_in[u.raw], u.loads)
                if u.n >= HL or u.per:
                    act.wait_ge(unit_done, u.done(1 - HL))
                nc.scalar.copy(whi[:, u.hl, :], raw[:, u.raw, :]).then_inc(hi_ready, 1)

            def inverse_root(to, of, ready, value, scale=1.0):
                n = to.shape[0]
                step.mark(nc.scalar.activation(ln_eps[:], eps[:], ACT.Ln))
                act.wait_ge(ready, value)
                step(nc.scalar.activation(to, of, ACT.Ln, bias=eps[0:n], scale=scale))
                return nc.scalar.activation(to, to, ACT.Exp, scale=-0.5)

            def norm_std(n):
                for i in range(4):
                    act.wait_ge(x_ready, 4 * n + i + 1)
                    nc.scalar.activation(h[:, 2 * i:2 * i + 2], xT[:, 2 * i:2 * i + 2], ACT.Square).then_inc(squares, 1)
                inverse_root(rstd[:], ps2[7][:, 0], sum_ready, n + 1, 1.0 / D).then_inc(std_ready, 1)

            def norm(n):
                if n:
                    norm_std(n)
                if n != N_FINAL:
                    for half in range(2):
                        act.wait_ge(h_ready, 2 * split_no(n) + half + 1)
                        nc.scalar.copy(hhi[:, 4 * half:4 * half + 4], h[:, 4 * half:4 * half + 4]).then_inc(hhi_ready, 1)

            for l in range(L):
                for at, v in ((P1_BADA, b_ada[l]), (P1_NORM, norm_g[l]), (P1_CB, conv_b[l]), (P1_GNM, gn_m[l]), (P1_GNR, gn_r[l])):
                    k = v.shape[0] // P
                    act.dma_start(prow[at:at + k, l, :], v.rearrange("(k p) -> k p", p=P)).then_inc(rows1_in, 16)
                act.dma_start(prow[P1_CW:P1_CW + 64, l, :], conv_w[l].rearrange("t (k p) -> (t k) p", p=P)).then_inc(rows1_in, 16)
            act.wait_ge(c_turned, 1)
            nc.scalar.activation(cact[:], ps[6][:, 256:256 + 2 * KD].rearrange("p (a k) -> p a k", a=2), ACT.Silu)\
                .then_inc(cact_ready, 1)
            norm_std(0)
            act.wait_ge(angle_ready, 1)
            nc.scalar.activation(sinT[:], ang[:], ACT.Sin).then_inc(sin_ready, 1)
            step(nc.scalar.activation(turns[:, 0], ang[:], ACT.Abs))
            step(nc.scalar.activation(turns[:, 1], turns[:, 0], ACT.Copy, bias=float(np.pi / 2), scale=-1.0))
            nc.scalar.activation(cosT[:], turns[:, 1], ACT.Sin).then_inc(sin_ready, 1)

            for i in range(LOOK):
                high(Unit(S_B1 + i))
            for l in range(L):
                norm(l)
                act.wait_ge(gate_f, l + 1)
                step(nc.scalar.activation(gt[:, 2], gt[:, 1], ACT.Abs))
                step(nc.scalar.activation(gt[:, 2], gt[:, 2], ACT.Exp, scale=-1.0))
                nc.scalar.activation(gt[:, 2], gt[:, 2], ACT.Ln, bias=ones[0:H, 0:1]).then_inc(gate_ln, 1)
                act.wait_ge(gate_m, l + 1)
                nc.scalar.activation(gt[:, 7], gt[:, 7], ACT.Exp, scale=-1.0).then_inc(gate_em, 1)
                with act.Fori(0, NPAIR) as pair:
                    step.enter(pair, 8)
                    for hh in range(2):
                        hd = Head(l, hh, pair)
                        u0 = Unit(S_B1 + l * UNIT_L1 + hh * HEAD_UNITS, pair, 2 * HEAD_UNITS)
                        q, k, v, o, z, rq, rk, rv, rz = (u0.plus(i) for i in range(HEAD_UNITS))
                        high(q.plus(LOOK))
                        high(k.plus(LOOK))
                        high(v.plus(LOOK))
                        act.wait_ge(unit_done, v.done())
                        nc.scalar.copy(vtok[:], ps2[v.bank]).then_inc(taken_s, 1)
                        act.wait_ge(conv_done, hd.count(1, 1))
                        nc.scalar.activation(qk[:], qacc[:], ACT.Silu).then_inc(act_done, 1)
                        high(o.plus(LOOK))
                        act.wait_ge(bc_done, hd.count(1, 1))
                        nc.scalar.copy(bcs[:], ps2[3]).then_inc(bc_copied, 1)
                        act.wait_ge(unit_done, o.done())
                        nc.scalar.activation(osig[:], ps2[o.bank], ACT.Tanh, scale=0.5).then_inc(taken_s, 1)
                        high(z.plus(LOOK))
                        act.wait_ge(arg_ready, hd.count(1, 1))
                        nc.scalar.activation(arg[:], arg[:], ACT.Exp).then_inc(exp_ready, 1)
                        act.wait_ge(unit_done, z.done())
                        nc.scalar.activation(zsil[:], ps2[z.bank], ACT.Silu).then_inc(taken_s, 1)
                        high(rq.plus(LOOK))
                        high(rk.plus(LOOK))
                        act.wait_ge(hc_ready, hd.count(2, 1))
                        nc.scalar.activation(sq, hn[:], ACT.Square).then_inc(sq_ready, 1)
                        high(rv.plus(LOOK))
                        inverse_root(den[:], ps2[6][:, 1], var_done, hd.count(2, 1)).then_inc(sd_ready, 1)
                        act.wait_ge(unit_done, rv.done())
                        nc.scalar.copy(vtok[:], ps2[rv.bank]).then_inc(taken_s, 1)
                        high(rz.plus(LOOK))
                        act.wait_ge(y_ready, hd.count(2, 1))
                        nc.scalar.copy(yhi[:, bass.ds(hd.h * 2, 2), :], yf).then_inc(yhi_ready, 1)
                        act.wait_ge(unit_done, rz.done())
                        nc.scalar.activation(zsil[:], ps2[rz.bank], ACT.Silu).then_inc(taken_s, 1)
                        act.wait_ge(hc_ready, hd.count(2, 2))
                        nc.scalar.activation(sq, hn[:], ACT.Square).then_inc(sq_ready, 1)
                        inverse_root(den[:], ps2[6][:, 1], var_done, hd.count(2, 2)).then_inc(sd_ready, 1)
                        act.wait_ge(y_ready, hd.count(2, 2))
                        nc.scalar.copy(yhi[:, bass.ds(hd.h * 2 + KD, 2), :], yf).then_inc(yhi_ready, 1)
                step.leave(NPAIR)
                for j in range(OUT1_UNITS):
                    high(Unit(S_B1 + l * UNIT_L1 + H * HEAD_UNITS + j + LOOK))
            norm(N_FINAL)

            def mixer(l, first):
                norm(N_MIX[l])
                for j in range(MIX_UNITS):
                    u = Unit(first + j)
                    high(u.plus(LOOK))
                    if j in (1, 3):
                        act.wait_ge(unit_done, u.done())
                        if j == 3:
                            act.wait_ge(gemm_taken, 6 * l + 1)
                        nc.scalar.activation(sig[:], ps2[u.bank], ACT.Tanh, scale=0.5).then_inc(sig_ready, 1)
                    if j in (5, 7):
                        i = j // 2 - 2
                        act.wait_ge(gemm_taken, 6 * l + 4 + 2 * i)
                        nc.scalar.activation(sq2[:, i], q2[:, i], ACT.Square).then_inc(sq2_ready, 1)
                    if j == MIX_UNITS - 1:
                        inverse_root(rs2[:], ps2[2][0:NH2], hss_done, l + 1).then_inc(hr_ready, 1)
                    if j >= 8:
                        act.wait_ge(unit_done, u.done())
                        nc.scalar.copy(v2[:, :, 256 * (j - 8):256 * (j - 7)], ps2[u.bank]).then_inc(v2_ready, 1)
                for n in range(NH2):
                    b, at = n % 2, NH2 * l + n
                    act.wait_ge(s2_ready, at + 1)
                    step.mark(nc.scalar.activation(p2[:, b, 0:P], s2[:, b, 0:P], ACT.Exp, bias=st2[:, b, 2:3],
                                                   accum_out=st2[:, b, 4:5]))
                    nc.scalar.activation(p2[:, b, P:P + S], s2[:, b, P:P + S], ACT.Exp, bias=st2[:, b, 3:4],
                                         accum_out=st2[:, b, 5:6]).then_inc(p2_sum, 1)
                    if n % 2 == 0 and n:
                        act.wait_ge(o2_done, at)
                        nc.scalar.copy(y2hi[:, CT + n // 2 - 1], ps2[6 + (n // 2 - 1) % 2][:, 0]).then_inc(y2hi_ready, 1)
                act.wait_ge(o2_done, NH2 * (l + 1))
                nc.scalar.copy(y2hi[:, KD - 1], ps2[7][:, 0]).then_inc(y2hi_ready, 1)
                act.wait_ge(ada_done, (A_MIX0, A_MIX1)[l] + ADA_MIX[l])
                nc.scalar.copy(arow[0:ADA_MIX[l]], ps[0][0:ADA_MIX[l], 0:S]).then_inc(arow_ready, 1)
                act.wait_ge(zc_ready, l + 1)
                nc.scalar.activation(sq2[:, 0], zacc[:], ACT.Square).then_inc(zsq_ready, 1)
                for j in range(2):
                    high(Unit(first + MIX_UNITS + LOOK + j))
                inverse_root(sig[:, 0], ps2[1][:, 1], zvar_done, l + 1).then_inc(zstd_ready, 1)
                act.wait_ge(zn_ready, l + 1)
                for t in range(CT):
                    step(nc.scalar.activation(q2[:, 0, t], zacc[:, t], ACT.Silu, bias=par2[:, l, P2_LB + t:P2_LB + t + 1],
                                              scale=par2[:, l, P2_LG + t:P2_LG + t + 1]))
                nc.scalar.copy(y2hi[:, 0:CT], q2[:, 0]).then_inc(y2hi_ready, 1)
                for j in range(2, OUT2_UNITS):
                    high(Unit(first + MIX_UNITS + LOOK + j))

            mixer(0, S_B2)
            norm(N_FFN[0])
            for j in range(FF_UNITS):
                u, i = Unit(S_FF + j), j // 2
                high(u.plus(LOOK))
                if j % 2 == 0:
                    act.wait_ge(unit_done, u.done())
                    nc.scalar.activation(fg[:, i % 2], ps2[u.bank], ACT.Silu).then_inc(fg_ready, 1)
                else:
                    act.wait_ge(fa_ready, i + 1)
                    nc.scalar.copy(fhi[:, 2 * i:2 * i + 2], fa[:, i % 2]).then_inc(fhi_ready, 1)
            for j in range(DOWN_UNITS):
                high(Unit(S_FF + FF_UNITS + j + LOOK))
            mixer(1, S_B3)
            norm(N_FFN[1])
            act.wait_ge(htok_done, 1)
            step.mark(nc.scalar.copy(htok[:, 0, 0:512], ps[0][:, :]))
            nc.scalar.copy(htok[:, 0, 512:D], ps[1][:, :]).then_inc(htok_ready, 1)
            act.wait_ge(e_ready, 1)
            nc.scalar.activation(lg[:, 11, 0, 0:2], lg[:, 10, 1, 0:2], ACT.Exp).then_inc(route_exp, 1)

            def take_tokens(gather, half):
                act.wait_ge(xg_done, gather.count(2, half + 1))
                nc.scalar.copy(xghi[:, 4 * half:4 * half + 4], ps4[7]).then_inc(xghi_ready, 1)

            def expert(job, following):
                for i in range(JOB_UNITS):
                    high(job.unit(i + LOOK))
                    c = i // 4
                    if i < JOB_UP and i % 4 == 1:
                        act.wait_ge(unit_done, job.unit(i).done())
                        nc.scalar.activation(mg[:, c % 2], ps[c % 2][:, :], ACT.Silu).then_inc(mg_ready, 1)
                    if i % 4 == 2 and 1 <= c <= JOB_UP // 4:
                        act.wait_ge(turned, job.count(JOB_UP // 4, c))
                        nc.scalar.copy(thi[:, 4 * c - 4:4 * c], ps4[4]).then_inc(thi_ready, 1)
                    if following is not None and i in (JOB_UP + 2, JOB_UP + 6):
                        take_tokens(following, (i - JOB_UP) // 4)
                act.wait_ge(unit_done, job.unit(JOB_UNITS - 1).done())
                step.mark(nc.scalar.copy(yexp[:, 0:512], ps[5][:, :]))
                nc.scalar.copy(yexp[:, 512:D], ps[6][:, :]).then_inc(yexp_ready, 1)

            for half in range(2):
                take_tokens(Job(0, 0), half)
            with act.Fori(0, NE) as e:
                step.enter(e, 1)
                expert(Job(0, e), Job(1, e))
            step.leave(NE)
            act.wait_ge(jobs_ready, 1)
            nx = act.value_load(jobs[0:1, 0:1], min_val=0, max_val=3)
            with act.If(nx > 0):
                with act.Fori(0, nx) as j:
                    step.enter(j, 1)
                    for half in range(2):
                        take_tokens(Job(NE + 1, j), half)
                    expert(Job(NE, j), None)
            for t in range(2):
                act.wait_ge(out_turned, 2 * t + 1)
                nc.scalar.copy(otok[:, t, 0:512], ps[2 * t][:, :]).then_inc(scalar_step, 1)
                act.wait_ge(out_turned, 2 * t + 2)
                nc.scalar.copy(otok[:, t, 512:D], ps[2 * t + 1][:, :]).then_inc(out_ready, 1)

        @block.tensor
        def _(pe):
            mm = nc.tensor.matmul

            def products(u, norm=None):
                pe.wait_ge(raw_free, u.free())
                for j in range(2):
                    for k in range(KD):
                        if norm is not None and j == 0 and k % 4 == 0:
                            pe.wait_ge(hlo_ready, 2 * split_no(norm) + k // 4 + 1)
                        w = slice(256 * k + P * j, 256 * k + P * j + P)
                        mm(ps2[u.bank][:, j], whi[:, u.hl, w], hhi[:, k], start=k == 0, stop=False)
                        mm(ps2[u.bank][:, j], whi[:, u.hl, w], hlo[:, k], start=False, stop=False)
                        last = mm(ps2[u.bank][:, j], wlo[:, u.hl, w], hhi[:, k], start=False, stop=k == KD - 1)
                last.then_inc(unit_done, 1)

            def token_products(u):
                pe.wait_ge(raw_free, u.free())
                for t in range(2):
                    for k in range(KD):
                        w, s = slice(256 * k, 256 * k + 256), slice(P * t, P * t + P)
                        mm(ps2[u.bank][:, t], hhi[:, k, s], whi[:, u.hl, w], start=k == 0, stop=False)
                        mm(ps2[u.bank][:, t], hlo[:, k, s], whi[:, u.hl, w], start=False, stop=False)
                        last = mm(ps2[u.bank][:, t], hhi[:, k, s], wlo[:, u.hl, w], start=False, stop=k == KD - 1)
                last.then_inc(unit_done, 1)

            def rows_product(u, hi, lo, tile, first, final):
                pe.wait_ge(raw_free, u.free())
                for i in range(2):
                    for d in range(KD):
                        w = slice(D * i + P * d, D * i + P * d + P)
                        o = ps2[2 + d // 2][:, d % 2]
                        start, stop = first and i == 0 and d % 2 == 0, final and i == 1
                        mm(o, whi[:, u.hl, w], hi[:, tile + i], start=start, stop=False, skip_group_check=True)
                        mm(o, whi[:, u.hl, w], lo[:, tile + i], start=False, stop=False, skip_group_check=True)
                        last = mm(o, wlo[:, u.hl, w], hi[:, tile + i], start=False, stop=stop, skip_group_check=True)
                last.then_inc(unit_done, 1)

            def norm(n):
                for k in range(KD):
                    if k % 2 == 0:
                        pe.wait_ge(squares, 4 * n + k // 2 + 1)
                    last = mm(ps2[7][:, 0], ones[:, 0:P], h[:, k], start=k == 0, stop=k == KD - 1)
                last.then_inc(sum_ready, 1)

            def ada(a, bank):
                pe.wait_ge(ada_free, a.sums())
                for j in range(2):
                    last = mm(bank[:, a.col + j:a.col + j + 1], acc[:, a.n % HALF, j * P:(j + 1) * P], ones[:, 0:1],
                              start=True, stop=True)
                last.then_inc(ada_done, 1)

            pe.wait_ge(const_in, 16)
            pe.wait_ge(c_in, 32)
            nc.tensor.transpose(ps[6][:, 256:256 + 2 * KD], crow[:, :], ident[0:2 * KD, 0:2 * KD]).then_inc(c_turned, 1)
            pe.wait_ge(x_in, 16)
            for k in range(KD):
                for t in range(2):
                    last = nc.tensor.transpose(ps2[k // 2][:, k % 2, t * P:(t + 1) * P], xtok[:, t, k * P:(k + 1) * P], ident)
                    if k == 0 and t == 0:
                        last.then_inc(unit_done, DONE0)
            last.then_inc(x_turned, 1)
            pe.wait_ge(memset_done, 1)
            norm(0)
            for a in ADA_AT_START:
                ada(a[0], ps[6])
            pe.wait_ge(rows_in, ROWS_LOADED)
            pe.wait_ge(rows1_in, ROWS1_LOADED)
            for i, rows in enumerate((P, P) + P2_ROWS + (CW * CT, CW * CT)):
                last = nc.tensor.transpose(ps4[4 + i // 4][:, i % 4, 0:rows], prow[0:rows, i, :], ident[0:rows, 0:rows])
            last.then_inc(rows_turned, 1)

            for l in range(L):
                if l:
                    norm(l)
                pe.wait_ge(gate_in, 16 * 3 * L)
                for g in range(2):
                    for k in range(KD):
                        if g == 0 and k % 4 == 0:
                            pe.wait_ge(h_ready, 2 * l + 1 + k // 4)
                        last = mm(ps2[7][0:H, g], wgate[:, l, k, g * H:(g + 1) * H], h[:, k], start=k == 0, stop=k == KD - 1)
                last.then_inc(gates_done, 1)
                pe.wait_ge(a_ready, l + 1)
                for t in range(2):
                    last = mm(ps[7][:, t * H:(t + 1) * H], gt[:, 5, t * P:(t + 1) * P], ident[0:H, 0:H], start=True, stop=True)
                last.then_inc(a_turned, 1)
                pe.wait_ge(hlo_ready, 2 * l + 2)
                pe.wait_ge(acol_ready, l + 1)
                if l == 0:
                    pe.wait_ge(sin_ready, 2)

                def scores(x):
                    for s, (o, t) in enumerate(((ps[2][:, 0:S], slice(0, S)), (ps[2][:, S:S + P], slice(P, S)))):
                        for d in range(2):
                            last = mm(o, x[:, 1, d, s * P:(s + 1) * P], x[:, 0, d, t], start=d == 0, stop=d == 1)
                    last.then_inc(scores_done, 1)

                def values(normaliser):
                    for o, w in [(ps2[4][:, v], lambda s, v=v: vtok[:, s, v * P:(v + 1) * P]) for v in range(2)] + \
                            ([(ps2[5][:, 0], lambda s: ones[:, 0:P])] if normaliser else []):
                        mm(o, w(0), sT[:, 0:S], start=True, stop=False)
                        last = mm(o[:, P:S], w(1), sT[:, S:S + P], start=False, stop=True)
                    last.then_inc(pv_done, 1)

                def head_mean(x, half, done):
                    for v in range(2):
                        last = mm(ps2[6][:, half], mean256[:], x[:, v], start=v == 0, stop=v == 1)
                    last.then_inc(done, 1)

                with pe.Fori(0, NPAIR) as pair:
                    ada_units = (ada_l0, ada_l1)[l](pair)
                    for hh in range(2):
                        hd = Head(l, hh, pair)
                        u0 = Unit(S_B1 + l * UNIT_L1 + hh * HEAD_UNITS, pair, 2 * HEAD_UNITS)
                        q, k, v, o, z, rq, rk, rv, rz = (u0.plus(i) for i in range(HEAD_UNITS))

                        def ada_after(j):
                            at = hh * HEAD_UNITS + j
                            i = ada_beside(l, at - (1 if at == 2 * HEAD_UNITS - 1 else 2))
                            if i == 0:
                                pe.wait_ge(mod_taken, pair + (1, 3)[l])
                            if i is not None:
                                ada(ada_units[i][0], ps[7])

                        products(q)
                        ada_after(0)
                        products(k)
                        ada_after(1)
                        pe.wait_ge(taken_v, hd.count(4, 1))
                        token_products(v)
                        ada_after(2)
                        mm(ps[3][:, :], ones[0:H, 0:P], gdiag[:, bass.ds(hd.h, 1)].rearrange("p a b s -> p (a b s)"),
                           start=True, stop=True).then_inc(bc_done, 1)
                        pe.wait_ge(taken_v, hd.count(4, 2))
                        products(o)
                        ada_after(3)
                        pe.wait_ge(act_done, hd.count(1, 1))
                        scores(qk)
                        pe.wait_ge(taken_s, hd.count(5, 1))
                        products(z)
                        ada_after(4)
                        pe.wait_ge(sT_ready, hd.count(2, 1))
                        values(True)
                        pe.wait_ge(taken_s, hd.count(5, 2))
                        products(rq)
                        ada_after(5)
                        pe.wait_ge(hn_ready, hd.count(2, 1))
                        head_mean(hn, 0, mean_done)
                        pe.wait_ge(taken_s, hd.count(5, 3))
                        products(rk)
                        ada_after(6)
                        pe.wait_ge(sq_ready, hd.count(2, 1))
                        head_mean(sq, 1, var_done)
                        pe.wait_ge(taken_v, hd.count(4, 3))
                        token_products(rv)
                        ada_after(7)
                        pe.wait_ge(rot_done, hd.count(1, 1))
                        scores(rot)
                        pe.wait_ge(taken_v, hd.count(4, 4))
                        products(rz)
                        ada_after(8)
                        pe.wait_ge(sT_ready, hd.count(2, 2))
                        pe.wait_ge(taken_s, hd.count(5, 4))
                        values(False)
                        pe.wait_ge(taken_s, hd.count(5, 5))
                        pe.wait_ge(hn_ready, hd.count(2, 2))
                        head_mean(hn, 0, mean_done)
                        pe.wait_ge(sq_ready, hd.count(2, 2))
                        head_mean(sq, 1, var_done)
                pe.wait_ge(ylo_ready, 2 * H * (l + 1))
                for j in range(OUT1_UNITS):
                    rows_product(Unit(S_B1 + l * UNIT_L1 + H * HEAD_UNITS + j), yhi, ylo, 2 * j, j == 0, j == OUT1_UNITS - 1)
            norm(N_FINAL)

            def mixer(l, first):
                n0, rows = NH2 * l, ADA_MIX[l]
                norm(N_MIX[l])
                free = {2: (gemm_taken, 6 * l + 1), 3: (sig_ready, 2 * l + 1), 4: (gemm_taken, 6 * l + 2),
                        5: (sig_ready, 2 * l + 2), 6: (gemm_taken, 6 * l + 3), 7: (gemm_taken, 6 * l + 4),
                        8: (gemm_taken, 6 * l + 5), 9: (gemm_taken, 6 * l + 6)}
                for j in range(MIX_UNITS):
                    u = Unit(first + j)
                    if j in free:
                        pe.wait_ge(*free[j])
                    if j >= 8:
                        token_products(u)
                    else:
                        products(u, N_MIX[l] if j == 0 else None)
                    if j == 8:
                        for i in range(2):
                            pe.wait_ge(sq2_ready, 2 * l + i + 1)
                            for t in range(CT):
                                last = mm(ps2[2][0:NH2, i], hsum[:, t, :], sq2[:, i, t], start=t == 0, stop=t == CT - 1)
                        last.then_inc(hss_done, 1)
                pe.wait_ge(hr_ready, l + 1)
                for i in range(2):
                    for t in range(CT):
                        last = mm(ps2[3 + 2 * i + t // 2][:, t % 2], hbc[:, t, :], rs2[:, i], start=True, stop=True)
                last.then_inc(hbc_done, 1)

                def scores(n):
                    o, part = ps[2 + n % 2], slice(HD2 * (n % 2), HD2 * (n % 2) + HD2)
                    if n >= 2:
                        pe.wait_ge(s2_ready, n0 + n - 1)
                    mm(o[:, 0:P], q2[part, 0, n // 2, 0:P], q2[part, 1, n // 2, 0:P], start=True, stop=True)
                    mm(o[:, P:P + S], q2[part, 0, n // 2, P:S], q2[part, 1, n // 2, 0:S], start=True, stop=True)\
                        .then_inc(sc2_done, 1)

                def ada_rows(i):
                    a = ADA_AT_MIX[l][i][0]
                    pe.wait_ge(raw_in[a.raw], a.loads)
                    for k in range(KD):
                        last = mm(ps[0][0:rows, 0:S], cpad[:, k, max(ADA_MIX) - 1 - i:max(ADA_MIX) - 1 - i + rows],
                                  raw[:, a.raw, S * k:S * k + S], start=i == 0 and k == 0, stop=i == rows - 1 and k == KD - 1,
                                  skip_group_check=True)
                    last.then_inc(ada_done, 1)

                pe.wait_ge(cpad_ready, l + 1)
                pe.wait_ge(qn_ready, l + 1)
                pe.wait_ge(v2_ready, 2 * l + 2)
                scores(0)
                for n in range(NH2):
                    if n + 1 < NH2:
                        scores(n + 1)
                    extra = rows - NH2
                    ada_rows(n + min(n, extra))
                    pe.wait_ge(p2_ready, n0 + n + 1)
                    if n >= 2:
                        pe.wait_ge(pT_ready, n0 + n - 1)
                    for i in range(3):
                        last = nc.tensor.transpose(ps[4 + n % 2][:, i * P:(i + 1) * P], p2[:, n % 2, i * P:(i + 1) * P], ident)
                    last.then_inc(pT_done, 1)
                    if n < extra:
                        ada_rows(2 * n + 1)
                    pe.wait_ge(pT_ready, n0 + n + 1)
                    if n % 2 == 0 and n >= 4:
                        pe.wait_ge(y2lo_ready, (CT + 1) * l + n // 2 - 1)
                    o = ps[6 + n // 2 % 2][HD2 * (n % 2):HD2 * (n % 2) + HD2, 0:S]
                    mm(o, v2[:, 0, HD2 * n:HD2 * n + HD2], pT[:, n % 2, 0:S], start=True, stop=False)
                    mm(o[:, P:S], v2[:, 1, HD2 * n:HD2 * n + HD2], pT[:, n % 2, S:S + P], start=False, stop=True)\
                        .then_inc(o2_done, 1)
                pe.wait_ge(conv_step, CW * CT * (l + 1))
                for t in range(CT):
                    last = mm(ps2[1][:, 0], mean512[:], zacc[:, t], start=t == 0, stop=t == CT - 1)
                last.then_inc(zmean_done, 1)
                for j in range(OUT2_UNITS):
                    u = Unit(first + MIX_UNITS + j)
                    if j == 0:
                        pe.wait_ge(y2lo_ready, (CT + 1) * l + CT)
                    if j == 2:
                        pe.wait_ge(y2lo_ready, (CT + 1) * (l + 1))
                    rows_product(u, y2hi, y2lo, (4, 6, 0, 2)[j], j == 0, j == OUT2_UNITS - 1)
                    if j == 0:
                        pe.wait_ge(arow_ready, l + 1)
                        for i in range(2):
                            last = nc.tensor.transpose(ps[0][:, S + rows * i:S + rows * i + rows], arow[0:rows, P * i:P * i + P],
                                                       ident[0:rows, 0:rows])
                        last.then_inc(arow_turned, 1)
                        pe.wait_ge(zsq_ready, l + 1)
                        for t in range(CT):
                            last = mm(ps2[1][:, 1], mean512[:], sq2[:, 0, t], start=t == 0, stop=t == CT - 1)
                        last.then_inc(zvar_done, 1)

            mixer(0, S_B2)
            norm(N_FFN[0])
            for j in range(FF_UNITS):
                if j >= 2:
                    pe.wait_ge((fg_ready, fa_ready)[j % 2], j // 2)
                products(Unit(S_FF + j), N_FFN[0] if j == 0 else None)
                if j % 2 == 0 and 1 <= j // 2 <= ADA_FF:
                    ada(ADA_AT_FF[j // 2 - 1][0], ps[7])
            for j in range(DOWN_UNITS):
                pe.wait_ge(flo_ready, j + 1)
                rows_product(Unit(S_FF + FF_UNITS + j), fhi, flo, 2 * j, j == 0, j == DOWN_UNITS - 1)
                if j % 2 == 0 and (FF_UNITS + j) // 2 <= ADA_FF:
                    ada(ADA_AT_FF[(FF_UNITS + j) // 2 - 1][0], ps[7])
            mixer(1, S_B3)
            norm(N_FFN[1])

            pe.wait_ge(router_in, 48)
            pe.wait_ge(h_ready, 2 * split_no(N_FFN[1]) + 2)
            for t in range(2):
                for k in range(KD):
                    last = mm(ps[7][:, t * NE:(t + 1) * NE], h[:, k, t * P:(t + 1) * P], wr[:, k], start=k == 0, stop=k == KD - 1)
            last.then_inc(logits_done, 1)
            for t in range(2):
                for k in range(KD):
                    last = nc.tensor.transpose(ps[2 * t + k // 4][:, P * (k % 4):P * (k % 4) + P], h[:, k, t * P:(t + 1) * P], ident)
            last.then_inc(htok_done, 1)
            pe.wait_ge(route_ready, 1)
            chosen = [lg[:, 9, t] for t in range(2)]
            mm(ps[6][:, 0:NE], before, chosen[0], start=True, stop=True)
            mm(ps[6][:, NE:2 * NE], ones[:, 0:P], chosen[0], start=True, stop=False)
            mm(ps[6][:, NE:2 * NE], before, chosen[1], start=False, stop=True)
            mm(ps[6][:, 2 * NE:3 * NE], ones[:, 0:P], chosen[0], start=True, stop=False)
            mm(ps[6][:, 2 * NE:3 * NE], ones[:, 0:P], chosen[1], start=False, stop=True).then_inc(rank_done, 1)

            def gather(g, half):
                for kk in range(4):
                    for t in range(2):
                        k = 4 * half + kk
                        last = mm(ps4[7][:, kk], htok[:, t, k * P:(k + 1) * P], pick[:, t], start=t == 0, stop=t == 1)
                last.then_inc(xg_done, 1)

            def spread(job, rnd):
                for i in range(2):
                    d = 2 * rnd + i
                    last = mm(ps2[7][:, i], yexp[:, d * P:(d + 1) * P], pickT[:], start=True, stop=True)
                last.then_inc(spread_done, 1)

            def expert(job, mine, following):
                chunks = JOB_UP // 4
                pe.wait_ge(xglo_ready, mine.count(2, 2))

                def turn(c):
                    pe.wait_ge(ma_ready, job.count(chunks, c + 1))
                    if c:
                        pe.wait_ge(tlo_ready, job.count(chunks, c))
                    for i in range(4):
                        last = nc.tensor.transpose(ps4[4][:, i], ma[:, c % 2, i * P:(i + 1) * P], ident)
                    last.then_inc(turned, 1)

                for i in range(JOB_UP):
                    u, c, kind, half = job.unit(i), i // 4, i % 4 // 2, i % 2
                    if c >= 2 and half == 0:
                        pe.wait_ge((mg_ready, ma_ready)[kind], job.count(chunks, c - 1))
                    pe.wait_ge(raw_free, u.free())
                    o = ps[2 * kind + c % 2][:, :]
                    for kk in range(4):
                        k, w = 4 * half + kk, slice(512 * kk, 512 * kk + 512)
                        mm(o, xghi[:, k], whi[:, u.hl, w], start=k == 0, stop=False)
                        mm(o, xglo[:, k], whi[:, u.hl, w], start=False, stop=False)
                        last = mm(o, xghi[:, k], wlo[:, u.hl, w], start=False, stop=k == KD - 1)
                    last.then_inc(unit_done, 1)
                    if c and i % 4 == 1:
                        turn(c - 1)
                    if i % 4 == 3 and 1 <= c <= 4:
                        if c == 1:
                            pe.wait_ge(yexp_ready, job.count(1, 1))
                            pe.wait_ge(pickT_ready, job.count(1, 1))
                        else:
                            pe.wait_ge(spread_taken, job.count(4, c - 1))
                        spread(job, c - 1)
                    if i == 4 * 5 + 3:
                        pe.wait_ge(spread_taken, job.count(4, 4))
                        for t in range(2):
                            last = nc.tensor.transpose(ps[7][:, t * P:(t + 1) * P], pickw[:, t], ident)
                        last.then_inc(pickT_done, 1)
                for d in range(JOB_DOWN):
                    u = job.unit(JOB_UP + d)
                    pe.wait_ge(tlo_ready, job.count(chunks, d // 2 + 1))
                    pe.wait_ge(raw_free, u.free())
                    for i in range(2):
                        f = 2 * d + i
                        for n in range(2):
                            o, w = ps[5 + n][:, :], slice(D * i + 512 * n, D * i + 512 * n + 512)
                            mm(o, thi[:, f], whi[:, u.hl, w], start=f == 0, stop=False)
                            mm(o, tlo[:, f], whi[:, u.hl, w], start=False, stop=False)
                            last = mm(o, thi[:, f], wlo[:, u.hl, w], start=False, stop=f == FE // P - 1)
                    last.then_inc(unit_done, 1)
                    if d == 0:
                        turn(chunks - 1)
                    if following is not None and d in (1, 5):
                        if d == 1:
                            pe.wait_ge(pick_ready, following.count(1, 1))
                            pe.wait_ge(pickT_ready, job.count(1, 2))
                        else:
                            pe.wait_ge(xglo_ready, following.count(2, 1))
                        gather(following, d // 4)

            pe.wait_ge(htok_ready, 2)
            pe.wait_ge(pick_ready, 1)
            for half in range(2):
                if half:
                    pe.wait_ge(xglo_ready, 1)
                gather(Job(0, 0), half)
            with pe.Fori(0, NE) as e:
                expert(Job(0, e), Job(0, e), Job(1, e))
            pe.wait_ge(jobs_ready, 1)
            nx = pe.value_load(jobs[0:1, 0:1], min_val=0, max_val=3)
            with pe.If(nx > 0):
                with pe.Fori(0, nx) as j:
                    mine = Job(NE + 1, j)
                    pe.wait_ge(pick_ready, mine.count(1, 1))
                    for half in range(2):
                        pe.wait_ge(xglo_ready, mine.count(2, half))
                        gather(mine, half)
                    expert(Job(NE, j), mine, None)
            end = Job(NE, nx)
            pe.wait_ge(yexp_ready, end.count(1, 1))
            pe.wait_ge(pickT_ready, end.count(1, 1))
            for rnd in range(4):
                if rnd:
                    pe.wait_ge(spread_taken, end.count(4, rnd))
                spread(end, rnd)
            pe.wait_ge(x_ready, 32)
            for t in range(2):
                for k in range(KD):
                    last = nc.tensor.transpose(ps[2 * t + k // 4][:, P * (k % 4):P * (k % 4) + P], xT[:, k, t * P:(t + 1) * P], ident)
                    if k % 4 == 3:
                        last.then_inc(out_turned, 1)

        @block.vector
        def _(dve):
            step = Chain(dve, vector_step)
            V = nc.vector

            def bc(ap, n):
                return ap.unsqueeze(1).broadcast_to([ap.shape[0], n, ap.shape[1]])

            def low(u):
                dve.wait_ge(hi_ready, u.count())
                if u.n >= HL or u.per:
                    dve.wait_ge(unit_done, u.done(1 - HL))
                V.tensor_tensor(wlo[:, u.hl, :], raw[:, u.raw, :], whi[:, u.hl, :].bitcast(F32), ALU.subtract).then_inc(raw_free, 1)

            def norm_low(n, half):
                at = slice(4 * half, 4 * half + 4)
                dve.wait_ge(hhi_ready, 2 * split_no(n) + half + 1)
                V.tensor_tensor(hlo[:, at], h[:, at], hhi[:, at].bitcast(F32), ALU.subtract).then_inc(hlo_ready, 1)

            def norm(n):
                dve.wait_ge(std_ready, n + 1)
                if n == N_FINAL:
                    for k in range(0, KD, 2):
                        step.mark(V.tensor_tensor(xT[:, k:k + 2], xT[:, k:k + 2], bc(rstd[:], 2), ALU.mult))
                    for k in range(KD):
                        if k % 2 == 0:
                            step.wait(back=3 - k // 2)
                        last = V.tensor_scalar(xT[:, k], xT[:, k], par2[:, 0, P2_FIN + k:P2_FIN + k + 1], None, ALU.mult)
                        if k % 2:
                            last.then_inc(x_ready, 1)
                    return
                for half in range(2):
                    at = slice(4 * half, 4 * half + 4)
                    step(V.tensor_tensor(h[:, at], xT[:, at], bc(rstd[:], 4), ALU.mult))
                    if half:
                        norm_low(n, 0)
                    for k in range(4 * half, 4 * half + 4):
                        shift = SHIFT[n] + k
                        last = V.tensor_scalar(h[:, k], h[:, k], amul[:, n, k:k + 1], mod[:, shift:shift + 1], ALU.mult, ALU.add)
                    last.then_inc(h_ready, 1)
                norm_low(n, 1)

            def residual(last_unit, gate):
                dve.wait_ge(unit_done, Unit(last_unit).done())
                for d in range(KD):
                    last = V.scalar_tensor_tensor(xT[:, d], ps2[2 + d // 2][:, d % 2], mod[:, gate + d:gate + d + 1], xT[:, d],
                                                  ALU.mult, ALU.add)
                    if d % 2:
                        last.then_inc(x_ready, 1)

            def ada(a, block, l, at):
                dve.wait_ge(raw_in[a.raw], a.loads)
                dve.wait_ge(ada_free, a.sums(0)) if a.n else None
                if a.n >= HALF:
                    dve.wait_ge(ada_done, a.count(1 - HALF))
                w = raw[:, a.raw, :].rearrange("p (k n) -> p k n", k=KD)
                sums = (acc[:, a.n % HALF], acc2[:])
                for k in range(KD):
                    if k < 2:
                        last = V.tensor_scalar(sums[k], w[:, k], cact[:, block, k:k + 1], None, ALU.mult)
                    else:
                        step.wait(back=1)
                        last = V.scalar_tensor_tensor(sums[k % 2], w[:, k], cact[:, block, k:k + 1], sums[k % 2], ALU.mult, ALU.add)
                    step.mark(last)
                step.wait()
                V.tensor_tensor(sums[0], sums[0], sums[1], ALU.add).then_inc(ada_free, 1)

            def take_mod(bank, col, n, block, l, at):
                par, base = (par1, P1_BADA) if block == 0 else (par2, P2_BADA)
                to = 3 * KD * (3 * l + block)
                return V.tensor_tensor(mod[:, bass.ds(at * 2 + to, 2 * n)], bank[:, col:col + 2 * n],
                                       par[:, l, bass.ds(at * 2 + base, 2 * n)], ALU.add)

            def amuls(norms):
                for n in norms:
                    l = (0, 1, None, 0, 0, 1, 1)[n]
                    g = par1[:, l, P1_NORM:P1_NORM + KD] if n < 2 else \
                        par2[:, l, P2_MIX:P2_MIX + KD] if n in N_MIX else par2[:, l, P2_FFN:P2_FFN + KD]
                    last = V.scalar_tensor_tensor(amul[:, n], mod[:, SHIFT[n] + KD:SHIFT[n] + 2 * KD], 1.0, g, ALU.add, ALU.mult)
                step(last)

            V.memset(ones[:], 1.0)
            V.memset(mean256[:], 1.0 / HD).then_inc(raw_free, FREE0)
            V.memset(eps[:], EPS).then_inc(memset_done, 1)
            dve.wait_ge(x_turned, 1)
            for b in range(4):
                V.tensor_copy(xT[:, 2 * b:2 * b + 2], ps2[b]).then_inc(x_ready, 1)
            dve.wait_ge(pos_in, 16)
            dve.wait_ge(const_in, 16)
            step(V.tensor_copy(posf[:], posi[:]))
            step(V.tensor_scalar(ang[:], posf[:], freq, None, ALU.mult))
            step(V.tensor_scalar(turns[:, 0], ang[:], float(np.float32(1 / (2 * np.pi))), ROUND, ALU.mult, ALU.add))
            step(V.tensor_scalar(turns[:, 0], turns[:, 0], -ROUND, None, ALU.add))
            for part in TWO_PI:
                step(V.scalar_tensor_tensor(ang[:], turns[:, 0], -part, ang[:], ALU.mult, ALU.add))
            V.tensor_scalar(ang[:], ang[:], -PI_BELOW, PI_BELOW, ALU.max, ALU.min).then_inc(angle_ready, 1)
            dve.wait_ge(cact_ready, 1)
            for a in ADA_AT_START:
                ada(*a)
            dve.wait_ge(rows_turned, 1)
            V.tensor_copy(par1[:], ps4[4][:, 0:2])
            for l in range(L):
                V.tensor_copy(par2[:, l, 0:P2_ROWS[l]], ps4[4][:, 2 + l, 0:P2_ROWS[l]])
                last = V.tensor_copy(taps2[:, l, 0:CW * CT], ps4[5][:, l, 0:CW * CT])
            step(last)
            dve.wait_ge(ada_done, ADA_START)
            take_mod(ps[6], 0, ADA_START, 0, 0, 0).then_inc(mod_taken, 1)
            dve.wait_ge(mod_taken, 1)
            amuls((0,))
            for i in range(LOOK):
                low(Unit(S_B1 + i))
            V.memset(qpad[:, :, :, 0:CONV_K - 1], 0.0)
            for l in range(L):
                if l:
                    amuls((1,))
                norm(l)
                dve.wait_ge(gates_done, l + 1)
                dve.wait_ge(gate_in, 16 * 3 * L)
                V.tensor_scalar(gt[:, 1], ps2[7][0:H, 1], gbias[:, l, 1:2], None, ALU.add).then_inc(gate_f, 1)
                V.tensor_scalar(gt[:, 0], ps2[7][0:H, 0], gbias[:, l, 0:1], None, ALU.add)
                dve.wait_ge(gate_f, l + 1)
                dve.wait_ge(gate_ln, l + 1)
                step(V.scalar_tensor_tensor(gt[:, 3], gt[:, 1], 0.0, gt[:, 2], ALU.min, ALU.subtract))
                step(V.tensor_tensor_scan(gt[:, 4], ones[0:H], gt[:, 3], 0.0, ALU.mult, ALU.add))
                V.tensor_tensor(gt[:, 5], gt[:, 0], gt[:, 4], ALU.subtract).then_inc(a_ready, 1)
                dve.wait_ge(a_ready, l + 1)
                step(V.tensor_tensor_scan(gt[:, 6], ones[0:H], gt[:, 5], 0.0, ALU.mult, ALU.max))
                V.tensor_tensor(gt[:, 7], gt[:, 4], gt[:, 6], ALU.add).then_inc(gate_m, 1)
                for i in range(H):
                    V.tensor_scalar(gdiag[:, i, 0], gt[:, 6], cst[0:H, C_ID + i:C_ID + i + 1], -1.0, ALU.mult, ALU.mult)
                dve.wait_ge(gate_em, l + 1)
                for i in range(H):
                    V.tensor_scalar(gdiag[:, i, 1], gt[:, 7], cst[0:H, C_ID + i:C_ID + i + 1], None, ALU.mult)
                dve.wait_ge(a_turned, l + 1)
                V.tensor_copy(acol[:], ps[7][:, 0:2 * H].rearrange("p (t h) -> p t h", t=2)).then_inc(acol_ready, 1)
                dve.wait_ge(acol_ready, l + 1)

                with dve.Fori(0, NPAIR) as pair:
                    step.enter(pair, STEPS_PAIR[l])
                    ada_units = (ada_l0, ada_l1)[l](pair)
                    for hh in range(2):
                        hd = Head(l, hh, pair)
                        u0 = Unit(S_B1 + l * UNIT_L1 + hh * HEAD_UNITS, pair, 2 * HEAD_UNITS)
                        q, k, v, o, z, rq, rk, rv, rz = (u0.plus(i) for i in range(HEAD_UNITS))

                        def column(base, tile):
                            return par1[:, l, bass.ds(hd.h * 2 + (base + tile), 1)]

                        def take(u, x):
                            dve.wait_ge(unit_done, u.done())
                            V.tensor_copy(qpad[:, x, :, CONV_K - 1:], ps2[u.bank]).then_inc(taken_v, 1)

                        def ada_after(j):
                            i = ada_beside(l, hh * HEAD_UNITS + j)
                            if i is not None:
                                ada(*ada_units[i])

                        low(q.plus(LOOK))
                        dve.wait_ge(raw_free, q.plus(LOOK).free())
                        ada_after(0)
                        take(q, 0)
                        low(k.plus(LOOK))
                        ada_after(1)
                        take(k, 1)
                        dve.wait_ge(taken_v, hd.count(4, 2))
                        for tap in range(CONV_K):
                            for x in range(2):
                                for t in range(2):
                                    w = column(P1_CW + tap * 2 * KD + x * KD, t)
                                    src = qpad[:, x, t, tap:tap + S]
                                    if tap == 0:
                                        last = V.tensor_scalar(qacc[:, x, t], src, w, column(P1_CB + x * KD, t), ALU.mult, ALU.add)
                                    else:
                                        step.wait(back=3)
                                        last = V.scalar_tensor_tensor(qacc[:, x, t], src, w, qacc[:, x, t], ALU.mult, ALU.add)
                                    if (tap, x, t) == (CONV_K - 1, 1, 1):
                                        last.then_inc(conv_done, 1)
                                    else:
                                        step.mark(last)
                        low(v.plus(LOOK))
                        ada_after(2)
                        low(o.plus(LOOK))
                        ada_after(3)
                        dve.wait_ge(bc_copied, hd.count(1, 1))
                        V.scalar_tensor_tensor(arg[:, 0:S], bcs[:, 0], acol[:, 0, bass.ds(hd.h, 1)], causal, ALU.add, ALU.add)
                        V.scalar_tensor_tensor(arg[:, S:S + P], bcs[:, 0, P:S], acol[:, 1, bass.ds(hd.h, 1)], causal[:, 0:P],
                                               ALU.add, ALU.add).then_inc(arg_ready, 1)
                        low(z.plus(LOOK))
                        dve.wait_ge(scores_done, hd.count(2, 1))
                        dve.wait_ge(exp_ready, hd.count(1, 1))
                        V.scalar_tensor_tensor(sT[:], ps[2][:, 0:S + P], HD ** -0.5, arg[:], ALU.mult, ALU.mult).then_inc(sT_ready, 1)
                        ada_after(4)
                        dve.wait_ge(taken_s, hd.count(5, 3))
                        step(V.tensor_scalar(osig[:], osig[:], 0.5, 0.5, ALU.mult, ALU.add))
                        step(V.tensor_tensor(osig[:], osig[:], zsil[:], ALU.mult))
                        dve.wait_ge(pv_done, hd.count(2, 1))
                        step(V.scalar_tensor_tensor(den[:], ps2[5][:, 0], -1.0, bcs[:, 1], ALU.mult, ALU.max))
                        step(V.tensor_tensor(den[:], ps2[5][:, 0], den[:], ALU.max))
                        step(V.reciprocal(den[:], den[:]))
                        V.tensor_tensor(hn[:], ps2[4], bc(den[:], 2), ALU.mult).then_inc(hn_ready, 1)

                        def rotate(u, x):
                            dve.wait_ge(unit_done, u.done())
                            if x:
                                step.wait()
                            step.mark(V.tensor_tensor(qacc[:, 0], ps2[u.bank], bc(cosT[:], 2), ALU.mult))
                            V.tensor_tensor(qacc[:, 1], ps2[u.bank], bc(sinT[:], 2), ALU.mult).then_inc(taken_v, 1)
                            dve.wait_ge(taken_v, hd.count(4, 3 + x))
                            step.mark(V.tensor_tensor(rot[:, x, 0], qacc[:, 0, 0], qacc[:, 1, 1], ALU.subtract))
                            last = V.tensor_tensor(rot[:, x, 1], qacc[:, 0, 1], qacc[:, 1, 0], ALU.add)
                            last.then_inc(rot_done, 1) if x else step.mark(last)

                        def centre(i):
                            dve.wait_ge(mean_done, hd.count(2, i))
                            V.tensor_tensor(hn[:], hn[:], bc(ps2[6][:, 0], 2), ALU.subtract).then_inc(hc_ready, 1)

                        def finish(i, base, gate):
                            dve.wait_ge(sd_ready, hd.count(2, i))
                            step(V.tensor_tensor(hn[:], hn[:], bc(den[:], 2), ALU.mult))
                            for t in range(2):
                                last = V.scalar_tensor_tensor(yf[:, t], hn[:, t], column(base, t), gate[:, t], ALU.mult, ALU.mult)
                            last.then_inc(y_ready, 1)

                        def y_low(i, tile):
                            dve.wait_ge(yhi_ready, hd.count(2, i))
                            at = bass.ds(hd.h * 2 + tile, 2)
                            V.tensor_tensor(ylo[:, at, :], yf, yhi[:, at, :].bitcast(F32), ALU.subtract).then_inc(ylo_ready, 1)

                        low(rq.plus(LOOK))
                        ada_after(5)
                        rotate(rq, 0)
                        centre(1)
                        low(rk.plus(LOOK))
                        ada_after(6)
                        rotate(rk, 1)
                        low(rv.plus(LOOK))
                        ada_after(7)
                        finish(1, P1_GNM, osig)
                        low(rz.plus(LOOK))
                        dve.wait_ge(scores_done, hd.count(2, 2))
                        for o, t in ((slice(0, S), S), (slice(S, S + P), P)):
                            last = V.scalar_tensor_tensor(sT[:, o], ps[2][:, o], HD ** -0.5,
                                                          cst[:, bass.ds(hd.h * S + C_DECAY, t)], ALU.mult, ALU.mult)
                        last.then_inc(sT_ready, 1)
                        y_low(1, 0)
                        ada_after(8)
                        dve.wait_ge(pv_done, hd.count(2, 2))
                        V.tensor_copy(hn[:], ps2[4]).then_inc(hn_ready, 1)
                        centre(2)
                        dve.wait_ge(taken_s, hd.count(5, 5))
                        finish(2, P1_GNR, zsil)
                        y_low(2, KD)
                    dve.wait_ge(ada_done, ada_units[-1][0].count())
                    if l == 0:
                        take_mod(ps[7], 0, 2, *ada_units[0][1:])
                        take_mod(ps[7], 4, 6, *ada_units[2][1:])
                        take_mod(ps[7], 16, 1, *ada_units[8][1:]).then_inc(mod_taken, 1)
                    else:
                        take_mod(ps[7], 0, ADA_TURN[1], *ada_units[0][1:]).then_inc(mod_taken, 1)
                step.leave(NPAIR)
                for j in range(OUT1_UNITS):
                    low(Unit(S_B1 + l * UNIT_L1 + H * HEAD_UNITS + j + LOOK))
                if l == 0:
                    dve.wait_ge(mod_taken, 3)
                residual(S_B1 + (l + 1) * UNIT_L1 - 1, 72 * l + 16)
            norm(N_FINAL)

            def mixer(l, first):
                V.memset(zpad[:, :, 0:CW - 1], 0.0)
                V.memset(mean512[:], 1.0 / D_CONV)
                step(V.memset(cpad[:], 0.0))
                V.tensor_copy(cpad[:, :, max(ADA_MIX) - 1:max(ADA_MIX)], cact[:, 1].unsqueeze(2)).then_inc(cpad_ready, 1)
                norm(N_MIX[l])
                dve.wait_ge(bias_in, 32 * (l + 1))
                step(V.memset(bias2[0:CHUNK, :, S - CHUNK:S], NEG))
                taps = [(t, tap) for tap in range(CW) for t in range(CT)]
                done = CW * CT * l

                def conv(n):
                    for _ in range(min(n, len(taps))):
                        t, tap = taps.pop(0)
                        at = done + CW * CT - len(taps)
                        w, src = taps2[:, l, tap * CT + t:tap * CT + t + 1], zpad[:, t, tap:tap + S]
                        if tap == 0:
                            last = V.tensor_scalar(zacc[:, t], src, w, par2[:, l, P2_CB + t:P2_CB + t + 1], ALU.mult, ALU.add)
                        else:
                            dve.wait_ge(conv_step, at - CT)
                            last = V.scalar_tensor_tensor(zacc[:, t], src, w, zacc[:, t], ALU.mult, ALU.add)
                        last.then_inc(conv_step, 1)

                for j in range(MIX_UNITS):
                    u = Unit(first + j)
                    low(u.plus(LOOK))
                    if j in (1, 3):
                        dve.wait_ge(sig_ready, 2 * l + j // 2 + 1)
                        step(V.tensor_scalar(sig[:], sig[:], 0.5, 0.5, ALU.mult, ALU.add))
                        V.tensor_tensor(zpad[:, j - 1:j + 1, CW - 1:], ps2[1 - u.bank], sig[:], ALU.mult).then_inc(gemm_taken, 1)
                        dve.wait_ge(gemm_taken, 6 * l + j // 2 + 1)
                    if 4 <= j < 8:
                        i, half = (j - 4) // 2, j % 2
                        dve.wait_ge(unit_done, u.done())
                        V.tensor_copy(q2[:, i, 2 * half:2 * half + 2], ps2[u.bank]).then_inc(gemm_taken, 1)
                    if j >= 4:
                        conv(10)
                dve.wait_ge(hbc_done, l + 1)
                for i in range(2):
                    for t in range(CT):
                        last = V.scalar_tensor_tensor(q2[:, i, t], q2[:, i, t], par2[:, l, P2_QN + i:P2_QN + i + 1],
                                                      ps2[3 + 2 * i + t // 2][:, t % 2], ALU.mult, ALU.mult)
                last.then_inc(qn_ready, 1)

                def pair_low(i):
                    dve.wait_ge(y2hi_ready, (CT + 1) * l + i + 1)
                    V.tensor_tensor(y2lo[:, CT + i], ps2[6 + i % 2][:, 0], y2hi[:, CT + i].bitcast(F32), ALU.subtract)\
                        .then_inc(y2lo_ready, 1)

                for n in range(NH2 + 1):
                    b, at = n % 2, NH2 * l + n
                    if n < NH2:
                        dve.wait_ge(sc2_done, at + 1)
                        step.mark(V.scalar_tensor_tensor(s2[:, b, 0:P], ps[2 + b][:, 0:P], HD2 ** -0.5, bias2[:, n, P:S],
                                                         ALU.mult, ALU.add))
                        step(V.scalar_tensor_tensor(s2[:, b, P:P + S], ps[2 + b][:, P:P + S], HD2 ** -0.5, bias2[:, n, :],
                                                    ALU.mult, ALU.add))
                        step.mark(V.reduce_max(st2[:, b, 0:1], s2[:, b, 0:P], AX.X))
                        step(V.reduce_max(st2[:, b, 1:2], s2[:, b, P:P + S], AX.X))
                        V.tensor_scalar(st2[:, b, 2:4], st2[:, b, 0:2], -1.0, None, ALU.mult).then_inc(s2_ready, 1)
                        conv(4)
                    if n:
                        b = (n - 1) % 2
                        dve.wait_ge(p2_sum, at)
                        step(V.reciprocal(st2[:, b, 6:8], st2[:, b, 4:6]))
                        V.tensor_scalar(p2[:, b, 0:P], p2[:, b, 0:P], st2[:, b, 6:7], None, ALU.mult)
                        V.tensor_scalar(p2[:, b, P:P + S], p2[:, b, P:P + S], st2[:, b, 7:8], None, ALU.mult).then_inc(p2_ready, 1)
                        conv(4)
                        dve.wait_ge(pT_done, at)
                        V.tensor_copy(pT[:, b], ps[4 + b][:, 0:S + P]).then_inc(pT_ready, 1)
                    if n >= 3 and n % 2:
                        pair_low((n - 3) // 2)
                pair_low(CT - 1)
                conv(len(taps))
                dve.wait_ge(zmean_done, l + 1)
                V.tensor_tensor(zacc[:], zacc[:], bc(ps2[1][:, 0], CT), ALU.subtract).then_inc(zc_ready, 1)
                for j in range(2):
                    low(Unit(first + MIX_UNITS + LOOK + j))
                dve.wait_ge(arow_turned, l + 1)
                rows, of = ADA_MIX[l], P2_BADA + 2 * (ADA2 - ADA_MIX[l])
                to = 3 * KD * (3 * l + 1) + of - P2_BADA
                for i in range(2):
                    last = V.tensor_tensor(mod[:, to:to + 2 * rows].rearrange("p (u j) -> p j u", j=2)[:, i],
                                           ps[0][:, S + rows * i:S + rows * i + rows],
                                           par2[:, l, of:of + 2 * rows].rearrange("p (u j) -> p j u", j=2)[:, i],
                                           ALU.add)
                last.then_inc(mod_taken, 1)
                dve.wait_ge(zstd_ready, l + 1)
                V.tensor_tensor(zacc[:], zacc[:], bc(sig[:, 0], CT), ALU.mult).then_inc(zn_ready, 1)
                dve.wait_ge(y2hi_ready, (CT + 1) * (l + 1))
                V.tensor_tensor(y2lo[:, 0:CT], q2[:, 0], y2hi[:, 0:CT].bitcast(F32), ALU.subtract).then_inc(y2lo_ready, 1)
                for j in range(2, OUT2_UNITS):
                    low(Unit(first + MIX_UNITS + LOOK + j))
                dve.wait_ge(mod_taken, (6, 8)[l])
                residual(first + UNIT_L2 - 1, 72 * l + 24 + 16)
                amuls((N_FFN[l],))

            dve.wait_ge(mod_taken, 5)
            amuls((N_MIX[0],))
            mixer(0, S_B2)
            norm(N_FFN[0])

            def ff_low(i):
                dve.wait_ge(fhi_ready, i + 1)
                V.tensor_tensor(flo[:, 2 * i:2 * i + 2], fa[:, i % 2], fhi[:, 2 * i:2 * i + 2].bitcast(F32), ALU.subtract)\
                    .then_inc(flo_ready, 1)

            for j in range(FF_UNITS):
                u, i = Unit(S_FF + j), j // 2
                low(u.plus(LOOK))
                if j % 2:
                    dve.wait_ge(fg_ready, i + 1)
                    dve.wait_ge(unit_done, u.done())
                    V.tensor_tensor(fa[:, i % 2], fg[:, i % 2], ps2[u.bank], ALU.mult).then_inc(fa_ready, 1)
                elif i:
                    ff_low(i - 1)
                if j % 2 == 0 and j // 2 < ADA_FF:
                    ada(*ADA_AT_FF[j // 2])
            for j in range(DOWN_UNITS):
                low(Unit(S_FF + FF_UNITS + j + LOOK))
                if j % 2 == 0 and (FF_UNITS + j) // 2 < ADA_FF:
                    ada(*ADA_AT_FF[(FF_UNITS + j) // 2])
                if j == 0:
                    ff_low(FF_UNITS // 2 - 1)
            dve.wait_ge(ada_done, A_MIX1)
            take_mod(ps[7], 0, ADA_FF, *ADA_AT_FF[0][1:]).then_inc(mod_taken, 1)
            residual(S_B3 - 1, 24 + 40)
            dve.wait_ge(mod_taken, 7)
            amuls((N_MIX[1],))
            mixer(1, S_B3)
            norm(N_FFN[1])

            dve.wait_ge(router_in, 48)
            dve.wait_ge(logits_done, 1)
            step(V.tensor_tensor(lg[:, 0], ps[7][:, 0:2 * NE].rearrange("p (t e) -> p t e", t=2), bc(rb[:], 2), ALU.add))

            def largest(src, col, dst):
                step(V.tensor_reduce(lg[:, 10, col, 4:6], lg[:, src], axis=AX.X, op=ALU.max))
                for t in range(2):
                    last = V.tensor_scalar(lg[:, dst, t], lg[:, src, t], lg[:, 10, col, 4 + t:5 + t], None, ALU.is_equal)
                step(last)
                for t in range(2):
                    last = V.tensor_tensor_scan(lg[:, dst + 1, t], ones[:, 0:NE], lg[:, dst, t], 0.0, ALU.mult, ALU.add)
                step(last)
                step(V.scalar_tensor_tensor(lg[:, dst], lg[:, dst + 1], 1.0, lg[:, dst], ALU.is_equal, ALU.mult))

            largest(0, 0, 1)
            step(V.scalar_tensor_tensor(lg[:, 3], lg[:, 1], NEG, lg[:, 0], ALU.mult, ALU.add))
            largest(3, 1, 4)
            V.tensor_tensor(lg[:, 9], lg[:, 1], lg[:, 4], ALU.add).then_inc(route_ready, 1)
            V.tensor_tensor(lg[:, 10, 1, 0:2], lg[:, 10, 1, 4:6], lg[:, 10, 0, 4:6], ALU.subtract).then_inc(e_ready, 1)
            dve.wait_ge(route_ready, 1)
            dve.wait_ge(htok_done, 1)
            step.mark(V.tensor_copy(htok[:, 1, 0:512], ps[2][:, :]))
            V.tensor_copy(htok[:, 1, 512:D], ps[3][:, :]).then_inc(htok_ready, 1)
            V.memset(comb[:], 0.0)
            V.memset(r1[:], 0.0)
            dve.wait_ge(route_exp, 1)
            step(V.tensor_scalar(lg[:, 11, 0, 2:4], lg[:, 11, 0, 0:2], 1.0, None, ALU.add))
            step(V.reciprocal(lg[:, 11, 0, 4:6], lg[:, 11, 0, 2:4]))
            step(V.tensor_tensor(lg[:, 11, 0, 6:8], lg[:, 11, 0, 0:2], lg[:, 11, 0, 4:6], ALU.mult))
            for t in range(2):
                step(V.tensor_scalar(comb[:, t, 0:NE], lg[:, 1, t], lg[:, 11, 0, 4 + t:5 + t], None, ALU.mult))
                step(V.scalar_tensor_tensor(comb[:, t, 0:NE], lg[:, 4, t], lg[:, 11, 0, 6 + t:7 + t], comb[:, t, 0:NE],
                                            ALU.mult, ALU.add))
            step(V.memset(posm[:], -1e6))
            dve.wait_ge(rank_done, 1)
            step(V.scalar_tensor_tensor(posm[:, :, 0:NE], ps[6][:, 0:2 * NE].rearrange("p (t e) -> p t e", t=2), 1e6, lg[:, 9],
                                        ALU.add, ALU.mult))
            step(V.tensor_scalar(posm[:, :, 0:NE], posm[:, :, 0:NE], -1e6, None, ALU.add))
            step(V.tensor_scalar(r1[:, 0], ps[6][0:1, 2 * NE:3 * NE], P + 0.5, None, ALU.is_gt))
            step(V.tensor_tensor_scan(r1[:, 1], ones[0:1, 0:NE], r1[:, 0], 0.0, ALU.mult, ALU.add))
            step(V.tensor_tensor(r1[:, 2], r1[:, 1], r1[:, 0], ALU.subtract))
            step(V.tensor_copy(r1[:, 9, 0:1], r1[:, 1, NE - 1:NE]))
            for j in range(3):
                step(V.scalar_tensor_tensor(r1[:, 3], r1[:, 2], float(j), r1[:, 0], ALU.is_equal, ALU.mult))
                step(V.tensor_tensor(r1[:, 4], r1[:, 3], iota[0:1, 0:NE], ALU.mult))
                step(V.reduce_sum(r1[:, 9, j + 1:j + 2], r1[:, 4], AX.X))
            V.tensor_copy(jobs[:], r1[:, 9]).then_inc(jobs_ready, 1)

            def picks(e, first):
                for t in range(2):
                    step.mark(V.tensor_scalar(pick[:, t], iota, float(first), posm[:, t, bass.ds(e, 1)], ALU.add, ALU.is_equal))
                step.wait()
                for t in range(2):
                    last = V.tensor_scalar(pickw[:, t], pick[:, t], comb[:, t, bass.ds(e, 1)], None, ALU.mult)
                last.then_inc(pick_ready, 1)

            def take_tokens(gather, half):
                at = slice(4 * half, 4 * half + 4)
                dve.wait_ge(xghi_ready, gather.count(2, half + 1))
                V.tensor_tensor(xglo[:, at], ps4[7], xghi[:, at].bitcast(F32), ALU.subtract).then_inc(xglo_ready, 1)

            def expert(job, following):
                chunks = JOB_UP // 4
                for i in range(JOB_UNITS):
                    u, c = job.unit(i), i // 4
                    low(u.plus(LOOK))
                    if i < JOB_UP and i % 4 == 3:
                        dve.wait_ge(mg_ready, job.count(chunks, c + 1))
                        dve.wait_ge(unit_done, u.done())
                        V.tensor_tensor(ma[:, c % 2], mg[:, c % 2], ps[2 + c % 2][:, :], ALU.mult).then_inc(ma_ready, 1)
                    if i % 4 == 2 and 1 <= c <= chunks:
                        dve.wait_ge(thi_ready, job.count(chunks, c))
                        at = slice(4 * c - 4, 4 * c)
                        V.tensor_tensor(tlo[:, at], ps4[4], thi[:, at].bitcast(F32), ALU.subtract).then_inc(tlo_ready, 1)
                    if i % 4 == 0 and 2 <= c <= 5:
                        rnd = c - 2
                        dve.wait_ge(spread_done, job.count(4, rnd + 1))
                        V.tensor_tensor(moe[:, 2 * rnd:2 * rnd + 2], moe[:, 2 * rnd:2 * rnd + 2], ps2[7], ALU.add)\
                            .then_inc(spread_taken, 1)
                    if i == 25:
                        dve.wait_ge(pickT_done, job.count(1, 1))
                        V.tensor_copy(pickT[:], ps[7][:, 0:S]).then_inc(pickT_ready, 1)
                    if following is not None and i == 26:
                        picks(following.turn + following.n, 0)
                    if following is not None and i in (JOB_UP + 3, JOB_UP + 7):
                        take_tokens(following, (i - JOB_UP) // 4)

            V.memset(pickT[:], 0.0).then_inc(pickT_ready, 1)
            V.memset(moe[:], 0.0)
            step.mark(V.memset(yexp[:, 0:512], 0.0))
            V.memset(yexp[:, 512:D], 0.0).then_inc(yexp_ready, 1)
            dve.wait_ge(yexp_ready, 1)
            picks(0, 0)
            for half in range(2):
                take_tokens(Job(0, 0), half)
            with dve.Fori(0, NE) as e:
                step.enter(e, 2)
                expert(Job(0, e), Job(1, e))
            step.leave(NE)
            dve.wait_ge(jobs_ready, 1)
            nx = dve.value_load(jobs[0:1, 0:1], min_val=0, max_val=3)
            with dve.If(nx > 0):
                with dve.Fori(0, nx) as j:
                    step.enter(j, 2)
                    picks(dve.value_load(jobs[0:1, bass.ds(j + 1, 1)], min_val=0, max_val=NE - 1), P)
                    for half in range(2):
                        take_tokens(Job(NE + 1, j), half)
                    expert(Job(NE, j), None)
            end = Job(NE, nx)
            for rnd in range(4):
                dve.wait_ge(spread_done, end.count(4, rnd + 1))
                V.tensor_tensor(moe[:, 2 * rnd:2 * rnd + 2], moe[:, 2 * rnd:2 * rnd + 2], ps2[7], ALU.add).then_inc(spread_taken, 1)
            dve.wait_ge(spread_taken, end.count(4, 4))
            for d in range(KD):
                g = 72 + 24 + 40 + d
                last = V.scalar_tensor_tensor(xT[:, d], moe[:, d], mod[:, g:g + 1], xT[:, d], ALU.mult, ALU.add)
                if d % 2:
                    last.then_inc(x_ready, 1)


def _shape_constants():
    c = np.zeros((P, C_ALL), np.float32)
    p, t = np.arange(P)[:, None], np.arange(S)[None, :]
    c[:, C_ID:C_ID + P] = np.eye(P)
    c[:, C_CAUSAL:C_CAUSAL + S] = np.where(p <= t, 0.0, NEG)
    for i in range(H):
        c[:, C_DECAY + S * i:C_DECAY + S * (i + 1)] = np.where(p <= t, (1.0 - 2.0 ** (-5.0 - i)) ** np.maximum(t - p, 0), 0.0)
    c[:, C_BEFORE:C_BEFORE + P] = p < np.arange(P)[None, :]
    c[:, C_IOTA:C_IOTA + P] = np.arange(P)[None, :]
    places = np.arange(P, dtype=np.float32) * np.float32(1.0 / (P - 1))
    c[:, C_FREQ] = np.float32(1.0) / (10000.0 ** places.astype(np.float64)).astype(np.float32)
    for j in range(CT):
        for half in range(2):
            c[HD2 * half:HD2 * half + HD2, C_HSUM + NH2 * j + 2 * j + half] = 1.0 / HD2
            at = C_HBC + P * j + HD2 * half
            c[2 * j + half, at:at + HD2] = 1.0
    return c


_INS = ['x', 'positions', 'consts', 'c', 'w_ada', 'b_ada', 'norm_g', 'w_in', 'conv_w', 'conv_b', 'b_igate', 'b_fgate',
        'gn_m', 'gn_r', 'w_out', 'final_g', 'c_2', 'w_ada_2', 'b_ada_2', 'norm_mix_g_2', 'norm_ffn_g_2', 'w_in_2',
        'w_out_2', 'conv_w_2', 'conv_b_2', 'conv_ln_g_2', 'conv_ln_b_2', 'q_norm_g_2', 'k_norm_g_2', 'rel_bias_2',
        'ffn_w_gate_2', 'ffn_w_up_2', 'ffn_w_down_2', 'moe_w_router_2', 'moe_b_router_2', 'moe_w_gate_2',
        'moe_w_up_2', 'moe_w_down_2']
_OUTS = [((1, S, D), 'float32')]


def kernel(**inputs):
    import numpy as _np
    import concourse.bacc as _bacc
    from concourse import mybir as _mybir
    from concourse.bass_utils import run_bass_kernel_spmd as _run

    nc = _bacc.Bacc("TRN2", target_bir_lowering=False, num_devices=1)
    arrays, args = {}, []
    for name in _INS:
        a = _shape_constants() if name == 'consts' else _np.ascontiguousarray(inputs[name])
        arrays[f"in_{name}_dram"] = a
        args.append(nc.dram_tensor(f"in_{name}_dram", a.shape, _mybir.dt.from_np(a.dtype), kind="ExternalInput").ap())
    for i, (shape, dtype) in enumerate(_OUTS):
        dt = _mybir.dt.from_np(_np.dtype(dtype))
        args.append(nc.dram_tensor(f"out_{i}_dram", shape, dt, kind="ExternalOutput").ap())
    two_block_model(nc, *args)
    r = _run(nc, [arrays], core_ids=[0])
    got = tuple(r.results[0][f"out_{i}_dram"] for i in range(len(_OUTS)))
    return got[0]
```
